# Optimizing a Trainium2 kernel written in Bass

```python
import math
import jax, jax.numpy as jnp
from jax import lax
import numpy as np

D_MODEL = 1024
BATCH = 1
SEQ = 256
DEPTH = 2
DEC_BATCH = 8
DEC_SEQ = 1
PAST_LEN = 2048
PAGE_SIZE = 128

A_HEADS = 6
A_NOPE = 64
A_ROPE = 32
A_VDIM = 64
Q_LORA = 256
KV_LORA = 128
ATTN_QBLOCK = 128
B_HEADS = 6
B_HDIM = 64
DIL_PATTERNS = ((128, 1), (512, 4), (2048, 16))
B_MAX_WINDOW = 2048
C_CH = 256
C_WIDTH = 31
A_WIDTH = A_HEADS * A_VDIM
B_WIDTH = B_HEADS * B_HDIM
MIX_WIDTH = A_WIDTH + B_WIDTH + C_CH
IN_COLS = Q_LORA + KV_LORA + A_ROPE + 3 * B_WIDTH + 2 * C_CH
PEER_HEADS = 8
N_KEYS = 128
N_EXPERTS = N_KEYS * N_KEYS
PEER_KDIM = 256
PEER_TOPK = 16
PEER_BLOCK = 128

ROPE_THETA = 10000.0
EPS = 1e-6
NEG_INF = -1e30

kernel_name = "hymba_mla_dilated_conformer_peer_step"

def rmsnorm(x, g):
    xf = x.astype(jnp.float32)
    y = xf * lax.rsqrt(jnp.mean(xf * xf, axis=-1, keepdims=True) + EPS)
    return (y * g.astype(jnp.float32)).astype(x.dtype)

def layernorm(x, g, b):
    xf = x.astype(jnp.float32)
    mu = jnp.mean(xf, axis=-1, keepdims=True)
    var = jnp.mean(jnp.square(xf - mu), axis=-1, keepdims=True)
    y = (xf - mu) * lax.rsqrt(var + EPS) * g.astype(jnp.float32) + b.astype(jnp.float32)
    return y.astype(x.dtype)

def rope(x, pos):
    dim = x.shape[-1]
    half = dim // 2
    inv = ROPE_THETA ** (-jnp.arange(half, dtype=jnp.float32) * 2.0 / dim)
    ang = pos.astype(jnp.float32)[:, None] * inv[None, :]
    shape = (pos.shape[0],) + (1,) * (x.ndim - 3) + (half,)
    cos = jnp.cos(ang).reshape(shape)
    sin = jnp.sin(ang).reshape(shape)
    xf = x.astype(jnp.float32)
    x1, x2 = xf[..., :half], xf[..., half:]
    return jnp.concatenate([x1 * cos - x2 * sin, x2 * cos + x1 * sin], axis=-1).astype(x.dtype)

def softmax_lse(s):
    m = jnp.max(s, axis=-1, keepdims=True)
    p = jnp.exp(s - m)
    den = jnp.sum(p, axis=-1, keepdims=True)
    return p / den, (m + jnp.log(den))[..., 0]

def project_in(hn, pos, w_in, q_norm, w_uq, kv_norm):
    B, T, _ = hn.shape
    z = hn @ w_in
    sizes = [Q_LORA, KV_LORA, A_ROPE, B_WIDTH, B_WIDTH, B_WIDTH, C_CH, C_CH]
    offs = [int(o) for o in np.cumsum(sizes)[:-1]]
    c_q, c_kv, k_r, qb, kb, vb, ga, gb = jnp.split(z, offs, axis=-1)
    q = (rmsnorm(c_q, q_norm) @ w_uq).reshape(B, T, A_HEADS, A_NOPE + A_ROPE)
    q_nope = q[..., :A_NOPE]
    q_rope = rope(q[..., A_NOPE:], pos)
    c_kv = rmsnorm(c_kv, kv_norm)
    k_r = rope(k_r, pos)
    qb = rope(qb.reshape(B, T, B_HEADS, B_HDIM), pos)
    kb = rope(kb.reshape(B, T, B_HEADS, B_HDIM), pos)
    vb = vb.reshape(B, T, B_HEADS, B_HDIM)
    g = ga * jax.nn.sigmoid(gb)
    return q_nope, q_rope, c_kv, k_r, qb, kb, vb, g

def mla_prompt(q_nope, q_rope, c_kv, k_r, w_ukv):
    B, T, _, _ = q_nope.shape
    kv = (c_kv @ w_ukv).reshape(B, T, A_HEADS, A_NOPE + A_VDIM)
    k_nope, v = kv[..., :A_NOPE], kv[..., A_NOPE:]
    scale = (A_NOPE + A_ROPE) ** -0.5
    kpos = jnp.arange(T)

    def block(i):
        start = i * ATTN_QBLOCK
        qn = lax.dynamic_slice_in_dim(q_nope, start, ATTN_QBLOCK, axis=1)
        qr = lax.dynamic_slice_in_dim(q_rope, start, ATTN_QBLOCK, axis=1)
        s = (jnp.einsum('bqhd,bkhd->bhqk', qn, k_nope)
             + jnp.einsum('bqhr,bkr->bhqk', qr, k_r)).astype(jnp.float32) * scale
        qpos = start + jnp.arange(ATTN_QBLOCK)
        s = jnp.where(kpos[None, :] <= qpos[:, None], s, NEG_INF)
        p = jax.nn.softmax(s, axis=-1).astype(v.dtype)
        return jnp.einsum('bhqk,bkhd->bqhd', p, v)

    o = lax.map(block, jnp.arange(T // ATTN_QBLOCK))
    return o.transpose(1, 0, 2, 3, 4).reshape(B, T, A_WIDTH)

def mla_sample(q_nope, q_rope, c_new, kr_new, past_c, past_r, w_ukv):
    Bd, Tq, _, _ = q_nope.shape
    w = w_ukv.reshape(KV_LORA, A_HEADS, A_NOPE + A_VDIM)
    w_uk, w_uv = w[..., :A_NOPE], w[..., A_NOPE:]
    scale = (A_NOPE + A_ROPE) ** -0.5
    q_lat = jnp.einsum('bqhd,chd->bqhc', q_nope, w_uk)
    s_past = (jnp.einsum('bqhc,bkc->bhqk', q_lat, past_c)
              + jnp.einsum('bqhr,bkr->bhqk', q_rope, past_r)).astype(jnp.float32) * scale
    s_new = (jnp.einsum('bqhc,bkc->bhqk', q_lat, c_new)
             + jnp.einsum('bqhr,bkr->bhqk', q_rope, kr_new)).astype(jnp.float32) * scale
    causal = jnp.arange(Tq)[:, None] >= jnp.arange(Tq)[None, :]
    s_new = jnp.where(causal, s_new, NEG_INF)
    p = jax.nn.softmax(jnp.concatenate([s_past, s_new], axis=-1), axis=-1).astype(past_c.dtype)
    P = past_c.shape[1]
    o_lat = (jnp.einsum('bhqk,bkc->bqhc', p[..., :P], past_c)
             + jnp.einsum('bhqk,bkc->bqhc', p[..., P:], c_new))
    o = jnp.einsum('bqhc,chd->bqhd', o_lat, w_uv)
    return o.reshape(Bd, Tq, A_WIDTH)

def dilated_prompt(q, k, v, window, dil):
    B, T, H, D = q.shape
    nk = window // dil
    blk = nk
    L = T // dil
    nb = -(-L // blk)
    Lp = nb * blk

    def to_blocks(x):
        x = x.reshape(B, L, dil, H, D).transpose(0, 2, 1, 3, 4)
        x = jnp.pad(x, ((0, 0), (0, 0), (0, Lp - L), (0, 0), (0, 0)))
        return x.reshape(B, dil, nb, blk, H, D)

    def with_prev(xb):
        prev = jnp.pad(xb[:, :, :-1], ((0, 0), (0, 0), (1, 0), (0, 0), (0, 0), (0, 0)))
        return jnp.concatenate([prev, xb], axis=3)

    qb = to_blocks(q)
    kk = with_prev(to_blocks(k))
    vv = with_prev(to_blocks(v))
    s = jnp.einsum('brnqhd,brnkhd->brnhqk', qb, kk).astype(jnp.float32) * (D ** -0.5)
    qi = jnp.arange(blk)[:, None]
    ki = jnp.arange(2 * blk)[None, :]
    dist = blk + qi - ki
    band = (dist >= 0) & (dist <= nk)
    not_first = jnp.arange(nb)[:, None, None] > 0
    mask = band[None] & (not_first | (ki >= blk)[None])
    s = jnp.where(mask[None, None, :, None], s, NEG_INF)
    p, lse = softmax_lse(s)
    o = jnp.einsum('brnhqk,brnkhd->brnqhd', p.astype(vv.dtype), vv)
    o = o.reshape(B, dil, Lp, H, D)[:, :, :L].transpose(0, 2, 1, 3, 4).reshape(B, T, H, D)
    lse = lse.transpose(0, 1, 2, 4, 3).reshape(B, dil, Lp, H)[:, :, :L]
    lse = lse.transpose(0, 2, 1, 3).reshape(B, T, H)
    return o, lse

def dilated_sample(q, k_ext, v_ext, buf_len, window, dil):
    Bd, Tq, H, D = q.shape
    nk = window // dil
    idx = buf_len + jnp.arange(Tq)[:, None] - dil * jnp.arange(nk + 1)[None, :]
    valid = idx >= 0
    idx = jnp.maximum(idx, 0)
    kg = k_ext[:, idx]
    vg = v_ext[:, idx]
    s = jnp.einsum('bqhd,bqjhd->bhqj', q, kg).astype(jnp.float32) * (D ** -0.5)
    s = jnp.where(valid[None, None], s, NEG_INF)
    p, lse = softmax_lse(s)
    o = jnp.einsum('bhqj,bqjhd->bqhd', p.astype(vg.dtype), vg)
    return o, lse.transpose(0, 2, 1)

def combine_dilations(results, dtype):
    outs = jnp.stack([r[0] for r in results], 0).astype(jnp.float32)
    w = jax.nn.softmax(jnp.stack([r[1] for r in results], 0), axis=0)
    o = jnp.sum(w[..., None] * outs, axis=0)
    B, T = o.shape[0], o.shape[1]
    return o.reshape(B, T, B_WIDTH).astype(dtype)

def conv_module(g_ext, conv_w, conv_b, ln_g, ln_b):
    y = lax.conv_general_dilated(g_ext, conv_w[:, None, :].astype(g_ext.dtype), (1,), 'VALID',
                                 dimension_numbers=('NWC', 'WIO', 'NWC'),
                                 feature_group_count=C_CH) + conv_b
    return jax.nn.silu(layernorm(y, ln_g, ln_b))

def peer(h, wq, subkeys, u, v):
    T = h.shape[0]
    q = (h @ wq).reshape(T, PEER_HEADS, 2, PEER_KDIM // 2)
    s = jnp.einsum('thpc,hpkc->thpk', q, subkeys).astype(jnp.float32)
    s_top, i_top = lax.top_k(s, PEER_TOPK)
    cand = s_top[:, :, 0, :, None] + s_top[:, :, 1, None, :]
    cand_idx = i_top[:, :, 0, :, None] * N_KEYS + i_top[:, :, 1, None, :]
    cs, ci = lax.top_k(cand.reshape(T, PEER_HEADS, PEER_TOPK * PEER_TOPK), PEER_TOPK)
    e = jnp.take_along_axis(cand_idx.reshape(T, PEER_HEADS, PEER_TOPK * PEER_TOPK), ci, axis=-1)
    g = jax.nn.softmax(cs, axis=-1)
    ue = u[e]
    act = jax.nn.gelu(jnp.einsum('td,thkd->thk', h, ue), approximate=False)
    ve = v[e]
    return jnp.einsum('thk,thkd->td', (g * act.astype(jnp.float32)).astype(ve.dtype), ve)

def peer_blocked(h, wq, subkeys, u, v):
    T, D = h.shape
    blk = min(PEER_BLOCK, T)
    nb = -(-T // blk)
    hp = jnp.pad(h, ((0, nb * blk - T), (0, 0))).reshape(nb, blk, D)
    out = lax.map(lambda hb: peer(hb, wq, subkeys, u, v), hp)
    return out.reshape(nb * blk, D)[:T]

def setup_inputs(seed: int = 0) -> dict:
    key = jax.random.key(seed)
    ks = iter(jax.random.split(key, 40))
    f32 = jnp.float32
    n_pages = PAST_LEN // PAGE_SIZE
    n_phys = (DEC_BATCH * n_pages * 5) // 4
    w_buf = min(B_MAX_WINDOW, PAST_LEN)

    def nrm(shape, scale=1.0):
        return jax.random.normal(next(ks), shape, f32) * scale

    def gain(shape):
        return 1.0 + nrm(shape, 0.02)

    x_prompt = nrm((BATCH, SEQ, D_MODEL))
    x_sample = nrm((DEC_BATCH, DEC_SEQ, D_MODEL))
    cache_kv_latent = nrm((DEPTH, n_phys, PAGE_SIZE, KV_LORA))
    cache_k_rope = nrm((DEPTH, n_phys, PAGE_SIZE, A_ROPE))
    state_win_k = nrm((DEPTH, DEC_BATCH, w_buf, B_HEADS, B_HDIM))
    state_win_v = nrm((DEPTH, DEC_BATCH, w_buf, B_HEADS, B_HDIM))
    state_conv = nrm((DEPTH, DEC_BATCH, C_WIDTH - 1, C_CH), 0.5)
    page_table = jax.random.permutation(next(ks), n_phys)[:DEC_BATCH * n_pages]
    page_table = page_table.reshape(DEC_BATCH, n_pages).astype(jnp.int32)
    return {
        "x_prompt": x_prompt,
        "x_sample": x_sample,
        "cache_kv_latent": cache_kv_latent,
        "cache_k_rope": cache_k_rope,
        "state_win_k": state_win_k,
        "state_win_v": state_win_v,
        "state_conv": state_conv,
        "page_table": page_table,
        "norm_mix": gain((DEPTH, D_MODEL)),
        "w_in": nrm((DEPTH, D_MODEL, IN_COLS), D_MODEL ** -0.5),
        "q_norm": gain((DEPTH, Q_LORA)),
        "w_uq": nrm((DEPTH, Q_LORA, A_HEADS * (A_NOPE + A_ROPE)), Q_LORA ** -0.5),
        "kv_norm": gain((DEPTH, KV_LORA)),
        "w_ukv": nrm((DEPTH, KV_LORA, A_HEADS * (A_NOPE + A_VDIM)), KV_LORA ** -0.5),
        "conv_w": nrm((DEPTH, C_WIDTH, C_CH), C_WIDTH ** -0.5),
        "conv_b": nrm((DEPTH, C_CH), 0.01),
        "conv_ln_g": gain((DEPTH, C_CH)),
        "conv_ln_b": nrm((DEPTH, C_CH), 0.01),
        "w_out": nrm((DEPTH, MIX_WIDTH, D_MODEL), MIX_WIDTH ** -0.5),
        "norm_ffn": gain((DEPTH, D_MODEL)),
        "peer_wq": nrm((DEPTH, D_MODEL, PEER_HEADS * PEER_KDIM), D_MODEL ** -0.5),
        "peer_subkeys": nrm((DEPTH, PEER_HEADS, 2, N_KEYS, PEER_KDIM // 2), (PEER_KDIM // 2) ** -0.5),
        "peer_u": nrm((DEPTH, N_EXPERTS, D_MODEL), D_MODEL ** -0.5),
        "peer_v": nrm((DEPTH, N_EXPERTS, D_MODEL), PEER_HEADS ** -0.5),
        "norm_final": gain((D_MODEL,)),
    }

def reference(x_prompt, x_sample, cache_kv_latent, cache_k_rope, state_win_k, state_win_v, state_conv,
              page_table, norm_mix, w_in, q_norm, w_uq, kv_norm, w_ukv, conv_w, conv_b, conv_ln_g,
              conv_ln_b, w_out, norm_ffn, peer_wq, peer_subkeys, peer_u, peer_v, norm_final):
    B, T, D = x_prompt.shape
    Bd, Tq, _ = x_sample.shape
    past_len = page_table.shape[1] * PAGE_SIZE
    buf_len = state_win_k.shape[2]
    win_p = min(B_MAX_WINDOW, T)
    win_s = min(B_MAX_WINDOW, buf_len + Tq)
    pos_p = jnp.arange(T, dtype=jnp.int32)
    pos_s = past_len + jnp.arange(Tq, dtype=jnp.int32)

    xp, xs = x_prompt, x_sample
    lat_p, kr_p, wk_p, wv_p, cv_p = [], [], [], [], []
    lat_s, kr_s, wk_s, wv_s, cv_s = [], [], [], [], []
    for l in range(DEPTH):
        hn = rmsnorm(xp, norm_mix[l])
        q_nope, q_rope, c_kv, k_r, qb, kb, vb, g = project_in(hn, pos_p, w_in[l], q_norm[l], w_uq[l], kv_norm[l])
        a_out = mla_prompt(q_nope, q_rope, c_kv, k_r, w_ukv[l])
        b_out = combine_dilations([dilated_prompt(qb, kb, vb, wdw, dl) for wdw, dl in DIL_PATTERNS], xp.dtype)
        g_ext = jnp.concatenate([jnp.zeros((B, C_WIDTH - 1, C_CH), g.dtype), g], axis=1)
        c_out = conv_module(g_ext, conv_w[l], conv_b[l], conv_ln_g[l], conv_ln_b[l])
        xp = xp + jnp.concatenate([a_out, b_out, c_out], axis=-1) @ w_out[l]
        hf = rmsnorm(xp, norm_ffn[l])
        xp = xp + peer_blocked(hf.reshape(B * T, D), peer_wq[l], peer_subkeys[l], peer_u[l], peer_v[l]).reshape(B, T, D)
        lat_p.append(c_kv)
        kr_p.append(k_r)
        wk_p.append(kb[:, T - win_p:])
        wv_p.append(vb[:, T - win_p:])
        cv_p.append(g_ext[:, g_ext.shape[1] - (C_WIDTH - 1):])

        hn = rmsnorm(xs, norm_mix[l])
        q_nope, q_rope, c_kv, k_r, qb, kb, vb, g = project_in(hn, pos_s, w_in[l], q_norm[l], w_uq[l], kv_norm[l])
        past_c = cache_kv_latent[l][page_table].reshape(Bd, past_len, KV_LORA)
        past_r = cache_k_rope[l][page_table].reshape(Bd, past_len, A_ROPE)
        a_out = mla_sample(q_nope, q_rope, c_kv, k_r, past_c, past_r, w_ukv[l])
        k_ext = jnp.concatenate([state_win_k[l], kb], axis=1)
        v_ext = jnp.concatenate([state_win_v[l], vb], axis=1)
        b_out = combine_dilations([dilated_sample(qb, k_ext, v_ext, buf_len, wdw, dl) for wdw, dl in DIL_PATTERNS], xs.dtype)
        c_ext = jnp.concatenate([state_conv[l], g], axis=1)
        c_out = conv_module(c_ext, conv_w[l], conv_b[l], conv_ln_g[l], conv_ln_b[l])
        xs = xs + jnp.concatenate([a_out, b_out, c_out], axis=-1) @ w_out[l]
        hf = rmsnorm(xs, norm_ffn[l])
        xs = xs + peer_blocked(hf.reshape(Bd * Tq, D), peer_wq[l], peer_subkeys[l], peer_u[l], peer_v[l]).reshape(Bd, Tq, D)
        lat_s.append(c_kv)
        kr_s.append(k_r)
        wk_s.append(k_ext[:, k_ext.shape[1] - win_s:])
        wv_s.append(v_ext[:, v_ext.shape[1] - win_s:])
        cv_s.append(c_ext[:, c_ext.shape[1] - (C_WIDTH - 1):])

    y_prompt = rmsnorm(xp, norm_final)
    y_sample = rmsnorm(xs, norm_final)
    return (y_prompt, y_sample,
            jnp.stack(lat_p), jnp.stack(kr_p), jnp.stack(wk_p), jnp.stack(wv_p), jnp.stack(cv_p),
            jnp.stack(lat_s), jnp.stack(kr_s), jnp.stack(wk_s), jnp.stack(wv_s), jnp.stack(cv_s))


_drawn_inputs = setup_inputs


def setup_inputs(seed=0):
    import zlib

    import numpy as np

    out = dict(_drawn_inputs(seed))
    spreads = {}
    factors = {'q_norm': 2.954, 'kv_norm': 2.756, 'conv_ln_b': 2.78, 'norm_final': 2.841}
    for name, (base, spread) in spreads.items():
        noise = np.random.default_rng([zlib.crc32(name.encode()), seed]).standard_normal(out[name].shape)
        drawn = base * np.exp(spread * noise) if base else spread * noise
        out[name] = __import__('jax').numpy.asarray(drawn.astype(out[name].dtype))
    for name, factor in factors.items():
        out[name] = (out[name] * factor).astype(out[name].dtype)
    return out
```

```python
from contextlib import ExitStack

import numpy as np
import concourse.bass as bass
from concourse import mybir

F32 = mybir.dt.float32
I32 = mybir.dt.int32
U32 = mybir.dt.uint32
ALU = mybir.AluOpType
ACT = mybir.ActivationFunctionType
AX = mybir.AxisListType.X

P = 128
D = 1024
KD = D // P
SEQ, NB = 256, 8
T = SEQ + NB
TOK = [(0, 128), (128, 128), (256, 8)]
DEPTH = 2
PAST, PAGE = 2048, 128
NPG = PAST // PAGE
NH = 6
HP = NH // 2
NOPE, ROPE, LAT = 64, 32, 128
HD = 64
QL = 256
CW, CC = 31, 256
CQ, CKV, KR, QB, KB, VB, GA, GB = 0, 256, 384, 416, 800, 1184, 1568, 1824
ZC = 2080
ZCH = [(0, 416), (416, 384), (800, 384), (1184, 384), (1568, 512)]
UQ = NH * (NOPE + ROPE)
SA, SB = float((NOPE + ROPE) ** -0.5), float(HD ** -0.5)
PH, NK, TOPK = 8, 128, 16
NSUB = 2 * PH
EPS = 1e-6
NEG = -1e30
DIL = (1, 4, 16)
UN = 4
LOOPS = NK // UN
GT = 8


def job_plan():
    jobs = [(("hT", k), "VA"[k % 2]) for k in range(KD)]
    jobs += [(("z", c, t), "A") for c in range(5) for t in range(3)]
    jobs += [(("cqT", 0), "A"), (("cqT", 1), "A"), (("ckvT",), "A"), (("krT",), "A"), (("ukT",), "A")]
    jobs += [(("q", t, n), "A") for t in range(3) for n in range(2)]
    jobs += [(("qbT", g), "V") for g in range(HP)] + [(("kbT", g), "V") for g in range(HP)]
    jobs += [(("qnT", g), "A") for g in range(HP)] + [(("qrT", g), "A") for g in range(2)] + [(("qrS",), "A")]
    jobs += [(("qlT", h), "V") for h in range(NH)]
    jobs += [(("va", t), "A") for t in range(2)]
    jobs += [(("cw",), "A"), (("sc", 0), "A"), (("sc", 1), "A"), (("gT", 0), "V"), (("gT", 1), "V")]
    for s in range(2 * NH + 2):
        if s < 2 * NH:
            jobs.append((("S", s), "V"))
        if 1 <= s <= 2 * NH:
            jobs.append((("PT", s - 1), "A"))
        if s >= 2:
            jobs.append((("O", s - 2), "V"))
    jobs += [(("mT", g), "A") for g in range(2 * HP)]
    jobs += [(("yt", t), "A") for t in range(3)]
    jobs += [(("ycT", c), "V") for c in range(2)]

    def pages(half):
        out = []
        for b in range(4 * half, 4 * half + 5):
            if b < 4 * half + 4:
                out += [(("cT", b, g), "AV"[g % 2]) for g in range(4)] + [(("rT", b), "A")]
            if b > 4 * half:
                out.append((("ST", b - 1), "A"))
        return out

    jobs += pages(0) + [(("ext",), "V")] + [(("qbc", b), "V") for b in range(NB)]
    jobs += [(("mx", 0), "V"), (("mb", 0), "V"), (("dn", 0), "V"), (("ol", 0), "V")] + pages(1)
    for n in (2, 1):
        jobs += [(("mx", n), "V"), (("mb", n), "V"), (("dn", n), "V")]
    jobs += [(("ol", 1), "V"), (("os",), "V"), (("ow",), "V")]
    jobs += [(("xo", c, t), "V") for c in range(2) for t in range(3)]
    jobs += [(("fT", k), "VA"[k % 2]) for k in range(KD)]
    jobs += [(("skT", g), "A") for g in range(4)]
    jobs += [(("pq", n), "A") for n in range(NSUB)]
    jobs += [(("s", t, g), "A") for t in range(3) for g in range(4)]
    jobs += [(("slot", t), "A") for t in range(3)]
    jobs += [(("xT", c, t), "V") for c in range(2) for t in range(3)]
    return jobs


JOBS = job_plan()
NUM = {name: n for n, (name, _) in enumerate(JOBS)}
READ = {}
for _n, (_name, _who) in enumerate(JOBS):
    READ[_name] = (_who, sum(w == _who for _, w in JOBS[:_n + 1]))


def program(nc, A, C, outs):
    (y_p, y_s, lat_p, kr_p, wk_p, wv_p, cv_p, lat_s, kr_s, wk_s, wv_s, cv_s) = outs
    with ExitStack() as ctx:
        def sb(name, shape, dt=F32):
            return ctx.enter_context(nc.sbuf_tensor(name, shape, dt))

        layer_sems = []

        def sem(name):
            s = ctx.enter_context(nc.semaphore(name))
            layer_sems.append(s)
            return s

        X = sb("X", [P, 3, D])
        hT = sb("hT", [P, KD, T])
        ident = sb("ident", [P, P])
        iota = sb("iota", [P, P])
        ones = sb("ones", [P, P])
        rope = sb("rope", [P, 3, 96])
        gains = sb("gains", [P, 2 * KD + 2 + 2 * 3])
        stat = sb("stat", [P, 16])
        bnst = sb("bnst", [P, 3, 8])
        nmx = sb("nmx", [P, 2 * NH, 2])
        den = sb("den", [P, 2 * NH, 2])
        rden = sb("rden", [P, 2 * NH, 2])
        diag = sb("diag", [NB, NB])
        pages = sb("pages", [1, NB * NPG], I32)
        slotT = sb("slotT", [P, 3, T])
        hotA = sb("hotA", [P, GT, P])
        hotB = sb("hotB", [P, 4, P])
        g_mix, g_ffn, g_q = gains[:, 0:KD], gains[:, KD:2 * KD], gains[:, 2 * KD:2 * KD + 2]
        g_cb, g_lg, g_lb = (gains[:, 2 * KD + 2 + 2 * i:2 * KD + 4 + 2 * i] for i in range(3))

        stream = sb("stream", [P, 9 * 1024 + 4 * T])
        wslot = [stream[:, i * 4096:(i + 1) * 4096] for i in range(2)]
        u_t = [stream[:, i * 1024:(i + 1) * 1024] for i in range(4)]
        v_t = [stream[:, (4 + i) * 1024:(5 + i) * 1024] for i in range(4)]
        uT = [hotA[:, :, :].rearrange("p a b -> p (a b)"), stream[:, 8192:9216]]
        act_t = [stream[:, 9216 + i * T:9216 + (i + 1) * T] for i in range(2)]
        wgt_t = [stream[:, 9216 + (2 + i) * T:9216 + (3 + i) * T] for i in range(2)]
        zeros = stream[:, 9216:9216 + 512]

        BIG = T * P
        big = sb("big", [P, BIG + 640])
        G = big[:, 0:BIG].rearrange("p (t j) -> p t j", j=P)
        at = [0]

        def cut(n):
            a = at[0]
            at[0] += n
            assert at[0] <= BIG + 640, at[0]
            return big[:, a:a + n]

        z = cut(3 * ZC).rearrange("p (t c) -> p t c", t=3)
        hn = z.rearrange("p t c -> p (t c)")[:, 0:3 * D].rearrange("p (t c) -> p t c", t=3)
        wuk, wuv = cut(NH * NOPE), cut(NH * HD)
        ukT = cut(HP * 128).rearrange("p (g c) -> p g c", g=HP)
        qnT = cut(HP * T).rearrange("p (g t) -> p g t", g=HP)
        qrT = cut(2 * T).rearrange("p (g t) -> p g t", g=2)
        qkT = cut(2 * HP * T)
        qbT = qkT[:, 0:HP * T].rearrange("p (g t) -> p g t", g=HP)
        kbT = qkT[:, HP * T:2 * HP * T].rearrange("p (g t) -> p g t", g=HP)
        krT = cut(T)
        ckvT = cut(T)
        cqT = cut(2 * T).rearrange("p (g t) -> p g t", g=2)
        qlT = cut(NH * T).rearrange("p (h t) -> p h t", h=NH)
        qrS = cut(NH * NB).rearrange("p (h b) -> p h b", h=NH)
        qrB = cut(NB * 4 * NH).rearrange("p (b i h) -> p b i h", b=NB, i=4)
        mixT = cut(KD * T).rearrange("p (k t) -> p k t", k=KD)
        kvg = cut(LAT)
        past = cut(4 * NPG * LAT).rearrange("p (b g c) -> p b g c", b=4, g=NPG)
        kw = cut(3 * 384).rearrange("p (d c) -> p d c", d=3)
        vw = cut(2 * 3 * 384).rearrange("p (s d c) -> p s d c", s=2, d=3)
        base = at[0]
        cnt = hotB[:, :, :].rearrange("p a b -> p (a b)")[:, 0:384]
        cbias = cut(384)
        mbias = cut(384)
        prob = slotT[:, :, :].rearrange("p s t -> p (s t)")[:, 0:768].rearrange("p (s c) -> p s c", s=2)
        probT = hotA[:, :, :].rearrange("p a b -> p (a b)")[:, 0:768].rearrange("p (s c) -> p s c", s=2)
        wuq = cut(2 * UQ).rearrange("p (k c) -> p k c", k=2)
        q = cut(3 * UQ).rearrange("p (t c) -> p t c", t=3)
        va = cut(2 * 384).rearrange("p (t c) -> p t c", t=2)
        oAB = cut(2 * 768).rearrange("p (t c) -> p t c", t=2)
        gT = cut(2 * 286).rearrange("p (c t) -> p c t", c=2)
        gsT = cut(2 * NB * CW).rearrange("p (c b j) -> p c b j", c=2, b=NB)
        cwT = cut(2 * CW).rearrange("p (c j) -> p c j", c=2)
        yT = qnT.rearrange("p g t -> p (g t)")[:, 0:2 * T].rearrange("p (c t) -> p c t", c=2)
        krr = vw.rearrange("p s d c -> p (s d c)")[:, 0:384].rearrange("p (t r c) -> p t r c", t=3, r=4)
        qrr = vw.rearrange("p s d c -> p (s d c)")[:, 1152:1152 + 768].rearrange("p (h r c) -> p h r c", h=NH, r=4)
        cwr = oAB[0:CW, 0, 0:256]
        scr = past.rearrange("p b g c -> p (b g c)")[0:120, 0:512].rearrange("p (s c) -> p s c", s=2)
        ropet = past.rearrange("p b g c -> p (b g c)")[:, 1024:1024 + 2 * 1152]
        junk = past.rearrange("p b g c -> p (b g c)")[:, 4096:4096 + 768]
        yt = q.rearrange("p t c -> p (t c)")[:, 0:768].rearrange("p (t c) -> p t c", t=3)
        ycs = q.rearrange("p t c -> p (t c)")[:, 768:768 + 3 * T].rearrange("p (s t) -> p s t", s=3)
        at[0] = base
        cT = cut(2 * NPG * 128).rearrange("p (s k) -> p s k", s=2)
        rT = cut(2 * 512).rearrange("p (s g k) -> p s g k", s=2, g=4)
        STm = cut(4 * 17 * NH).rearrange("p (b g h) -> p b g h", b=4, g=17)
        STw = cut(NB * 4 * NH).rearrange("p (b g h) -> p b g h", b=NB, g=4)
        smc = cut(4)
        smx = cut(3 * 48).rearrange("p (n c) -> p n c", n=3)
        sden = cut(3 * 48).rearrange("p (n c) -> p n c", n=3)
        srd = cut(3 * 48).rearrange("p (n c) -> p n c", n=3)
        sdg = cut(3 * 48).rearrange("p (n c) -> p n c", n=3)
        extS = cut(48).rearrange("p (h b) -> p h b", h=NH)[0:NB]
        olT = cut(48).rearrange("p (b h) -> p b h", b=NB)
        kprod = qkT[:, 0:3 * 384].rearrange("p (d c) -> p d c", d=3)
        pastr = stream[:, 8192:8192 + 4 * NPG * ROPE].rearrange("p (b g c) -> p b g c", b=4, g=NPG)
        at[0] = 0
        hf = cut(3 * D).rearrange("p (t c) -> p t c", t=3)
        sk = cut(NSUB * 128).rearrange("p (n c) -> p n c", n=NSUB)
        skT = cut(NSUB * 128).rearrange("p (n c) -> p n c", n=NSUB)
        pqT = cut(NSUB * T).rearrange("p (n t) -> p n t", n=NSUB)
        sc = cut(3 * NSUB * NK).rearrange("p (t n c) -> p t n c", t=3, n=NSUB)
        top = cut(NSUB * TOPK).rearrange("p (n c) -> p n c", n=NSUB)
        topi = cut(NSUB * TOPK).rearrange("p (n c) -> p n c", n=NSUB)
        topf = cut(NSUB * TOPK).rearrange("p (n c) -> p n c", n=NSUB)
        cand = cut(PH * 256).rearrange("p (h c) -> p h c", h=PH)
        cs = cut(PH * TOPK).rearrange("p (h c) -> p h c", h=PH)
        ci = cut(PH * TOPK).rearrange("p (h c) -> p h c", h=PH)
        cab = cut(2 * PH * TOPK).rearrange("p (s h c) -> p s h c", s=2, h=PH)
        cabf = cut(2 * PH * TOPK).rearrange("p (s h c) -> p s h c", s=2, h=PH)
        hot = cut(PH * TOPK * TOPK).rearrange("p (h k a) -> p h k a", h=PH, k=TOPK)
        sel = cut(3 * 3 * 128).rearrange("p (t s c) -> p t s c", t=3, s=3)
        hsum = cut(2 * PH).rearrange("p (s h) -> p s h", s=2)
        hotB2 = big[:, BIG:BIG + 512].rearrange("p (a b) -> p a b", a=4)
        yacc = big[:, 0:KD * T].rearrange("p (k t) -> p k t", k=KD)
        fin = stream[:, 0:3 * D].rearrange("p (t c) -> p t c", t=3)
        gfin = stream[:, 4096:4096 + D]

        ps = ctx.enter_context(nc.psum_tensor("ps", [P, 8, 512], F32))

        product = sem("product")
        moved_v = sem("moved_by_vector")
        moved_a = sem("moved_by_scalar")
        small_ld = sem("small_loads")
        w_ld = [sem("weights_even"), sem("weights_odd")]
        uq_ld = sem("wuq_loaded")
        conv_ld = sem("conv_loaded")
        past_ld = sem("past_loaded")
        kw_ld = sem("window_keys_loaded")
        kw_used = sem("window_keys_used")
        vw_ld = [sem("window_values_even"), sem("window_values_odd")]
        vw_used = sem("window_values_used")
        sk_ld = sem("subkeys_loaded")
        vstep = sem("vector_step")
        pad_set = sem("pads_set")
        sq_ready = sem("squares_ready")
        std_ready = sem("std_ready")
        hn_ready = sem("normed_ready")
        lat_ready = sem("latents_ready")
        qk_ready = sem("window_qk_ready")
        q_ready = sem("q_rotated")
        sig_ready = sem("sigmoid_ready")
        g_ready = sem("glu_ready")
        nmx_ready = sem("negmax_ready")
        exp_ready = sem("exp_ready")
        cnt_ready = sem("counted_ready")
        y_ready = sem("conv_ready")
        ln_ready = sem("conv_normed")
        smx_ready = sem("sample_max_ready")
        sdg_ready = sem("sample_diag_ready")
        sexp_ready = sem("sample_exp_ready")
        sden_ready = sem("sample_den_ready")
        stored = sem("stores_done")
        cand_max = sem("gate_logits_ready")
        gexp = sem("gate_exp_ready")
        sel_ready = sem("selection_ready")
        hotA_ready = sem("onehot_a_ready")
        hotB_ready = sem("onehot_b_ready")
        g_prod = sem("gate_product")
        g_moved = sem("gate_moved")
        g_done = sem("gates_done")
        acc_zero = sem("acc_zero")
        u_ld = [sem(f"u_loaded{i}") for i in range(UN)]
        v_ld = [sem(f"v_loaded{i}") for i in range(UN)]
        u_free = [sem(f"u_free{i}") for i in range(UN)]
        v_free = [sem(f"v_free{i}") for i in range(UN)]
        turned = sem("u_turned")
        acc_done = sem("acc_done")
        uT_v = sem("uT_by_vector")
        uT_a = sem("uT_by_scalar")
        z_prod = sem("expert_inputs")
        gelu_done = sem("gelu_done")
        w_ready = sem("expert_weights")
        y_moved = sem("peer_out_moved")
        copied = sem("window_copied")
        ended = sem("engines_at_layer_end")
        f_gld = ctx.enter_context(nc.semaphore("final_gain_loaded"))
        store = ctx.enter_context(nc.semaphore("store"))
        consts_ld = ctx.enter_context(nc.semaphore("consts_loaded"))
        ones_set = ctx.enter_context(nc.semaphore("ones_set"))
        go = [ctx.enter_context(nc.semaphore(f"next_layer_{e}")) for e in ("pe", "act", "dve", "pool")]
        f_sq, f_std, f_out, f_step, f_y = (ctx.enter_context(nc.semaphore(n)) for n in
                                     ("final_squares", "final_std", "final_stored", "final_step", "final_y"))
        moved = {"V": moved_v, "A": moved_a}
        def wait_moved(eng, *name):
            who, n = READ[name]
            eng.wait_ge(moved[who], n)

        def bank(*name):
            return ps[:, NUM[name] % 8]

        def arrive(eng, *name):
            eng.wait_ge(product, NUM[name] + 1)
            return bank(*name)

        def layer_end(eng, i):
            eng.nop().then_inc(ended, 1)
            eng.wait_ge(go[i], 1)
            eng.sem_clear(go[i])

        def L(name, l):
            a = A[name][bass.ds(l, 1)]
            names = " ".join("abcdef"[:len(a.shape) - 1])
            return a.rearrange(f"o {names} -> (o {names.split(' ')[0]}) {' '.join(names.split(' ')[1:])}")

        def O(ap, l):
            a = ap[bass.ds(l, 1)]
            names = "abcdef"[:len(a.shape) - 1]
            return a.rearrange(f"o {' '.join(names)} -> (o {names[0]}) {' '.join(names[1:])}")

        WCH = ([("w_in", c0, n) for c0, n in ZCH] + [("w_out", 512 * c, 512) for c in range(2)]
               + [("peer_wq", 512 * c, 512) for c in range(4)])

        W_LAST = [NUM["z", c, 2] + 1 for c in range(5)] + [NUM["xo", c, 2] + 1 for c in range(2)]
        W_LAST += [NUM["pq", 4 * c + 3] + 1 for c in range(4)]

        def wview(n):
            k = WCH[n][2]
            return wslot[n % 2][:, 0:KD * k].rearrange("p (k c) -> p k c", k=KD)

        block = ctx.enter_context(nc.Block())

        @block.sync
        def _(sp):
            sp.dma_start(ident[:, :], C["ident"]).then_inc(consts_ld, 16)
            sp.dma_start(iota[:, :], C["iota"]).then_inc(consts_ld, 16)
            sp.dma_start(rope[:, :, :], C["rope"]).then_inc(consts_ld, 16)
            sp.dma_start(diag[:, :], C["diag"]).then_inc(consts_ld, 16)
            sp.dma_start(pages[0:1, :], A["page_table"].rearrange("(o b) g -> o (b g)", o=1)).then_inc(consts_ld, 16)
            for t, (t0, n) in enumerate(TOK[:2]):
                sp.dma_start(X[:, t, :], A["x_prompt"][0, t0:t0 + n, :]).then_inc(consts_ld, 16)
            sp.dma_start(X[0:NB, 2, :], A["x_sample"].rearrange("b s d -> (b s) d")).then_inc(consts_ld, 16)
            sp.wait_ge(consts_ld, 16 * 8)

            with sp.Fori(0, DEPTH) as l:
                def load_w(n):
                    if n >= 2:
                        sp.wait_ge(product, W_LAST[n - 2])
                    name, c0, k = WCH[n]
                    src = L(name, l).rearrange("(k p) c -> p k c", p=P)[:, :, c0:c0 + k]
                    sp.dma_start(wview(n), src).then_inc(w_ld[n % 2], 16)

                def load_past(half):
                    with sp.Fori(0, 4) as b:
                        with sp.Fori(0, NPG) as g:
                            pg = sp.value_load(pages[0:1, bass.ds((half * 4 + b) * NPG + g, 1)], min_val=0,
                                               max_val=A["cache_kv_latent"].shape[1] - 1)
                            c_src = L("cache_kv_latent", l)[bass.ds(pg, 1)].rearrange("o p c -> (o p) c")
                            r_src = L("cache_k_rope", l)[bass.ds(pg, 1)].rearrange("o p c -> (o p) c")
                            c_dst = past[:, bass.ds(b, 1), bass.ds(g, 1), :].rearrange("p b g c -> p (b g c)")
                            r_dst = pastr[:, bass.ds(b, 1), bass.ds(g, 1), :].rearrange("p b g c -> p (b g c)")
                            sp.dma_start(c_dst, c_src).then_inc(past_ld, 16)
                            sp.dma_start(r_dst, r_src).then_inc(past_ld, 16)

                def window_rows(name, b, d):
                    lo = PAST - 128 * d
                    rows = L(name, l)[b, lo:PAST, :, :]
                    return rows.rearrange("(k r) h c -> k r (h c)", r=d)[:, 0, :]

                load_w(0)
                load_w(1)
                with nc.allow_non_contiguous_dma(reason="per-channel gains, a few KB"):
                    sp.dma_start(g_mix, L("norm_mix", l).rearrange("(k p) -> p k", p=P)).then_inc(small_ld, 16)
                    sp.dma_start(g_ffn, L("norm_ffn", l).rearrange("(k p) -> p k", p=P)).then_inc(small_ld, 16)
                    sp.dma_start(g_q, L("q_norm", l).rearrange("(k p) -> p k", p=P)).then_inc(small_ld, 16)
                    sp.dma_start(g_cb, L("conv_b", l).rearrange("(k p) -> p k", p=P)).then_inc(small_ld, 16)
                    sp.dma_start(g_lg, L("conv_ln_g", l).rearrange("(k p) -> p k", p=P)).then_inc(small_ld, 16)
                    sp.dma_start(g_lb, L("conv_ln_b", l).rearrange("(k p) -> p k", p=P)).then_inc(small_ld, 16)
                sp.dma_start(kvg, A["kv_norm"][bass.ds(l, 1)].to_broadcast([P, LAT])).then_inc(small_ld, 16)
                for i, m in enumerate((cnt, cbias, mbias)):
                    sp.dma_start(m, C["masks"][:, i * 384:(i + 1) * 384]).then_inc(small_ld, 16)
                sp.dma_start(wuq, L("w_uq", l).rearrange("(k p) c -> p k c", p=P)).then_inc(uq_ld, 16)
                wukv_src = L("w_ukv", l).rearrange("c (h a x) -> c a h x", h=NH, a=2)
                sp.dma_start(wuk.rearrange("p (h x) -> p h x", h=NH), wukv_src[:, 0]).then_inc(uq_ld, 16)
                sp.dma_start(wuv.rearrange("p (h x) -> p h x", h=NH), wukv_src[:, 1]).then_inc(uq_ld, 16)
                sp.dma_start(cwr, L("conv_w", l)).then_inc(conv_ld, 16)
                sp.dma_start(scr, L("state_conv", l).rearrange("(s b) j c -> (b j) s c", s=2)).then_inc(conv_ld, 16)
                for n in range(2, 7):
                    load_w(n)
                wait_moved(sp, "sc", 1)
                sp.wait_ge(q_ready, 1)
                sp.wait_ge(y_ready, 1)
                sp.wait_ge(product, W_LAST[3])
                load_past(0)

                def load_kw(b):
                    if b >= 1:
                        sp.wait_ge(kw_used, b)
                    for i, d in enumerate(DIL):
                        sp.dma_start(kw[:, i, :], window_rows("state_win_k", b, d)).then_inc(kw_ld, 16)

                def load_vw(b):
                    if b >= 2:
                        sp.wait_ge(vw_used, b - 1)
                    for i, d in enumerate(DIL):
                        sp.dma_start(vw[:, b % 2, i, :], window_rows("state_win_v", b, d)).then_inc(vw_ld[b % 2], 16)

                load_kw(0)
                wait_moved(sp, "qrS")
                load_vw(0)
                load_vw(1)
                for b in range(1, NB):
                    load_kw(b)
                sp.wait_ge(product, NUM["ol", 0] + 1)
                load_past(1)
                for b in range(2, NB):
                    load_vw(b)
                sp.wait_ge(stored, 1)
                sp.wait_ge(product, W_LAST[6])
                for n in range(NSUB):
                    sp.dma_start(sk[:, n, :], L("peer_subkeys", l)[n // 2, n % 2]).then_inc(sk_ld, 16)
                for n in range(7, 11):
                    load_w(n)
                sp.wait_ge(product, NUM["slot", 2] + 1)
                u_l = L("peer_u", l).rearrange("(i j) d -> i j d", j=NK)
                v_l = L("peer_v", l).rearrange("(i j) d -> i j d", j=NK)
                for k in range(UN):
                    sp.nop().then_inc(u_free[k], 1)
                    sp.nop().then_inc(v_free[k], 1)
                with sp.Fori(0, NB) as b:
                    for half, (src, dst) in enumerate((("state_win_k", wk_s), ("state_win_v", wv_s))):
                        s_ap = L(src, l)[bass.ds(b, 1), 1:PAST].rearrange("o r h c -> (o r) (h c)")
                        d_ap = O(dst, l)[bass.ds(b, 1), 0:PAST - 1].rearrange("o r h c -> (o r) (h c)")
                        for m in range(2):
                            for k in range(UN):
                                j = b * (4 * UN) + (half * 2 * UN + m * UN + k)
                                sp.wait_ge(u_free[k], 1)
                                sp.sem_clear(u_free[k])
                                sp.dma_start(u_t[k], u_l[:, bass.ds(j, 1), :].rearrange("i o d -> i (o d)")).then_inc(u_ld[k], 16)
                                sp.wait_ge(v_free[k], 1)
                                sp.sem_clear(v_free[k])
                                sp.dma_start(v_t[k], v_l[:, bass.ds(j, 1), :].rearrange("i o d -> i (o d)")).then_inc(v_ld[k], 16)
                            if m == 0:
                                sp.dma_start(d_ap, s_ap).then_inc(copied, 16)
                sp.wait_ge(copied, 16 * 2 * NB)
                sp.wait_ge(ended, 4)
                for s in layer_sems:
                    sp.sem_clear(s)
                for s in go:
                    sp.nop().then_inc(s, 1)
            sp.dma_start(gfin, A["norm_final"].rearrange("(o d) -> o d", o=1).to_broadcast([P, D])).then_inc(f_gld, 16)
            for t, (t0, n) in enumerate(TOK):
                sp.wait_ge(f_y, t + 1)
                dst = y_p[0, t0:t0 + n, :] if t < 2 else y_s.rearrange("b s d -> (b s) d")
                sp.dma_start(dst, fin[0:n, t, :]).then_inc(f_out, 16)
            sp.wait_ge(f_out, 16 * 3)

        @block.gpsimd
        def _(pool):
            pool.memset(ones[:, :], 1.0)
            pool.memset(stat[:, :], 1.0).then_inc(ones_set, 1)
            with pool.Fori(0, DEPTH) as l:
                pool.memset(z[:, 2, :], 0.0).then_inc(pad_set, 1)
                pool.memset(gT[:, :, 0:CW - 1], 0.0)
                pool.memset(qrB.rearrange("p b i h -> p (b i h)"), 0.0).then_inc(pad_set, 1)
                n_st = [0]

                def put(dst, src):
                    pool.dma_start(dst, src).then_inc(store, 16)
                    n_st[0] += 16

                def put_tokens(prompt, sample, col, n, rows=2):
                    for t in range(2):
                        put(O(prompt, l)[0, 128 * t:128 * t + 128], z[:, t, col:col + n])
                    put(sample, z[0:NB, 2, col:col + n])

                pool.wait_ge(lat_ready, 2)
                for t in range(2):
                    put(O(lat_p, l)[0, 128 * t:128 * t + 128, :], z[:, t, CKV:CKV + LAT])
                    put(O(kr_p, l)[0, 128 * t:128 * t + 128, :], z[:, t, KR:KR + ROPE])
                put(O(lat_s, l)[:, 0, :], z[0:NB, 2, CKV:CKV + LAT])
                put(O(kr_s, l)[:, 0, :], z[0:NB, 2, KR:KR + ROPE])
                pool.wait_ge(qk_ready, 1)
                for t in range(2):
                    put(O(wk_p, l)[0, 128 * t:128 * t + 128].rearrange("r h c -> r (h c)"), z[:, t, KB:KB + 384])
                put(O(wk_s, l)[:, PAST - 1].rearrange("b h c -> b (h c)"), z[0:NB, 2, KB:KB + 384])
                wait_moved(pool, "z", 3, 2)
                for t in range(2):
                    put(O(wv_p, l)[0, 128 * t:128 * t + 128].rearrange("r h c -> r (h c)"), z[:, t, VB:VB + 384])
                put(O(wv_s, l)[:, PAST - 1].rearrange("b h c -> b (h c)"), z[0:NB, 2, VB:VB + 384])
                pool.wait_ge(g_ready, 1)
                put(O(cv_p, l)[0], z[128 - (CW - 1):128, 1, GA:GA + CC])
                put(O(cv_s, l)[:, CW - 2, :], z[0:NB, 2, GA:GA + CC])
                put(O(cv_s, l)[:, 0:CW - 2, :], L("state_conv", l)[:, 1:CW - 1, :])
                pool.wait_ge(store, l * n_st[0] + n_st[0])
                pool.nop().then_inc(stored, 1)
                layer_end(pool, 3)

        @block.tensor
        def _(pe):
            def begin(*name):
                n = NUM[name]
                if n >= 8:
                    wait_moved(pe, *JOBS[n - 8][0])
                return ps[:, n % 8]

            def turn(*name, parts):
                o = begin(*name)
                for src, rows, cols, c0 in parts:
                    mm = pe.transpose(o[0:cols, c0:c0 + rows], src, ident[0:rows, 0:rows])
                mm.then_inc(product, 1)

            def dense(name, parts, n_out, cols):
                o = begin(*name)
                for i, (lhs, rhs) in enumerate(parts):
                    mm = pe.matmul(o[0:n_out, 0:cols], lhs, rhs, start=(i == 0), stop=(i == len(parts) - 1))
                mm.then_inc(product, 1)

            def tokens(src, c0, n=128):
                return [(src[0:m, t, c0:c0 + n], m, n, t0) for t, (t0, m) in enumerate(TOK)]

            pe.wait_ge(consts_ld, 16 * 8)
            pe.wait_ge(ones_set, 1)
            with pe.Fori(0, DEPTH) as l:
                pe.wait_ge(hn_ready, 3)
                for k in range(KD):
                    turn("hT", k, parts=tokens(hn, k * 128))
                wait_moved(pe, "hT", KD - 2)
                wait_moved(pe, "hT", KD - 1)
                for c, (c0, n) in enumerate(ZCH):
                    pe.wait_ge(w_ld[c % 2], 16 * (c // 2 + 1))
                    for t, (t0, m) in enumerate(TOK):
                        dense(("z", c, t), [(hT[:, k, t0:t0 + m], wview(c)[:, k, :]) for k in range(KD)], m, n)
                pe.wait_ge(lat_ready, 1)
                for k in range(2):
                    turn("cqT", k, parts=tokens(z, CQ + 128 * k))
                pe.wait_ge(lat_ready, 3)
                turn("ckvT", parts=tokens(z, CKV))
                turn("krT", parts=[(krr[0:m, t, :, :].rearrange("p r c -> p (r c)"), m, 128, t0) for t, (t0, m) in enumerate(TOK)])
                pe.wait_ge(uq_ld, 48)
                turn("ukT", parts=[(wuk[:, 128 * g:128 * g + 128], 128, 128, g * 128) for g in range(HP)])
                wait_moved(pe, "cqT", 1)
                for t, (t0, m) in enumerate(TOK):
                    for n in range(2):
                        dense(("q", t, n), [(cqT[:, k, t0:t0 + m], wuq[:, k, n * 288:(n + 1) * 288]) for k in range(2)], m, 288)
                pe.wait_ge(qk_ready, 1)
                for g in range(HP):
                    turn("qbT", g, parts=tokens(z, QB + 128 * g))
                for g in range(HP):
                    turn("kbT", g, parts=tokens(z, KB + 128 * g))
                pe.wait_ge(q_ready, 1)
                for g in range(HP):
                    turn("qnT", g, parts=tokens(q, 128 * g))
                for g, hs in enumerate((4, 2)):
                    turn("qrT", g, parts=tokens(q, NH * NOPE + 128 * g, 32 * hs))
                turn("qrS", parts=[(qrr[0:NB, h, :, :].rearrange("p r c -> p (r c)"), NB, 128, h * NB)
                                   for h in range(NH)])
                wait_moved(pe, "qnT", HP - 1)
                for h in range(NH):
                    r0 = 64 * (h % 2)
                    dense(("qlT", h), [(ukT[r0:r0 + 64, h // 2, :], qnT[r0:r0 + 64, h // 2, :])], 128, T)
                for t in range(2):
                    dense(("va", t), [(ckvT[:, 128 * t:128 * t + 128], wuv)], 128, 384)
                pe.wait_ge(conv_ld, 32)
                turn("cw", parts=[(cwr[:, 128 * c:128 * c + 128], CW, 128, CW * c) for c in range(2)])
                for c in range(2):
                    turn("sc", c, parts=[(scr[:, s, 128 * c:128 * c + 128], 120, 128, 120 * s) for s in range(2)])
                pe.wait_ge(g_ready, 1)
                for c in range(2):
                    turn("gT", c, parts=tokens(z, GA + 128 * c))
                wait_moved(pe, "qlT", NH - 1)
                wait_moved(pe, "va", 1)

                def scores(u):
                    o = begin("S", u)
                    h = u % NH
                    for i, c0 in ((0, 0), (1, 128)):
                        K = 128 * (i + 1)
                        qs = slice(128 * i, 128 * i + 128)
                        if u < NH:
                            r0 = 32 * (h % 4)
                            pe.matmul(o[:, c0:c0 + K], qlT[:, h, qs], ckvT[:, 0:K], start=True, stop=False)
                            mm = pe.matmul(o[:, c0:c0 + K], qrT[r0:r0 + 32, h // 4, qs], krT[r0:r0 + 32, 0:K], start=False, stop=True)
                        else:
                            r0 = 64 * (h % 2)
                            mm = pe.matmul(o[:, c0:c0 + K], qbT[r0:r0 + 64, h // 2, qs], kbT[r0:r0 + 64, h // 2, 0:K], start=True, stop=True)
                    mm.then_inc(product, 1)

                def turn_probs(u):
                    if u < NH:
                        pe.wait_ge(exp_ready, u + 1)
                    else:
                        pe.wait_ge(cnt_ready, u - NH + 1)
                    turn("PT", u, parts=[(prob[:, u % 2, 128 * i:128 * i + 128], 128, 128, 128 * i) for i in range(3)])

                def mix_values(u):
                    wait_moved(pe, "PT", u)
                    o = begin("O", u)
                    v = [va[:, t, 64 * u:64 * u + 64] if u < NH else z[:, t, VB + 64 * (u - NH):VB + 64 * (u - NH) + 64] for t in range(2)]
                    pt = probT[:, u % 2, :]
                    pe.matmul(o[:, 0:64], pt[:, 0:128], v[0], start=True, stop=True)
                    pe.matmul(o[:, 64:128], pt[:, 128:256], v[0], start=True, stop=False)
                    pe.matmul(o[:, 64:128], pt[:, 256:384], v[1], start=False, stop=True).then_inc(product, 1)

                for s in range(2 * NH + 2):
                    if s < 2 * NH:
                        scores(s)
                    if 1 <= s <= 2 * NH:
                        turn_probs(s - 1)
                    if s >= 2:
                        mix_values(s - 2)
                wait_moved(pe, "O", 2 * NH - 1)
                for g in range(2 * HP):
                    turn("mT", g, parts=[(oAB[:, t, 128 * g:128 * g + 128], 128, 128, 128 * t) for t in range(2)])
                pe.wait_ge(y_ready, 1)
                for t, (t0, m) in enumerate(TOK):
                    turn("yt", t, parts=[(yT[:, c, t0:t0 + m], 128, m, 128 * c) for c in range(2)])
                pe.wait_ge(ln_ready, 3)
                for c in range(2):
                    turn("ycT", c, parts=tokens(yt, 128 * c))

                def score_past(b):
                    wait_moved(pe, "cT", b, 3)
                    wait_moved(pe, "rT", b)
                    o = begin("ST", b)
                    for g in range(NPG // 4):
                        pe.matmul(o[:, 24 * g:24 * g + 24], rT[:, b % 2, g, :], qrB[:, b, :, :], start=True, stop=False, skip_group_check=True)
                        for i in range(4 * g, 4 * g + 4):
                            mm = pe.matmul(o[:, NH * i:NH * i + NH], cT[:, b % 2, 128 * i:128 * i + 128], qlT[:, :, SEQ + b],
                                           start=False, stop=True, skip_group_check=True)
                    mm.then_inc(product, 1)

                def past_half(half):
                    pe.wait_ge(past_ld, 16 * 2 * 4 * NPG * (half + 1))
                    for b in range(4 * half, 4 * half + 5):
                        if b < 4 * half + 4:
                            for g in range(4):
                                turn("cT", b, g, parts=[(past[:, b % 4, 4 * g + i, :], 128, 128, 128 * i) for i in range(4)])
                            turn("rT", b, parts=[(pastr[:, b % 4, 4 * g:4 * g + 4, :].rearrange("p g c -> p (g c)"), 128, 128, 128 * g) for g in range(4)])
                        if b > 4 * half:
                            score_past(b - 1)

                def maxima(n, c):
                    pe.wait_ge(smx_ready, n + 1 if n < 1 else (2 if n == 2 else 3))
                    turn("mx", n, parts=[(smx[:, n, 0:c], 128, c, 0)])
                    pe.wait_ge(sdg_ready, n + 1 if n < 1 else (2 if n == 2 else 3))
                    dense(("mb", n), [(ones[0:c, :], sdg[0:c, n, 0:c])], 128, c)
                    pe.wait_ge(sden_ready, n + 1 if n < 1 else (2 if n == 2 else 3))
                    dense(("dn", n), [(ones[:, :], sden[:, n, 0:c])], 128, c)

                def latent_mix(half):
                    o = begin("ol", half)
                    pe.matmul(o[:, 0:24], z[0:NB, 2, CKV:CKV + LAT], STm[0:NB, :, NPG, :], start=True, stop=False, skip_group_check=True)
                    for b in range(4):
                        for g in range(NPG):
                            mm = pe.matmul(o[:, NH * b:NH * b + NH], past[:, b, g, :], STm[:, b, g, :], start=False,
                                           stop=(g == NPG - 1), skip_group_check=True)
                    mm.then_inc(product, 1)

                past_half(0)
                o = begin("ext")
                pe.matmul(o[0:NB, 0:48], ckvT[:, SEQ:T], qlT[:, :, SEQ:T], start=True, stop=False)
                pe.matmul(o[0:NB, 0:48], krT[0:32, SEQ:T], qrS[0:32, :, :], start=False, stop=True).then_inc(product, 1)
                for b in range(NB):
                    dense(("qbc", b), [(ident[0:NB, b:b + 1].to_broadcast([NB, P]), z[0:NB, 2, QB:QB + 384])], 128, 384)
                maxima(0, 24)
                latent_mix(0)
                past_half(1)
                maxima(2, 48)
                maxima(1, 24)
                latent_mix(1)
                wait_moved(pe, "ol", 1)
                o = begin("os")
                for h in range(NH):
                    r0 = 64 * (h % 2)
                    mm = pe.matmul(o[r0:r0 + 64, NB * (h // 2):NB * (h // 2) + NB], wuv[:, HD * h:HD * h + HD], olT[:, :, h],
                                   start=True, stop=True, skip_group_check=True)
                mm.then_inc(product, 1)
                o = begin("ow")
                for h in range(NH):
                    r0 = 64 * (h % 2)
                    pe.matmul(o[r0:r0 + 64, NB * (h // 2):NB * (h // 2) + NB], z[0:NB, 2, VB + 64 * h:VB + 64 * h + 64], STw[0:NB, :, 3, h],
                              start=(h < 2), stop=False, skip_group_check=True)
                for b in range(NB):
                    pe.wait_ge(vw_ld[b % 2], 48 * (b // 2 + 1))
                    for d in range(3):
                        for h in range(NH):
                            r0 = 64 * (h % 2)
                            c0 = NB * (h // 2) + b
                            mm = pe.matmul(o[r0:r0 + 64, c0:c0 + 1], vw[:, b % 2, d, 64 * h:64 * h + 64], STw[:, b, d, h:h + 1],
                                           start=False, stop=(d == 2), skip_group_check=True)
                    mm.then_inc(vw_used if b < NB - 1 else product, 1)
                wait_moved(pe, "mT", 5)
                wait_moved(pe, "ow")
                for c in range(2):
                    pe.wait_ge(w_ld[(5 + c) % 2], 16 * ((5 + c) // 2 + 1))
                    for t, (t0, m) in enumerate(TOK):
                        dense(("xo", c, t), [(mixT[:, k, t0:t0 + m], wview(5 + c)[:, k, :]) for k in range(KD)], m, 512)
                pe.wait_ge(hn_ready, 6)
                for k in range(KD):
                    turn("fT", k, parts=tokens(hf, k * 128))
                pe.wait_ge(sk_ld, 16 * NSUB)
                for g in range(4):
                    turn("skT", g, parts=[(sk[:, 4 * g + i, :], 128, 128, 128 * i) for i in range(4)])
                wait_moved(pe, "fT", KD - 2)
                wait_moved(pe, "fT", KD - 1)
                for n in range(NSUB):
                    w = 7 + n // 4
                    if n % 4 == 0:
                        pe.wait_ge(w_ld[w % 2], 16 * (w // 2 + 1))
                    dense(("pq", n), [(wview(w)[:, k, 128 * (n % 4):128 * (n % 4) + 128], hT[:, k, :]) for k in range(KD)], 128, T)
                wait_moved(pe, "pq", NSUB - 1)
                for t, (t0, m) in enumerate(TOK):
                    for g in range(4):
                        o = begin("s", t, g)
                        for i in range(4):
                            n = 4 * g + i
                            mm = pe.matmul(o[0:m, 128 * i:128 * i + 128], pqT[:, n, t0:t0 + m], skT[:, n, :], start=True, stop=True)
                        mm.then_inc(product, 1)
                for t, (t0, m) in enumerate(TOK):
                    pe.wait_ge(sel_ready, t + 1)
                    turn("slot", t, parts=[(sel[0:m, t, s, :], m, 128, 128 * s) for s in range(3)])
                wait_moved(pe, "slot", 2)
                for _ in range(2):
                    pe.nop().then_inc(g_prod, 1)
                with pe.Fori(0, T // GT) as it:
                    for g in range(2):
                        pe.wait_ge(hotA_ready, it * 2 + (g + 1))
                        pe.wait_ge(hotB_ready, it * 2 + (g + 1))
                        pe.wait_ge(g_moved, it * 2 + (g + 1))
                        hb = hotB if g == 0 else hotB2
                        for k in range(4):
                            mm = pe.matmul(ps[:, 6 + g, 128 * k:128 * k + 128], hotA[:, 4 * g + k, :], hb[:, k, :], start=True, stop=True)
                        mm.then_inc(g_prod, 1)
                pe.wait_ge(g_moved, 2 * (T // GT) + 2)
                pe.wait_ge(acc_zero, 1)
                for n in range(5):
                    pe.matmul(ps[:, n, 0:512 if n < 4 else 64], zeros[:, 0:128], zeros[:, 0:512 if n < 4 else 64],
                              start=True, stop=False, skip_group_check=True)
                with pe.Fori(0, LOOPS) as it:
                    def turn_u(k):
                        pe.wait_ge(u_ld[k], it * 16 + 16)
                        for half, sem_ in ((0, uT_v), (1, uT_a)):
                            pe.wait_ge(sem_, it * UN + (k + 1))
                            for i in range(4):
                                c = 4 * half + i
                                mm = pe.transpose(ps[:, 6 + half, 128 * i:128 * i + 128], u_t[k][:, 128 * c:128 * c + 128], ident[:, :])
                            mm.then_inc(turned, 1)

                    def inputs(k):
                        pe.wait_ge(uT_v, it * UN + (k + 2))
                        pe.wait_ge(uT_a, it * UN + (k + 2))
                        pe.wait_ge(gelu_done, it * UN + (k + 1))
                        for c in range(KD):
                            mm = pe.matmul(ps[:, 5, 0:T], uT[k % 2][:, 128 * c:128 * c + 128], hT[:, c, :], start=(c == 0), stop=(c == KD - 1))
                            if c == 0:
                                mm.then_inc(u_free[k], 1)
                        mm.then_inc(z_prod, 1)

                    def outputs(k):
                        pe.wait_ge(v_ld[k], it * 16 + 16)
                        pe.wait_ge(w_ready, it * UN + (k + 1))
                        for c in range(KD):
                            w = v_t[k][:, 128 * c:128 * c + 128]
                            pe.matmul(ps[:, c // 2, 256 * (c % 2):256 * (c % 2) + 256], w, wgt_t[k % 2][:, 0:SEQ],
                                      start=False, stop=False, skip_group_check=True)
                            mm = pe.matmul(ps[:, 4, NB * c:NB * c + NB], w, wgt_t[k % 2][:, SEQ:T],
                                           start=False, stop=False, skip_group_check=True)
                        mm.then_inc(v_free[k], 1)

                    for k in range(UN + 2):
                        if k < UN:
                            turn_u(k)
                        if 1 <= k <= UN:
                            inputs(k - 1)
                        if k >= 2:
                            outputs(k - 2)
                pe.transpose(ps[:, 5, 0:128], ident[:, :], ident[:, :]).then_inc(acc_done, 1)
                pe.wait_ge(y_moved, 1)
                for c in range(2):
                    for t, (t0, m) in enumerate(TOK):
                        turn("xT", c, t, parts=[(yacc[:, 4 * c + i, t0:t0 + m], 128, m, 128 * i) for i in range(4)])
                pe.wait_ge(product, len(JOBS))
                layer_end(pe, 0)

        @block.scalar
        def _(act):
            def read(*name):
                who, n = READ[name]
                seen[0] += 1
                assert who == "A" and n == seen[0], name
                return arrive(act, *name)

            seen = [0]
            act.wait_ge(ones_set, 1)
            act.wait_ge(consts_ld, 16 * 8)
            with act.Fori(0, DEPTH) as l:
                seen[0] = 0

                def roots(k, cols):
                    act.wait_ge(sq_ready, k[0])
                    act.activation(stat[:, cols], stat[:, cols], ACT.Sqrt).then_inc(std_ready, 1)

                roots((3,), slice(0, 3))
                act.wait_ge(small_ld, 16 * 10)
                for k in range(1, KD, 2):
                    o = read("hT", k)
                    act.activation(hT[:, k, :], o[:, 0:T], ACT.Copy, scale=g_mix[:, k:k + 1]).then_inc(moved_a, 1)
                act.wait_ge(pad_set, 2)
                for c, (c0, n) in enumerate(ZCH):
                    for t, (t0, m) in enumerate(TOK):
                        o = read("z", c, t)
                        if c < 4:
                            act.copy(z[0:m, t, c0:c0 + n], o[0:m, 0:n]).then_inc(moved_a, 1)
                        else:
                            act.copy(z[0:m, t, GA:GA + CC], o[0:m, 0:CC])
                            act.activation(z[0:m, t, GB:GB + CC], o[0:m, CC:2 * CC], ACT.Sigmoid).then_inc(moved_a, 1)
                    if c == 1:
                        roots((4,), slice(3, 9))
                for k in range(2):
                    o = read("cqT", k)
                    act.activation(cqT[:, k, :], o[:, 0:T], ACT.Copy, scale=g_q[:, k:k + 1]).then_inc(moved_a, 1)
                o = read("ckvT")
                act.copy(ckvT, o[:, 0:T]).then_inc(moved_a, 1)
                o = read("krT")
                act.copy(krT, o[:, 0:T]).then_inc(moved_a, 1)
                o = read("ukT")
                act.copy(ukT.rearrange("p g c -> p (g c)"), o[:, 0:384]).then_inc(moved_a, 1)
                for t, (t0, m) in enumerate(TOK):
                    for n in range(2):
                        o = read("q", t, n)
                        oh = o[0:m, 0:288].rearrange("p (h x) -> p h x", h=3)
                        qn = q[0:m, t, 192 * n:192 * n + 192].rearrange("p (h x) -> p h x", h=3)
                        qr = q[0:m, t, NH * NOPE + 96 * n:NH * NOPE + 96 * n + 96].rearrange("p (h x) -> p h x", h=3)
                        act.copy(qn, oh[:, :, 0:NOPE])
                        act.copy(qr, oh[:, :, NOPE:]).then_inc(moved_a, 1)
                for g in range(HP):
                    o = read("qnT", g)
                    act.copy(qnT[:, g, :], o[:, 0:T]).then_inc(moved_a, 1)
                o = read("qrT", 0)
                act.copy(qrT[:, 0, :], o[:, 0:T]).then_inc(moved_a, 1)
                o = read("qrT", 1)
                act.copy(qrT[0:64, 1, :], o[0:64, 0:T]).then_inc(moved_a, 1)
                o = read("qrS")
                for i in range(4):
                    act.copy(qrB[32 * i:32 * i + 32, :, i, :], o[32 * i:32 * i + 32, 0:48].rearrange("p (h b) -> p b h", h=NH))
                act.copy(qrS.rearrange("p h b -> p (h b)"), o[:, 0:48]).then_inc(moved_a, 1)
                for t in range(2):
                    o = read("va", t)
                    act.copy(va[:, t, :], o[:, 0:384]).then_inc(moved_a, 1)
                o = read("cw")
                act.copy(cwT.rearrange("p c j -> p (c j)"), o[:, 0:2 * CW]).then_inc(moved_a, 1)
                for c in range(2):
                    o = read("sc", c)
                    act.copy(gsT[:, c, :, 0:CW - 1], o[:, 0:240].rearrange("p (b j) -> p b j", b=NB)).then_inc(moved_a, 1)
                for s in range(2 * NH + 1):
                    if s < 2 * NH:
                        act.wait_ge(nmx_ready, s + 1)
                        for i, c0 in ((0, 0), (1, 128)):
                            pr = prob[:, s % 2, c0:c0 + 128 * (i + 1)]
                            e = act.activation(pr, pr, ACT.Exp, bias=nmx[:, s, i:i + 1], scale=SA if s < NH else SB,
                                               accum_out=den[:, s, i:i + 1] if s < NH else None)
                        e.then_inc(exp_ready, 1)
                    if s >= 1:
                        o = read("PT", s - 1)
                        act.copy(probT[:, (s - 1) % 2, :], o[:, 0:384]).then_inc(moved_a, 1)
                for g in range(2 * HP):
                    o = read("mT", g)
                    act.copy(mixT[:, g, 0:SEQ], o[:, 0:SEQ]).then_inc(moved_a, 1)
                for t, (t0, m) in enumerate(TOK):
                    o = read("yt", t)
                    act.copy(yt[0:m, t, :], o[0:m, 0:CC]).then_inc(moved_a, 1)
                roots((5,), slice(9, 12))
                for c in range(2):
                    o = arrive(act, "ycT", c)
                    act.activation(ycs[:, c, :], o[:, 0:T], ACT.Sigmoid, bias=g_lb[:, c:c + 1], scale=g_lg[:, c:c + 1]).then_inc(sig_ready, 1)

                def past_half(half):
                    for b in range(4 * half, 4 * half + 5):
                        if b < 4 * half + 4:
                            for g in range(0, 4, 2):
                                o = read("cT", b, g)
                                act.copy(cT[:, b % 2, 512 * g:512 * g + 512], o[:, 0:512]).then_inc(moved_a, 1)
                            o = read("rT", b)
                            act.copy(rT[:, b % 2, :, :].rearrange("p g k -> p (g k)"), o[:, 0:512]).then_inc(moved_a, 1)
                        if b > 4 * half:
                            o = read("ST", b - 1)
                            act.copy(STm[:, (b - 1) % 4, 0:NPG, :].rearrange("p g h -> p (g h)"), o[:, 0:NPG * NH]).then_inc(moved_a, 1)

                def sample_exp(n, S, scale):
                    wait_moved(act, "mb", n)
                    flat = S.rearrange("p b g h -> p (b g h)")
                    act.activation(flat, flat, ACT.Exp, scale=scale).then_inc(sexp_ready, 1)

                past_half(0)
                sample_exp(0, STm, SA)
                past_half(1)
                sample_exp(2, STw, SB)
                sample_exp(1, STm, SA)
                roots((8,), slice(0, 3))
                for k in range(1, KD, 2):
                    o = read("fT", k)
                    act.activation(hT[:, k, :], o[:, 0:T], ACT.Copy, scale=g_ffn[:, k:k + 1]).then_inc(moved_a, 1)
                for g in range(4):
                    o = read("skT", g)
                    act.copy(skT[:, 4 * g:4 * g + 4, :].rearrange("p n c -> p (n c)"), o[:, 0:512]).then_inc(moved_a, 1)
                for n in range(NSUB):
                    o = read("pq", n)
                    act.copy(pqT[:, n, :], o[:, 0:T]).then_inc(moved_a, 1)
                for t, (t0, m) in enumerate(TOK):
                    for g in range(4):
                        o = read("s", t, g)
                        act.copy(sc[0:m, t, 4 * g:4 * g + 4, :].rearrange("p n c -> p (n c)"), o[0:m, 0:512]).then_inc(moved_a, 1)
                for t, (t0, m) in enumerate(TOK):
                    act.wait_ge(cand_max, t + 1)
                    act.activation(sel[0:m, t, 2, :], sel[0:m, t, 2, :], ACT.Exp).then_inc(gexp, 1)
                    o = read("slot", t)
                    act.copy(slotT[:, :, t0:t0 + m], o[:, 0:384].rearrange("p (s c) -> p s c", s=3)[:, :, 0:m]).then_inc(moved_a, 1)
                for _ in range(2):
                    act.nop().then_inc(g_moved, 1)
                with act.Fori(0, T // GT) as it:
                    for g in range(2):
                        act.wait_ge(g_prod, it * 2 + (g + 3))
                        act.copy(G[:, bass.ds(it * GT + 4 * g, 4), :].rearrange("p t j -> p (t j)"), ps[:, 6 + g, :]).then_inc(g_moved, 1)
                act.nop().then_inc(uT_a, 1)
                act.nop().then_inc(gelu_done, 1)
                with act.Fori(0, LOOPS) as it:
                    for k in range(UN + 1):
                        if k < UN:
                            act.wait_ge(turned, it * (2 * UN) + (2 * k + 2))
                            act.copy(uT[k % 2][:, 512:1024], ps[:, 7, :]).then_inc(uT_a, 1)
                        if k >= 1:
                            act.wait_ge(z_prod, it * UN + k)
                            act.activation(act_t[(k - 1) % 2], ps[:, 5, 0:T], ACT.Gelu).then_inc(gelu_done, 1)
                act.wait_ge(gelu_done, NK + 1)
                layer_end(act, 1)
            act.wait_ge(f_sq, 3)
            act.activation(stat[:, 0:3], stat[:, 0:3], ACT.Sqrt).then_inc(f_std, 1)

        @block.vector
        def _(dve):
            steps, seen, last_tap = [0], [0], [0, 0]

            def step(ins):
                steps[0] += 1
                ins.then_inc(vstep, 1)
                return steps[0]

            def settle():
                dve.wait_ge(vstep, steps[0])

            def read(*name):
                who, n = READ[name]
                seen[0] += 1
                assert who == "V" and n == seen[0], name
                return arrive(dve, *name)

            def squares(dst, done):
                for t, (t0, m) in enumerate(TOK):
                    dve.tensor_tensor_reduce(dst[0:m, t, :], X[0:m, t, :], X[0:m, t, :], 1.0 / D, EPS, ALU.mult, ALU.add,
                                             stat[0:m, t:t + 1]).then_inc(done, 1)

            def rotate(x1, x2, cos, sin, ta, tb):
                step(dve.tensor_tensor(ta, x1, sin, ALU.mult))
                step(dve.tensor_tensor(tb, x2, sin, ALU.mult))
                settle()
                step(dve.tensor_tensor(x1, x1, cos, ALU.mult))
                step(dve.tensor_tensor(x2, x2, cos, ALU.mult))
                settle()
                step(dve.tensor_tensor(x1, x1, tb, ALU.subtract))
                return dve.tensor_tensor(x2, x2, ta, ALU.add)

            dve.wait_ge(consts_ld, 16 * 8)
            dve.wait_ge(ones_set, 1)
            with dve.Fori(0, DEPTH) as l:
                steps[0], seen[0] = 0, 0

                def norm(dst, k):
                    squares(dst, sq_ready)
                    dve.wait_ge(std_ready, k)
                    step(dve.reciprocal(stat[:, 0:3], stat[:, 0:3]))
                    settle()
                    for t, (t0, m) in enumerate(TOK):
                        dve.tensor_scalar(dst[0:m, t, :], X[0:m, t, :], stat[0:m, t:t + 1], None, ALU.mult).then_inc(hn_ready, 1)

                norm(hn, 1)
                dve.wait_ge(small_ld, 16 * 10)
                for k in range(0, KD, 2):
                    o = read("hT", k)
                    dve.tensor_scalar(hT[:, k, :], o[:, 0:T], g_mix[:, k:k + 1], None, ALU.mult).then_inc(moved_v, 1)
                wait_moved(dve, "z", 0, 2)
                dve.wait_ge(pad_set, 2)
                for i, (c0, n) in enumerate(((CQ, QL), (CKV, LAT))):
                    for t in range(3):
                        zz = z[:, t, c0:c0 + n]
                        step(dve.tensor_tensor_reduce(junk[:, 0:n], zz, zz, 1.0 / n, EPS, ALU.mult, ALU.add, stat[:, 3 + 3 * i + t:4 + 3 * i + t]))
                        settle()
                dve.nop().then_inc(sq_ready, 1)
                dve.wait_ge(std_ready, 2)
                step(dve.reciprocal(stat[:, 3:9], stat[:, 3:9]))
                settle()
                cq, ckv = z[:, :, CQ:CQ + QL], z[:, :, CKV:CKV + LAT]
                dve.tensor_tensor(cq, cq, stat[:, 3:6].unsqueeze(2).to_broadcast([P, 3, QL]), ALU.mult).then_inc(lat_ready, 1)
                step(dve.tensor_tensor(ckv, ckv, stat[:, 6:9].unsqueeze(2).to_broadcast([P, 3, LAT]), ALU.mult))
                settle()
                step(dve.tensor_tensor(ckv, ckv, kvg.unsqueeze(1).to_broadcast([P, 3, LAT]), ALU.mult))
                cosA, sinA, cosB, sinB = rope[:, :, 0:16], rope[:, :, 16:32], rope[:, :, 32:64], rope[:, :, 64:96]
                ra = ropet[:, 0:1152]
                rb = ropet[:, 1152:2304]

                def cut3(a, n):
                    return a[:, 0:3 * n].rearrange("p (t c) -> p t c", t=3)

                rotate(z[:, :, KR:KR + 16], z[:, :, KR + 16:KR + 32], cosA, sinA, cut3(ra, 16), cut3(rb, 16)).then_inc(lat_ready, 1)
                dve.wait_ge(lat_ready, 2)
                settle()
                dve.tensor_copy(krr, z[:, :, KR:KR + ROPE].unsqueeze(2).to_broadcast([P, 3, 4, ROPE])).then_inc(lat_ready, 1)
                wait_moved(dve, "z", 2, 2)
                for t in range(3):
                    x = z[:, t, QB:QB + 768].rearrange("p (h s c) -> p h s c", h=2 * NH, s=2)
                    tt = [r[:, 384 * t:384 * t + 384].rearrange("p (h c) -> p h c", h=2 * NH) for r in (ra, rb)]
                    last = rotate(x[:, :, 0, :], x[:, :, 1, :], cosB[:, t, :].unsqueeze(1).to_broadcast([P, 2 * NH, 32]),
                                  sinB[:, t, :].unsqueeze(1).to_broadcast([P, 2 * NH, 32]), tt[0], tt[1])
                    step(last)
                settle()
                dve.nop().then_inc(qk_ready, 1)
                wait_moved(dve, "z", 4, 2)
                dve.tensor_tensor(z[:, :, GA:GA + CC], z[:, :, GA:GA + CC], z[:, :, GB:GB + CC], ALU.mult).then_inc(g_ready, 1)
                wait_moved(dve, "q", 2, 1)
                for t, (t0, m) in enumerate(TOK):
                    x = q[0:m, t, NH * NOPE:].rearrange("p (h c) -> p h c", h=NH)
                    tt = [r[0:m, 96 * t:96 * t + 96].rearrange("p (h c) -> p h c", h=NH) for r in (ra, rb)]
                    step(rotate(x[:, :, 0:16], x[:, :, 16:32], cosA[0:m, t, :].unsqueeze(1).to_broadcast([m, NH, 16]),
                                sinA[0:m, t, :].unsqueeze(1).to_broadcast([m, NH, 16]), tt[0], tt[1]))
                settle()
                dve.tensor_copy(qrr[0:NB], q[0:NB, 2, NH * NOPE:].rearrange("p (h c) -> p h c", h=NH).unsqueeze(2).to_broadcast([NB, NH, 4, ROPE])).then_inc(q_ready, 1)
                for g in range(HP):
                    o = read("qbT", g)
                    dve.tensor_copy(qbT[:, g, :], o[:, 0:T]).then_inc(moved_v, 1)
                for g in range(HP):
                    o = read("kbT", g)
                    dve.tensor_copy(kbT[:, g, :], o[:, 0:T]).then_inc(moved_v, 1)
                for h in range(NH):
                    o = read("qlT", h)
                    dve.tensor_copy(qlT[:, h, :], o[:, 0:T]).then_inc(moved_v, 1)
                for c in range(2):
                    o = read("gT", c)
                    step(dve.tensor_copy(gT[:, c, CW - 1:CW - 1 + SEQ], o[:, 0:SEQ]))
                    dve.tensor_copy(gsT[:, c, :, CW - 1], o[:, SEQ:T]).then_inc(moved_v, 1)
                wait_moved(dve, "sc", 1)
                wait_moved(dve, "gT", 1)
                settle()

                def tap(n):
                    j, c = n // 2, n % 2
                    y, x, w = yT[:, c, 0:SEQ], gT[:, c, j:j + SEQ], cwT[:, c, j:j + 1]
                    if j == 0:
                        last_tap[c] = step(dve.tensor_scalar(y, x, w, g_cb[:, c:c + 1], ALU.mult, ALU.add))
                    else:
                        dve.wait_ge(vstep, last_tap[c])
                        last_tap[c] = step(dve.scalar_tensor_tensor(y, x, w, y, ALU.mult, ALU.add))

                taps = iter(range(2 * CW))
                for s in range(2 * NH + 2):
                    if s < 2 * NH:
                        o = read("S", s)
                        dve.tensor_tensor(prob[:, s % 2, :], o[:, 0:384], mbias if s < NH else cbias, ALU.add).then_inc(moved_v, 1)
                        wait_moved(dve, "S", s)
                        for i, c0 in ((0, 0), (1, 128)):
                            step(dve.tensor_reduce(nmx[:, s, i:i + 1], prob[:, s % 2, c0:c0 + 128 * (i + 1)], AX, ALU.max))
                        settle()
                        dve.tensor_scalar(nmx[:, s, :], nmx[:, s, :], -SA if s < NH else -SB, None, ALU.mult).then_inc(nmx_ready, 1)
                    u = s - 1
                    if NH <= u < 2 * NH:
                        dve.wait_ge(exp_ready, u + 1)
                        for i, c0 in ((0, 0), (1, 128)):
                            c1 = c0 + 128 * (i + 1)
                            e = dve.tensor_tensor_reduce(prob[:, u % 2, c0:c1], prob[:, u % 2, c0:c1], cnt[:, c0:c1], 1.0, 0.0,
                                                         ALU.mult, ALU.add, den[:, u, i:i + 1])
                            if i == 0:
                                step(e)
                        e.then_inc(cnt_ready, 1)
                    for n in range(5):
                        k = next(taps, None)
                        if k is not None:
                            tap(k)
                    u = s - 2
                    if u >= 0:
                        if u < NH:
                            dve.wait_ge(exp_ready, u + 1)
                        else:
                            dve.wait_ge(cnt_ready, u - NH + 1)
                        step(dve.reciprocal(rden[:, u, :], den[:, u, :]))
                        o = read("O", u)
                        settle()
                        dve.tensor_tensor(oAB[:, :, 64 * u:64 * u + 64], o[:, 0:128].rearrange("p (t c) -> p t c", t=2),
                                          rden[:, u, :].unsqueeze(2).to_broadcast([P, 2, 64]), ALU.mult).then_inc(moved_v, 1)
                for k in taps:
                    tap(k)
                for c in range(2):
                    t1 = junk[:, c * 248:(c + 1) * 248].rearrange("p (b j) -> p b j", b=NB)
                    step(dve.tensor_tensor(t1, gsT[:, c, :, :], cwT[:, c, :].unsqueeze(1).to_broadcast([P, NB, CW]), ALU.mult))
                    settle()
                    step(dve.tensor_reduce(yT[:, c, SEQ:T], t1, AX, ALU.add))
                    settle()
                    step(dve.tensor_scalar(yT[:, c, SEQ:T], yT[:, c, SEQ:T], g_cb[:, c:c + 1], None, ALU.add))
                settle()
                dve.nop().then_inc(y_ready, 1)
                for t, (t0, m) in enumerate(TOK):
                    wait_moved(dve, "yt", t)
                    step(dve.bn_stats(bnst[0:m, t, 0:6], yt[0:m, t, :]))
                    settle()
                    step(dve.bn_aggr(bnst[0:m, t, 6:8], bnst[0:m, t, 0:6]))
                    settle()
                    step(dve.tensor_scalar(stat[0:m, 9 + t:10 + t], bnst[0:m, t, 7:8], EPS, None, ALU.add))
                settle()
                dve.nop().then_inc(sq_ready, 1)
                dve.wait_ge(std_ready, 3)
                step(dve.reciprocal(stat[:, 9:12], stat[:, 9:12]))
                settle()
                for t, (t0, m) in enumerate(TOK):
                    dve.tensor_scalar(yt[0:m, t, :], yt[0:m, t, :], bnst[0:m, t, 6:7], stat[0:m, 9 + t:10 + t],
                                      ALU.subtract, ALU.mult).then_inc(ln_ready, 1)
                for c in range(2):
                    o = read("ycT", c)
                    dve.wait_ge(sig_ready, c + 1)
                    step(dve.tensor_scalar(ycs[:, 2, :], o[:, 0:T], g_lg[:, c:c + 1], g_lb[:, c:c + 1], ALU.mult, ALU.add))
                    settle()
                    dve.tensor_tensor(mixT[:, 6 + c, :], ycs[:, 2, :], ycs[:, c, :], ALU.mult).then_inc(moved_v, 1)
                    wait_moved(dve, "ycT", c)

                def past_half(half):
                    for b in range(4 * half, 4 * half + 4):
                        for g in range(1, 4, 2):
                            o = read("cT", b, g)
                            dve.tensor_copy(cT[:, b % 2, 512 * g:512 * g + 512], o[:, 0:512]).then_inc(moved_v, 1)

                def new_keys(half):
                    step(dve.tensor_tensor(STm[0:NB, :, NPG, :], extS[:, :, 4 * half:4 * half + 4].rearrange("p h b -> p b h"),
                                           diag[:, 4 * half:4 * half + 4].unsqueeze(2).to_broadcast([NB, 4, NH]), ALU.add))
                    settle()

                def chain(n, S, c, order, last_slot):
                    ng, nb = S.shape[2], S.shape[1]

                    def bc(a):
                        return a.rearrange("p (b h) -> p b h", b=nb).unsqueeze(2).to_broadcast([P, nb, ng, NH])

                    dve.tensor_reduce(smx[:, n, 0:c].rearrange("p (b h) -> p b h", b=nb), S.rearrange("p b g h -> p b h g"),
                                      AX, ALU.max).then_inc(smx_ready, 1)
                    o = read("mx", n)
                    dve.tensor_reduce(smc[0:c, n:n + 1], o[0:c, 0:128], AX, ALU.max).then_inc(moved_v, 1)
                    wait_moved(dve, "mx", n)
                    dve.tensor_scalar(sdg[0:c, n, 0:c], ident[0:c, 0:c], smc[0:c, n:n + 1], None, ALU.mult).then_inc(sdg_ready, 1)
                    o = read("mb", n)
                    for b in range(nb):
                        e = dve.tensor_tensor(S[:, b, :, :], S[:, b, :, :], o[:, NH * b:NH * b + NH].unsqueeze(1).to_broadcast([P, ng, NH]),
                                              ALU.subtract)
                        if b < nb - 1:
                            step(e)
                    settle()
                    e.then_inc(moved_v, 1)
                    dve.wait_ge(sexp_ready, order)
                    if last_slot:
                        step(dve.tensor_scalar(S[:, :, ng - 1, :], S[:, :, ng - 1, :], float(len(DIL)), None, ALU.mult))
                        settle()
                    dve.tensor_reduce(sden[:, n, 0:c].rearrange("p (b h) -> p b h", b=nb), S.rearrange("p b g h -> p b h g"),
                                      AX, ALU.add).then_inc(sden_ready, 1)
                    o = read("dn", n)
                    dve.reciprocal(srd[:, n, 0:c], o[:, 0:c]).then_inc(moved_v, 1)
                    wait_moved(dve, "dn", n)

                def latents_out(half):
                    o = read("ol", half)
                    dve.tensor_tensor(olT[:, 4 * half:4 * half + 4, :].rearrange("p b h -> p (b h)"), o[:, 0:24],
                                      srd[:, half, 0:24], ALU.mult).then_inc(moved_v, 1)

                past_half(0)
                step(dve.memset(STm[:, :, NPG, :], NEG))
                step(dve.memset(STw[:, :, 3, :], NEG))
                settle()
                o = read("ext")
                dve.tensor_copy(extS.rearrange("p h b -> p (h b)"), o[0:NB, 0:48]).then_inc(moved_v, 1)
                wait_moved(dve, "ext")
                new_keys(0)
                for b in range(NB):
                    o = read("qbc", b)
                    dve.wait_ge(kw_ld, 48 * (b + 1))
                    e = dve.tensor_tensor(kprod, kw, o[:, 0:384].unsqueeze(1).to_broadcast([P, 3, 384]), ALU.mult)
                    e.then_inc(moved_v, 1)
                    wait_moved(dve, "qbc", b)
                    dve.tensor_reduce(STw[:, b, 0:3, :], kprod.rearrange("p d (h c) -> p d h c", h=NH), AX, ALU.add).then_inc(kw_used, 1)
                    dve.wait_ge(kw_used, b + 1)
                step(dve.tensor_tensor(kprod[0:NB, 0, :], z[0:NB, 2, QB:QB + 384], z[0:NB, 2, KB:KB + 384], ALU.mult))
                settle()
                step(dve.tensor_reduce(kprod[0:NB, 1, 0:NH], kprod[0:NB, 0, :].rearrange("p (h c) -> p h c", h=NH), AX, ALU.add))
                settle()
                step(dve.tensor_tensor(STw[0:NB, :, 3, :], kprod[0:NB, 1, 0:NH].unsqueeze(1).to_broadcast([NB, NB, NH]),
                                       diag[:, :].unsqueeze(2).to_broadcast([NB, NB, NH]), ALU.add))
                for b in range(4):
                    wait_moved(dve, "ST", b)
                settle()
                chain(0, STm, 24, 1, False)
                latents_out(0)
                past_half(1)
                wait_moved(dve, "ST", 7)
                step(dve.memset(STm[:, :, NPG, :], NEG))
                settle()
                new_keys(1)
                chain(2, STw, 48, 2, True)
                chain(1, STm, 24, 3, False)
                latents_out(1)
                o = read("os")
                dve.tensor_copy(mixT[:, 0:3, SEQ:T], o[:, 0:24].rearrange("p (g b) -> p g b", g=3)).then_inc(moved_v, 1)
                o = read("ow")
                rd = srd[:, 2, :].rearrange("p (b g a) -> p b g a", b=NB, g=HP)
                for a in range(2):
                    e = dve.tensor_tensor(mixT[64 * a:64 * a + 64, 3:6, SEQ:T], o[64 * a:64 * a + 64, 0:24].rearrange("p (g b) -> p g b", g=3),
                                          rd[64 * a:64 * a + 64, :, :, a].rearrange("p b g -> p g b"), ALU.mult)
                    if a == 0:
                        step(e)
                settle()
                e.then_inc(moved_v, 1)

                def add_to_x(name):
                    for c in range(2):
                        for t, (t0, m) in enumerate(TOK):
                            o = read(name, c, t)
                            xs = X[0:m, t, 512 * c:512 * c + 512]
                            dve.tensor_tensor(xs, xs, o[0:m, 0:512], ALU.add).then_inc(moved_v, 1)
                    wait_moved(dve, name, 1, 2)

                add_to_x("xo")
                dve.wait_ge(stored, 1)
                norm(hf, 4)
                for k in range(0, KD, 2):
                    o = read("fT", k)
                    dve.tensor_scalar(hT[:, k, :], o[:, 0:T], g_ffn[:, k:k + 1], None, ALU.mult).then_inc(moved_v, 1)

                def top16(v, ix, src):
                    step(dve.max(v[:, 0:8], src))
                    settle()
                    step(dve.max_index(ix[:, 0:8], v[:, 0:8], src))
                    settle()
                    step(dve.match_replace(src, v[:, 0:8], src, -3.0e38))
                    settle()
                    step(dve.max(v[:, 8:16], src))
                    settle()
                    step(dve.max_index(ix[:, 8:16], v[:, 8:16], src))

                for t, (t0, m) in enumerate(TOK):
                    wait_moved(dve, "s", t, 3)
                    for n in range(NSUB):
                        top16(top[0:m, n, :], topi[0:m, n, :].bitcast(U32), sc[0:m, t, n, :])
                    settle()
                    step(dve.tensor_copy(topf[0:m, :, :], topi[0:m, :, :].bitcast(U32)))
                    tv = top[0:m, :, :].rearrange("p (h s) k -> p h s k", s=2)
                    tf = topf[0:m, :, :].rearrange("p (h s) k -> p h s k", s=2)
                    step(dve.tensor_tensor(cand[0:m, :, :].rearrange("p h (a b) -> p h a b", a=TOPK),
                                           tv[:, :, 0, :].unsqueeze(3).to_broadcast([m, PH, TOPK, TOPK]),
                                           tv[:, :, 1, :].unsqueeze(2).to_broadcast([m, PH, TOPK, TOPK]), ALU.add))
                    settle()
                    for h in range(PH):
                        top16(cs[0:m, h, :], ci[0:m, h, :].bitcast(U32), cand[0:m, h, :])
                    settle()
                    civ = ci[0:m, :, :].bitcast(U32)
                    step(dve.tensor_single_scalar(cab[0:m, 0].bitcast(U32), civ, 4, ALU.logical_shift_right))
                    step(dve.tensor_single_scalar(cab[0:m, 1].bitcast(U32), civ, 15, ALU.bitwise_and))
                    settle()
                    step(dve.tensor_copy(cabf[0:m], cab[0:m].bitcast(U32)))
                    settle()
                    for s in range(2):
                        io = iota[0:m, 0:TOPK].unsqueeze(1).to_broadcast([m, PH * TOPK, TOPK])
                        ch = cabf[0:m, s, :, :].rearrange("p h k -> p (h k)").unsqueeze(2).to_broadcast([m, PH * TOPK, TOPK])
                        step(dve.tensor_tensor(hot[0:m].rearrange("p h k a -> p (h k) a"), io, ch, ALU.is_equal))
                        settle()
                        step(dve.tensor_tensor(hot[0:m], hot[0:m], tf[:, :, s, :].unsqueeze(2).to_broadcast([m, PH, TOPK, TOPK]), ALU.mult))
                        settle()
                        step(dve.tensor_reduce(sel[0:m, t, s, :], hot[0:m].rearrange("p h k a -> p (h k) a"), AX, ALU.add))
                        settle()
                    gt = sel[0:m, t, 2, :].rearrange("p (h k) -> p h k", h=PH)
                    dve.tensor_tensor(gt, cs[0:m, :, :], cs[0:m, :, 0:1].to_broadcast([m, PH, TOPK]), ALU.subtract).then_inc(cand_max, 1)
                    dve.wait_ge(gexp, t + 1)
                    step(dve.tensor_reduce(hsum[0:m, 0, :], gt, AX, ALU.add))
                    settle()
                    step(dve.reciprocal(hsum[0:m, 1, :], hsum[0:m, 0, :]))
                    settle()
                    dve.tensor_tensor(gt, gt, hsum[0:m, 1, :].unsqueeze(2).to_broadcast([m, PH, TOPK]), ALU.mult).then_inc(sel_ready, 1)
                    dve.wait_ge(sel_ready, t + 1)
                dve.memset(zeros, 0.0).then_inc(acc_zero, 1)
                wait_moved(dve, "slot", 2)
                with dve.Fori(0, T // GT) as it:
                    for g in range(2):
                        dve.wait_ge(g_prod, it * 2 + (g + 1))
                        hb = hotB if g == 0 else hotB2
                        ta = slotT[:, 0, bass.ds(it * GT + 4 * g, 4)].unsqueeze(2).to_broadcast([P, 4, P])
                        dve.tensor_tensor(hotA[:, 4 * g:4 * g + 4, :], iota[:, :].unsqueeze(1).to_broadcast([P, 4, P]), ta,
                                          ALU.is_equal).then_inc(hotA_ready, 1)
                        for k in range(4):
                            tk = bass.ds(it * GT + (4 * g + k), 1)
                            e = dve.tensor_scalar(hb[:, k, :], iota[:, :], slotT[:, 1, tk], slotT[:, 2, tk], ALU.is_equal, ALU.mult)
                        e.then_inc(hotB_ready, 1)
                dve.nop().then_inc(uT_v, 1)
                with dve.Fori(0, LOOPS) as it:
                    for k in range(UN + 1):
                        if k < UN:
                            dve.wait_ge(turned, it * (2 * UN) + (2 * k + 1))
                            dve.tensor_copy(uT[k % 2][:, 0:512], ps[:, 6, :]).then_inc(uT_v, 1)
                        if k >= 1:
                            dve.wait_ge(gelu_done, it * UN + (k + 1))
                            j = it * UN + (k - 1)
                            dve.tensor_tensor(wgt_t[(k - 1) % 2], act_t[(k - 1) % 2], G[:, :, bass.ds(j, 1)].rearrange("p t o -> p (t o)"),
                                              ALU.mult).then_inc(w_ready, 1)
                dve.wait_ge(acc_done, 1)
                dve.wait_ge(w_ready, NK)
                for n in range(4):
                    step(dve.tensor_copy(yacc[:, 2 * n:2 * n + 2, 0:SEQ], ps[:, n, :].rearrange("p (c t) -> p c t", c=2)))
                step(dve.tensor_copy(yacc[:, :, SEQ:T], ps[:, 4, 0:64].rearrange("p (c t) -> p c t", c=KD)))
                settle()
                dve.nop().then_inc(y_moved, 1)
                add_to_x("xT")
                layer_end(dve, 2)
            squares(fin, f_sq)
            dve.wait_ge(f_std, 1)
            dve.reciprocal(stat[:, 0:3], stat[:, 0:3]).then_inc(f_step, 1)
            dve.wait_ge(f_step, 1)
            dve.wait_ge(f_gld, 16)
            for t, (t0, m) in enumerate(TOK):
                dve.scalar_tensor_tensor(fin[0:m, t, :], X[0:m, t, :], stat[0:m, t:t + 1], gfin[0:m, :], ALU.mult, ALU.mult).then_inc(f_y, 1)


def constants():
    f = np.float32
    pos = np.zeros((P, 3), f)
    pos[:, 0], pos[:, 1] = np.arange(P), P + np.arange(P)
    pos[:, 2] = PAST
    rope = np.zeros((P, 3, 96), f)
    for dim, a in ((ROPE, 0), (HD, 32)):
        half = dim // 2
        inv = np.power(f(10000.0), -np.arange(half, dtype=f) * f(2.0) / f(dim)).astype(f)
        ang = (pos[:, :, None] * inv).astype(f)
        rope[:, :, a:a + half] = np.cos(ang)
        rope[:, :, a + half:a + 2 * half] = np.sin(ang)
    qi = np.arange(P)[:, None]
    dist = np.concatenate([qi - np.arange(P), P + qi - np.arange(2 * P)], axis=1)
    cnt = sum(((dist >= 0) & (dist <= 128 * d) & (dist % d == 0)).astype(f) for d in DIL)
    masks = np.concatenate([cnt, np.where(cnt > 0, 0, NEG), np.where(dist >= 0, 0, NEG)], axis=1).astype(f)
    return {
        "ident": np.eye(P, dtype=f),
        "iota": np.tile(np.arange(P, dtype=f), (P, 1)),
        "rope": rope,
        "diag": np.where(np.eye(NB) > 0, 0, NEG).astype(f),
        "masks": masks,
    }


_OUTS = [(1, SEQ, D), (NB, 1, D), (DEPTH, 1, SEQ, LAT), (DEPTH, 1, SEQ, ROPE), (DEPTH, 1, SEQ, NH, HD), (DEPTH, 1, SEQ, NH, HD),
         (DEPTH, 1, CW - 1, CC), (DEPTH, NB, 1, LAT), (DEPTH, NB, 1, ROPE), (DEPTH, NB, PAST, NH, HD), (DEPTH, NB, PAST, NH, HD),
         (DEPTH, NB, CW - 1, CC)]


def kernel(**inputs):
    import concourse.bacc as _bacc
    from concourse.bass_utils import run_bass_kernel_spmd as _run

    nc = _bacc.Bacc("TRN2", target_bir_lowering=False, num_devices=1)
    arrays, A, C = {}, {}, {}
    for name, a in inputs.items():
        a = np.ascontiguousarray(a)
        arrays[f"in_{name}"] = a
        A[name] = nc.dram_tensor(f"in_{name}", a.shape, mybir.dt.from_np(a.dtype), kind="ExternalInput").ap()
    for name, a in constants().items():
        arrays[f"const_{name}"] = a
        C[name] = nc.dram_tensor(f"const_{name}", a.shape, F32, kind="ExternalInput").ap()
    outs = [nc.dram_tensor(f"out_{i}", s, F32, kind="ExternalOutput").ap() for i, s in enumerate(_OUTS)]
    program(nc, A, C, outs)
    r = _run(nc, [arrays], core_ids=[0])
    return tuple(r.results[0][f"out_{i}"] for i in range(len(_OUTS)))
```

```python
from contextlib import ExitStack

import numpy as np
import concourse.bass as bass
from concourse import mybir

F32 = mybir.dt.float32
I32 = mybir.dt.int32
U32 = mybir.dt.uint32
ALU = mybir.AluOpType
ACT = mybir.ActivationFunctionType
AX = mybir.AxisListType.X

P = 128
D = 1024
KD = D // P
SEQ, NB = 256, 8
T = SEQ + NB
TOK = [(0, 128), (128, 128), (256, 8)]
DEPTH = 2
PAST, PAGE = 2048, 128
NPG = PAST // PAGE
NH = 6
HP = NH // 2
NOPE, ROPE, LAT = 64, 32, 128
HD = 64
QL = 256
CW, CC = 31, 256
CQ, CKV, KR, QB, KB, VB, GA, GB = 0, 256, 384, 416, 800, 1184, 1568, 1824
ZC = 2080
ZCH = [(0, 416), (416, 384), (800, 384), (1184, 384), (1568, 512)]
UQ = NH * (NOPE + ROPE)
SA, SB = float((NOPE + ROPE) ** -0.5), float(HD ** -0.5)
PH, NK, TOPK = 8, 128, 16
NSUB = 2 * PH
EPS = 1e-6
NEG = -1e30
DIL = (1, 4, 16)
UN = 4
LOOPS = NK // UN
GT = 8


def job_plan():
    jobs = [(("hT", k), "VA"[k % 2]) for k in range(KD)]
    jobs += [(("z", c, t), "A") for c in range(5) for t in range(3)]
    jobs += [(("cqT", 0), "A"), (("cqT", 1), "A"), (("ckvT",), "A"), (("krT",), "A"), (("ukT",), "A")]
    jobs += [(("q", t, n), "A") for t in range(3) for n in range(2)]
    jobs += [(("qbT", g), "V") for g in range(HP)] + [(("kbT", g), "V") for g in range(HP)]
    jobs += [(("qnT", g), "A") for g in range(HP)] + [(("qrT", g), "A") for g in range(2)] + [(("qrS",), "A")]
    jobs += [(("qlT", h), "V") for h in range(NH)]
    jobs += [(("va", t), "A") for t in range(2)]
    jobs += [(("cw",), "A"), (("sc", 0), "A"), (("sc", 1), "A"), (("gT", 0), "V"), (("gT", 1), "V")]
    for s in range(2 * NH + 2):
        if s < 2 * NH:
            jobs.append((("S", s), "V"))
        if 1 <= s <= 2 * NH:
            jobs.append((("PT", s - 1), "A"))
        if s >= 2:
            jobs.append((("O", s - 2), "V"))
    jobs += [(("mT", g), "A") for g in range(2 * HP)]
    jobs += [(("yt", t), "A") for t in range(3)]
    jobs += [(("ycT", c), "V") for c in range(2)]

    def pages(half):
        out = []
        for b in range(4 * half, 4 * half + 5):
            if b < 4 * half + 4:
                out += [(("cT", b, g), "AV"[g % 2]) for g in range(4)] + [(("rT", b), "A")]
            if b > 4 * half:
                out.append((("ST", b - 1), "A"))
        return out

    jobs += pages(0) + [(("ext",), "V")] + [(("qbc", b), "V") for b in range(NB)]
    jobs += [(("mx", 0), "V"), (("mb", 0), "V"), (("dn", 0), "V"), (("ol", 0), "V")] + pages(1)
    for n in (2, 1):
        jobs += [(("mx", n), "V"), (("mb", n), "V"), (("dn", n), "V")]
    jobs += [(("ol", 1), "V"), (("os",), "V"), (("ow",), "V")]
    jobs += [(("xo", c, t), "V") for c in range(2) for t in range(3)]
    jobs += [(("fT", k), "VA"[k % 2]) for k in range(KD)]
    jobs += [(("skT", g), "A") for g in range(4)]
    jobs += [(("pq", n), "A") for n in range(NSUB)]
    jobs += [(("s", t, g), "A") for t in (2, 0, 1) for g in range(4)]
    jobs += [(("slot", 2), "A")]
    for b in range(NB + 1):
        if b < NB:
            jobs += [(("gu", b, 0), "A"), (("gu", b, 1), "A")]
        if b:
            jobs.append((("gz", b - 1), "A"))
    jobs += [(("slot", 0), "A"), (("gy", 0), "V"), (("gy", 1), "V"), (("slot", 1), "A")]
    jobs += [(("xT", c, t), "V") for c in range(2) for t in range(2)]
    return jobs


JOBS = job_plan()
NUM = {name: n for n, (name, _) in enumerate(JOBS)}
READ = {}
for _n, (_name, _who) in enumerate(JOBS):
    READ[_name] = (_who, sum(w == _who for _, w in JOBS[:_n + 1]))


def program(nc, A, C, outs):
    (y_p, y_s, lat_p, kr_p, wk_p, wv_p, cv_p, lat_s, kr_s, wk_s, wv_s, cv_s) = outs
    with ExitStack() as ctx:
        def sb(name, shape, dt=F32):
            return ctx.enter_context(nc.sbuf_tensor(name, shape, dt))

        layer_sems = []

        def sem(name):
            s = ctx.enter_context(nc.semaphore(name))
            layer_sems.append(s)
            return s

        X = sb("X", [P, 3, D])
        hT = sb("hT", [P, KD, T])
        ident = sb("ident", [P, P])
        iota = sb("iota", [P, P])
        ones = sb("ones", [P, P])
        rope = sb("rope", [P, 3, 96])
        gains = sb("gains", [P, 2 * KD + 2 + 2 * 3])
        stat = sb("stat", [P, 16])
        bnst = sb("bnst", [P, 3, 8])
        nmx = sb("nmx", [P, 2 * NH, 2])
        den = sb("den", [P, 2 * NH, 2])
        rden = sb("rden", [P, 2 * NH, 2])
        diag = sb("diag", [NB, NB])
        pages = sb("pages", [P, NB], I32)
        pidx = sb("pidx", [P, NB], I32)
        sub = sb("sub", [P, 1])
        eoff = sb("eoff", [P, 1])
        eidx = sb("eidx", [P, NB], I32)
        efl = sb("efl", [P, NB])
        coef = sb("coef", [P, NB, NB])
        gel = sb("gel", [P, NB])
        slotT = sb("slotT", [P, 3, T])
        hotA = sb("hotA", [P, GT, P])
        hotB = sb("hotB", [P, 4, P])
        g_mix, g_ffn, g_q = gains[:, 0:KD], gains[:, KD:2 * KD], gains[:, 2 * KD:2 * KD + 2]
        g_cb, g_lg, g_lb = (gains[:, 2 * KD + 2 + 2 * i:2 * KD + 4 + 2 * i] for i in range(3))

        stream = sb("stream", [P, 9 * 1024 + 4 * T])
        wslot = [stream[:, i * 4096:(i + 1) * 4096] for i in range(2)]
        u_t = [stream[:, i * 1024:(i + 1) * 1024] for i in range(4)]
        v_t = [stream[:, (4 + i) * 1024:(5 + i) * 1024] for i in range(4)]
        uT = [hotA[:, :, :].rearrange("p a b -> p (a b)"), stream[:, 8192:9216]]
        act_t = [stream[:, 9216 + i * T:9216 + (i + 1) * T] for i in range(2)]
        wgt_t = [stream[:, 9216 + (2 + i) * T:9216 + (3 + i) * T] for i in range(2)]
        gath = u_t + v_t
        zeros = stream[:, 9216:9216 + 512]

        BIG = SEQ * P
        big = sb("big", [P, BIG + 1664])
        G = big[:, 0:BIG].rearrange("p (t j) -> p t j", j=P)
        at = [0]

        def cut(n):
            a = at[0]
            at[0] += n
            assert at[0] <= BIG + 1664, at[0]
            return big[:, a:a + n]

        z = cut(3 * ZC).rearrange("p (t c) -> p t c", t=3)
        hn = z.rearrange("p t c -> p (t c)")[:, 0:3 * D].rearrange("p (t c) -> p t c", t=3)
        wuk, wuv = cut(NH * NOPE), cut(NH * HD)
        ukT = cut(HP * 128).rearrange("p (g c) -> p g c", g=HP)
        qnT = cut(HP * T).rearrange("p (g t) -> p g t", g=HP)
        qrT = cut(2 * T).rearrange("p (g t) -> p g t", g=2)
        qkT = cut(2 * HP * T)
        qbT = qkT[:, 0:HP * T].rearrange("p (g t) -> p g t", g=HP)
        kbT = qkT[:, HP * T:2 * HP * T].rearrange("p (g t) -> p g t", g=HP)
        krT = cut(T)
        ckvT = cut(T)
        cqT = cut(2 * T).rearrange("p (g t) -> p g t", g=2)
        qlT = cut(NH * T).rearrange("p (h t) -> p h t", h=NH)
        qrS = cut(NH * NB).rearrange("p (h b) -> p h b", h=NH)
        qrB = cut(NB * 4 * NH).rearrange("p (b i h) -> p b i h", b=NB, i=4)
        mixT = cut(KD * T).rearrange("p (k t) -> p k t", k=KD)
        kvg = cut(LAT)
        past = cut(4 * NPG * LAT).rearrange("p (b g c) -> p b g c", b=4, g=NPG)
        kw = cut(3 * 384).rearrange("p (d c) -> p d c", d=3)
        vw = cut(2 * 3 * 384).rearrange("p (s d c) -> p s d c", s=2, d=3)
        base = at[0]
        cnt = hotB[:, :, :].rearrange("p a b -> p (a b)")[:, 0:384]
        cbias = cut(384)
        mbias = cut(384)
        prob = slotT[:, :, :].rearrange("p s t -> p (s t)")[:, 0:768].rearrange("p (s c) -> p s c", s=2)
        probT = hotA[:, :, :].rearrange("p a b -> p (a b)")[:, 0:768].rearrange("p (s c) -> p s c", s=2)
        wuq = cut(2 * UQ).rearrange("p (k c) -> p k c", k=2)
        q = cut(3 * UQ).rearrange("p (t c) -> p t c", t=3)
        va = cut(2 * 384).rearrange("p (t c) -> p t c", t=2)
        oAB = cut(2 * 768).rearrange("p (t c) -> p t c", t=2)
        gT = cut(2 * 286).rearrange("p (c t) -> p c t", c=2)
        gsT = cut(2 * NB * CW).rearrange("p (c b j) -> p c b j", c=2, b=NB)
        cwT = cut(2 * CW).rearrange("p (c j) -> p c j", c=2)
        yT = qnT.rearrange("p g t -> p (g t)")[:, 0:2 * T].rearrange("p (c t) -> p c t", c=2)
        krr = kw.rearrange("p d c -> p (d c)")[:, 0:384].rearrange("p (t r c) -> p t r c", t=3, r=4)
        qrr = kw.rearrange("p d c -> p (d c)")[:, 384:384 + 768].rearrange("p (h r c) -> p h r c", h=NH, r=4)
        cwr = oAB[0:CW, 0, 0:256]
        scr = probT.rearrange("p s c -> p (s c)")[0:120, 0:512].rearrange("p (s c) -> p s c", s=2)
        ropet = vw.rearrange("p s d c -> p (s d c)")
        junk = oAB.rearrange("p t c -> p (t c)")[:, 512:512 + 768]
        yt = q.rearrange("p t c -> p (t c)")[:, 0:768].rearrange("p (t c) -> p t c", t=3)
        ycs = q.rearrange("p t c -> p (t c)")[:, 768:768 + 3 * T].rearrange("p (s t) -> p s t", s=3)
        at[0] = base
        cT = cut(2 * NPG * 128).rearrange("p (s k) -> p s k", s=2)
        rT = cut(2 * 512).rearrange("p (s g k) -> p s g k", s=2, g=4)
        STm = cut(4 * 17 * NH).rearrange("p (b g h) -> p b g h", b=4, g=17)
        STw = cut(NB * 4 * NH).rearrange("p (b g h) -> p b g h", b=NB, g=4)
        smc = cut(4)
        smx = cut(3 * 48).rearrange("p (n c) -> p n c", n=3)
        sden = cut(3 * 48).rearrange("p (n c) -> p n c", n=3)
        srd = cut(3 * 48).rearrange("p (n c) -> p n c", n=3)
        sdg = cut(3 * 48).rearrange("p (n c) -> p n c", n=3)
        extS = cut(48).rearrange("p (h b) -> p h b", h=NH)[0:NB]
        olT = cut(48).rearrange("p (b h) -> p b h", b=NB)
        kprod = qkT[:, 0:3 * 384].rearrange("p (d c) -> p d c", d=3)
        pastr = stream[:, 8192:8192 + 4 * NPG * ROPE].rearrange("p (b g c) -> p b g c", b=4, g=NPG)
        at[0] = 0
        hf = cut(3 * D).rearrange("p (t c) -> p t c", t=3)
        sk = cut(NSUB * 128).rearrange("p (n c) -> p n c", n=NSUB)
        skT = cut(NSUB * 128).rearrange("p (n c) -> p n c", n=NSUB)
        pqT = cut(NSUB * T).rearrange("p (n t) -> p n t", n=NSUB)
        sc = cut(3 * NSUB * NK).rearrange("p (t n c) -> p t n c", t=3, n=NSUB)
        top = cut(NSUB * TOPK).rearrange("p (n c) -> p n c", n=NSUB)
        topi = cut(NSUB * TOPK).rearrange("p (n c) -> p n c", n=NSUB)
        topf = cut(NSUB * TOPK).rearrange("p (n c) -> p n c", n=NSUB)
        cand = cut(PH * 256).rearrange("p (h c) -> p h c", h=PH)
        cs = cut(PH * TOPK).rearrange("p (h c) -> p h c", h=PH)
        ci = cut(PH * TOPK).rearrange("p (h c) -> p h c", h=PH)
        cab = cut(2 * PH * TOPK).rearrange("p (s h c) -> p s h c", s=2, h=PH)
        cabf = cut(2 * PH * TOPK).rearrange("p (s h c) -> p s h c", s=2, h=PH)
        hot = cut(PH * TOPK * TOPK).rearrange("p (h k a) -> p h k a", h=PH, k=TOPK)
        sel = cut(3 * 3 * 128).rearrange("p (t s c) -> p t s c", t=3, s=3)
        hsum = cut(2 * PH).rearrange("p (s h) -> p s h", s=2)
        hotB2 = big[:, BIG:BIG + 512].rearrange("p (a b) -> p a b", a=4)
        yacc = big[:, 0:KD * SEQ].rearrange("p (k t) -> p k t", k=KD)
        scp = hotB2.rearrange("p a b -> p (a b)")[:, 0:NK]
        tpk = hotB2.rearrange("p a b -> p (a b)")[:, 128:160].rearrange("p (s k) -> p s k", s=2)
        tpi = hotB2.rearrange("p a b -> p (a b)")[:, 160:176]
        tq = hotB2.rearrange("p a b -> p (a b)")[0:64, 176:208].rearrange("p (s k) -> p s k", s=2)
        pcs = hotB2.rearrange("p a b -> p (a b)")[0:64, 208:224]
        pci = hotB2.rearrange("p a b -> p (a b)")[0:64, 224:240]
        pab = hotB2.rearrange("p a b -> p (a b)")[0:64, 240:272].rearrange("p (s k) -> p s k", s=2)
        pabf = hotB2.rearrange("p a b -> p (a b)")[0:64, 272:304].rearrange("p (s k) -> p s k", s=2)
        psel = hotB2.rearrange("p a b -> p (a b)")[0:64, 304:352].rearrange("p (s k) -> p s k", s=3)
        psum2 = hotB2.rearrange("p a b -> p (a b)")[0:64, 352:354]
        pcand = cut(256)[0:64].rearrange("p (a b) -> p a b", a=TOPK)
        phot = cut(256)[0:64].rearrange("p (a b) -> p a b", a=TOPK)
        fin = stream[:, 0:3 * D].rearrange("p (t c) -> p t c", t=3)
        gfin = stream[:, 4096:4096 + D]

        ps = ctx.enter_context(nc.psum_tensor("ps", [P, 8, 512], F32))

        product = sem("product")
        moved_v = sem("moved_by_vector")
        moved_a = sem("moved_by_scalar")
        small_ld = sem("small_loads")
        w_ld = [sem("weights_even"), sem("weights_odd")]
        uq_ld = sem("wuq_loaded")
        conv_ld = sem("conv_loaded")
        kw_ld = sem("window_keys_loaded")
        kw_used = sem("window_keys_used")
        vw_ld = [sem("window_values_even"), sem("window_values_odd")]
        vw_used = sem("window_values_used")
        sk_ld = sem("subkeys_loaded")
        vstep = sem("vector_step")
        pad_set = sem("pads_set")
        sq_ready = sem("squares_ready")
        std_ready = sem("std_ready")
        hn_ready = sem("normed_ready")
        lat_ready = sem("latents_ready")
        qk_ready = sem("window_qk_ready")
        q_ready = sem("q_rotated")
        sig_ready = sem("sigmoid_ready")
        g_ready = sem("glu_ready")
        nmx_ready = sem("negmax_ready")
        exp_ready = sem("exp_ready")
        cnt_ready = sem("counted_ready")
        y_ready = sem("conv_ready")
        ln_ready = sem("conv_normed")
        smx_ready = sem("sample_max_ready")
        sdg_ready = sem("sample_diag_ready")
        sexp_ready = sem("sample_exp_ready")
        sden_ready = sem("sample_den_ready")
        stored = sem("stores_done")
        cand_max = sem("gate_logits_ready")
        gexp = sem("gate_exp_ready")
        sel_ready = sem("selection_ready")
        scp_ld = sem("sample_scores_spread")
        p1_ready = sem("sample_tops_ready")
        tq_ld = sem("sample_tops_paired")
        p2_ready = sem("sample_gates_ready")
        psel_ld = sem("sample_selection_gathered")
        e_ready = sem("expert_rows_ready")
        coef_ready = sem("sample_weights_ready")
        hotA_ready = sem("onehot_a_ready")
        hotB_ready = sem("onehot_b_ready")
        g_prod = sem("gate_product")
        g_moved = sem("gate_moved")
        g_done = sem("gates_done")
        acc_zero = sem("acc_zero")
        u_ld = [sem(f"u_loaded{i}") for i in range(UN)]
        v_ld = [sem(f"v_loaded{i}") for i in range(UN)]
        u_free = [sem(f"u_free{i}") for i in range(UN)]
        v_free = [sem(f"v_free{i}") for i in range(UN)]
        turned = sem("u_turned")
        acc_done = sem("acc_done")
        uT_v = sem("uT_by_vector")
        uT_a = sem("uT_by_scalar")
        z_prod = sem("expert_inputs")
        gelu_done = sem("gelu_done")
        w_ready = sem("expert_weights")
        y_moved = sem("peer_out_moved")
        copied = sem("window_copied")
        ended = sem("engines_at_layer_end")
        f_gld = ctx.enter_context(nc.semaphore("final_gain_loaded"))
        store = ctx.enter_context(nc.semaphore("store"))
        past_ld = ctx.enter_context(nc.semaphore("past_loaded"))
        erow_u_ld = [ctx.enter_context(nc.semaphore(f"u_rows_gathered{b}")) for b in range(NB)]
        erow_v_ld = ctx.enter_context(nc.semaphore("v_rows_gathered"))
        rows_ready = ctx.enter_context(nc.semaphore("past_rows_ready"))
        past_asked = ctx.enter_context(nc.semaphore("past_asked"))
        consts_ld = ctx.enter_context(nc.semaphore("consts_loaded"))
        ones_set = ctx.enter_context(nc.semaphore("ones_set"))
        go = [ctx.enter_context(nc.semaphore(f"next_layer_{e}")) for e in ("pe", "act", "dve", "pool")]
        f_sq, f_std, f_out, f_step, f_y = (ctx.enter_context(nc.semaphore(n)) for n in
                                     ("final_squares", "final_std", "final_stored", "final_step", "final_y"))
        moved = {"V": moved_v, "A": moved_a}
        def wait_moved(eng, *name):
            who, n = READ[name]
            eng.wait_ge(moved[who], n)

        def bank(*name):
            return ps[:, NUM[name] % 8]

        def arrive(eng, *name):
            eng.wait_ge(product, NUM[name] + 1)
            return bank(*name)

        def layer_end(eng, i):
            eng.nop().then_inc(ended, 1)
            eng.wait_ge(go[i], 1)
            eng.sem_clear(go[i])

        def L(name, l):
            a = A[name][bass.ds(l, 1)]
            names = " ".join("abcdef"[:len(a.shape) - 1])
            return a.rearrange(f"o {names} -> (o {names.split(' ')[0]}) {' '.join(names.split(' ')[1:])}")

        def O(ap, l):
            a = ap[bass.ds(l, 1)]
            names = "abcdef"[:len(a.shape) - 1]
            return a.rearrange(f"o {' '.join(names)} -> (o {names[0]}) {' '.join(names[1:])}")

        WCH = ([("w_in", c0, n) for c0, n in ZCH] + [("w_out", 512 * c, 512) for c in range(2)]
               + [("peer_wq", 512 * c, 512) for c in range(4)])

        W_LAST = [NUM["z", c, 2] + 1 for c in range(5)] + [NUM["xo", c, 2] + 1 for c in range(2)]
        W_LAST += [NUM["pq", 4 * c + 3] + 1 for c in range(4)]

        def wview(n):
            k = WCH[n][2]
            return wslot[n % 2][:, 0:KD * k].rearrange("p (k c) -> p k c", k=KD)

        block = ctx.enter_context(nc.Block())

        @block.sync
        def _(sp):
            sp.dma_start(ident[:, :], C["ident"]).then_inc(consts_ld, 16)
            sp.dma_start(iota[:, :], C["iota"]).then_inc(consts_ld, 16)
            sp.dma_start(rope[:, :, :], C["rope"]).then_inc(consts_ld, 16)
            sp.dma_start(diag[:, :], C["diag"]).then_inc(consts_ld, 16)
            sp.dma_start(sub[:, :], C["sub"]).then_inc(consts_ld, 16)
            with nc.allow_non_contiguous_dma(reason="page numbers to the partitions that load them, 4 KB once"):
                for g in range(P // 8):
                    sp.dma_start(pages[8 * g:8 * g + 8, :],
                                 A["page_table"].rearrange("b g -> g b")[g:g + 1, :].to_broadcast([8, NB])).then_inc(consts_ld, 16)
            for t, (t0, n) in enumerate(TOK[:2]):
                sp.dma_start(X[:, t, :], A["x_prompt"][0, t0:t0 + n, :]).then_inc(consts_ld, 16)
            sp.dma_start(X[0:NB, 2, :], A["x_sample"].rearrange("b s d -> (b s) d")).then_inc(consts_ld, 16)
            sp.wait_ge(consts_ld, 16 * 24)

            with sp.Fori(0, DEPTH) as l:
                def load_w(n):
                    if n >= 2:
                        sp.wait_ge(product, W_LAST[n - 2])
                    name, c0, k = WCH[n]
                    src = L(name, l).rearrange("(k p) c -> p k c", p=P)[:, :, c0:c0 + k]
                    sp.dma_start(wview(n), src).then_inc(w_ld[n % 2], 16)

                def window_rows(name, b, d):
                    lo = PAST - 128 * d
                    rows = L(name, l)[b, lo:PAST, :, :]
                    return rows.rearrange("(k r) h c -> k r (h c)", r=d)[:, 0, :]

                load_w(0)
                load_w(1)
                with nc.allow_non_contiguous_dma(reason="per-channel gains, a few KB"):
                    sp.dma_start(g_mix, L("norm_mix", l).rearrange("(k p) -> p k", p=P)).then_inc(small_ld, 16)
                    sp.dma_start(g_ffn, L("norm_ffn", l).rearrange("(k p) -> p k", p=P)).then_inc(small_ld, 16)
                    sp.dma_start(g_q, L("q_norm", l).rearrange("(k p) -> p k", p=P)).then_inc(small_ld, 16)
                    sp.dma_start(g_cb, L("conv_b", l).rearrange("(k p) -> p k", p=P)).then_inc(small_ld, 16)
                    sp.dma_start(g_lg, L("conv_ln_g", l).rearrange("(k p) -> p k", p=P)).then_inc(small_ld, 16)
                    sp.dma_start(g_lb, L("conv_ln_b", l).rearrange("(k p) -> p k", p=P)).then_inc(small_ld, 16)
                sp.dma_start(kvg, A["kv_norm"][bass.ds(l, 1)].to_broadcast([P, LAT])).then_inc(small_ld, 16)
                for i, m in enumerate((cnt, cbias, mbias)):
                    sp.dma_start(m, C["masks"][:, i * 384:(i + 1) * 384]).then_inc(small_ld, 16)
                sp.dma_start(wuq, L("w_uq", l).rearrange("(k p) c -> p k c", p=P)).then_inc(uq_ld, 16)
                wukv_src = L("w_ukv", l).rearrange("c (h a x) -> c a h x", h=NH, a=2)
                sp.dma_start(wuk.rearrange("p (h x) -> p h x", h=NH), wukv_src[:, 0]).then_inc(uq_ld, 16)
                sp.dma_start(wuv.rearrange("p (h x) -> p h x", h=NH), wukv_src[:, 1]).then_inc(uq_ld, 16)
                sp.dma_start(cwr, L("conv_w", l)).then_inc(conv_ld, 16)
                sp.dma_start(scr, L("state_conv", l).rearrange("(s b) j c -> (b j) s c", s=2)).then_inc(conv_ld, 16)
                for n in range(2, 7):
                    load_w(n)

                def load_kw(b):
                    if b >= 1:
                        sp.wait_ge(kw_used, b)
                    for i, d in enumerate(DIL):
                        sp.dma_start(kw[:, i, :], window_rows("state_win_k", b, d)).then_inc(kw_ld, 16)

                def load_vw(b):
                    if b >= 2:
                        sp.wait_ge(vw_used, b - 1)
                    for i, d in enumerate(DIL):
                        sp.dma_start(vw[:, b % 2, i, :], window_rows("state_win_v", b, d)).then_inc(vw_ld[b % 2], 16)

                wait_moved(sp, "qrS")
                load_kw(0)
                sp.wait_ge(q_ready, 1)
                load_vw(0)
                load_vw(1)
                for b in range(1, NB):
                    load_kw(b)
                for b in range(2, NB):
                    load_vw(b)
                sp.wait_ge(stored, 1)
                sp.wait_ge(product, W_LAST[6])
                for n in range(NSUB):
                    sp.dma_start(sk[:, n, :], L("peer_subkeys", l)[n // 2, n % 2]).then_inc(sk_ld, 16)
                for n in range(7, 11):
                    load_w(n)
                wait_moved(sp, "s", 2, 3)
                for side in range(2):
                    src_ = sc[0:NB, 2, :, :].rearrange("b (h s) c -> b h s c", s=2)[:, :, side, :]
                    for h in range(PH):
                        sp.dma_start(scp[64 * side + NB * h:64 * side + NB * h + NB, :], src_[:, h, :]).then_inc(scp_ld, 16)
                sp.wait_ge(p1_ready, 1)
                sp.dma_start(tq, tpk[64:128, :, :]).then_inc(tq_ld, 16)
                sp.wait_ge(p2_ready, 1)
                for h in range(PH):
                    sp.dma_start(sel[0:NB, 2, :, TOPK * h:TOPK * h + TOPK], psel[NB * h:NB * h + NB, :, :]).then_inc(psel_ld, 16)
                sp.wait_ge(product, NUM["gy", 1] + 1)
                u_l = L("peer_u", l).rearrange("(i j) d -> i j d", j=NK)
                v_l = L("peer_v", l).rearrange("(i j) d -> i j d", j=NK)
                for k in range(UN):
                    sp.nop().then_inc(u_free[k], 1)
                    sp.nop().then_inc(v_free[k], 1)
                with sp.Fori(0, NB) as b:
                    for half, (src, dst) in enumerate((("state_win_k", wk_s), ("state_win_v", wv_s))):
                        s_ap = L(src, l)[bass.ds(b, 1), 1:PAST].rearrange("o r h c -> (o r) (h c)")
                        d_ap = O(dst, l)[bass.ds(b, 1), 0:PAST - 1].rearrange("o r h c -> (o r) (h c)")
                        for m in range(2):
                            for k in range(UN):
                                j = b * (4 * UN) + (half * 2 * UN + m * UN + k)
                                sp.wait_ge(u_free[k], 1)
                                sp.sem_clear(u_free[k])
                                sp.dma_start(u_t[k], u_l[:, bass.ds(j, 1), :].rearrange("i o d -> i (o d)")).then_inc(u_ld[k], 16)
                                sp.wait_ge(v_free[k], 1)
                                sp.sem_clear(v_free[k])
                                sp.dma_start(v_t[k], v_l[:, bass.ds(j, 1), :].rearrange("i o d -> i (o d)")).then_inc(v_ld[k], 16)
                            if m == 0:
                                sp.dma_start(d_ap, s_ap).then_inc(copied, 16)
                sp.wait_ge(copied, 16 * 2 * NB)
                sp.wait_ge(ended, 4)
                for s in layer_sems:
                    sp.sem_clear(s)
                for s in go:
                    sp.nop().then_inc(s, 1)
            sp.dma_start(gfin, A["norm_final"].rearrange("(o d) -> o d", o=1).to_broadcast([P, D])).then_inc(f_gld, 16)
            for t, (t0, n) in enumerate(TOK):
                sp.wait_ge(f_y, t + 1)
                dst = y_p[0, t0:t0 + n, :] if t < 2 else y_s.rearrange("b s d -> (b s) d")
                sp.dma_start(dst, fin[0:n, t, :]).then_inc(f_out, 16)
            sp.wait_ge(f_out, 16 * 3)

        @block.gpsimd
        def _(pool):
            pool.memset(ones[:, :], 1.0)
            pool.memset(stat[:, :], 1.0).then_inc(ones_set, 1)
            with pool.Fori(0, DEPTH) as l:
                pool.wait_ge(rows_ready, l + 1)
                pool.nop().then_inc(past_asked, 1)
                pool.memset(z[:, 2, :], 0.0).then_inc(pad_set, 1)
                pool.memset(gT[:, :, 0:CW - 1], 0.0)
                pool.memset(qrB.rearrange("p b i h -> p (b i h)"), 0.0).then_inc(pad_set, 1)
                n_st = [0]

                def load_past(half):
                    for b in range(4):
                        row = bass.IndirectOffsetOnAxis(ap=pidx[:, 4 * half + b:4 * half + b + 1].bitcast(U32), axis=0)
                        for dst, name in ((past, "cache_kv_latent"), (pastr, "cache_k_rope")):
                            pool.indirect_dma_start(dst[:, b, :, :].rearrange("p g c -> p (g c)"), None,
                                                    A[name].rearrange("l n (s t) c -> (l n s) (t c)", s=8), row).then_inc(past_ld, 16)

                load_past(0)

                def put(dst, src):
                    pool.dma_start(dst, src).then_inc(store, 16)
                    n_st[0] += 16

                def put_tokens(prompt, sample, col, n, rows=2):
                    for t in range(2):
                        put(O(prompt, l)[0, 128 * t:128 * t + 128], z[:, t, col:col + n])
                    put(sample, z[0:NB, 2, col:col + n])

                pool.wait_ge(lat_ready, 2)
                for t in range(2):
                    put(O(lat_p, l)[0, 128 * t:128 * t + 128, :], z[:, t, CKV:CKV + LAT])
                    put(O(kr_p, l)[0, 128 * t:128 * t + 128, :], z[:, t, KR:KR + ROPE])
                put(O(lat_s, l)[:, 0, :], z[0:NB, 2, CKV:CKV + LAT])
                put(O(kr_s, l)[:, 0, :], z[0:NB, 2, KR:KR + ROPE])
                pool.wait_ge(qk_ready, 1)
                for t in range(2):
                    put(O(wk_p, l)[0, 128 * t:128 * t + 128].rearrange("r h c -> r (h c)"), z[:, t, KB:KB + 384])
                put(O(wk_s, l)[:, PAST - 1].rearrange("b h c -> b (h c)"), z[0:NB, 2, KB:KB + 384])
                wait_moved(pool, "z", 3, 2)
                for t in range(2):
                    put(O(wv_p, l)[0, 128 * t:128 * t + 128].rearrange("r h c -> r (h c)"), z[:, t, VB:VB + 384])
                put(O(wv_s, l)[:, PAST - 1].rearrange("b h c -> b (h c)"), z[0:NB, 2, VB:VB + 384])
                pool.wait_ge(g_ready, 1)
                put(O(cv_p, l)[0], z[128 - (CW - 1):128, 1, GA:GA + CC])
                put(O(cv_s, l)[:, CW - 2, :], z[0:NB, 2, GA:GA + CC])
                put(O(cv_s, l)[:, 0:CW - 2, :], L("state_conv", l)[:, 1:CW - 1, :])
                pool.wait_ge(store, l * n_st[0] + n_st[0])
                pool.nop().then_inc(stored, 1)
                pool.wait_ge(product, NUM["ol", 0] + 1)
                load_past(1)
                pool.wait_ge(e_ready, 1)
                for name in ("peer_u", "peer_v"):
                    for b in range(NB):
                        if name == "peer_v":
                            pool.wait_ge(product, NUM["gu", b, 1] + 1)
                        row = bass.IndirectOffsetOnAxis(ap=eidx[:, b:b + 1].bitcast(U32), axis=0)
                        pool.indirect_dma_start(gath[b], None, A[name].rearrange("l e d -> (l e) d"), row).then_inc(erow_u_ld[b] if name == "peer_u" else erow_v_ld, 16)
                layer_end(pool, 3)

        @block.tensor
        def _(pe):
            def begin(*name):
                n = NUM[name]
                if n >= 8:
                    wait_moved(pe, *JOBS[n - 8][0])
                return ps[:, n % 8]

            def turn(*name, parts):
                o = begin(*name)
                for src, rows, cols, c0 in parts:
                    mm = pe.transpose(o[0:cols, c0:c0 + rows], src, ident[0:rows, 0:rows])
                mm.then_inc(product, 1)

            def dense(name, parts, n_out, cols):
                o = begin(*name)
                for i, (lhs, rhs) in enumerate(parts):
                    mm = pe.matmul(o[0:n_out, 0:cols], lhs, rhs, start=(i == 0), stop=(i == len(parts) - 1))
                mm.then_inc(product, 1)

            def tokens(src, c0, n=128):
                return [(src[0:m, t, c0:c0 + n], m, n, t0) for t, (t0, m) in enumerate(TOK)]

            pe.wait_ge(consts_ld, 16 * 24)
            pe.wait_ge(ones_set, 1)
            with pe.Fori(0, DEPTH) as l:
                pe.wait_ge(hn_ready, 3)
                for k in range(KD):
                    turn("hT", k, parts=tokens(hn, k * 128))
                wait_moved(pe, "hT", KD - 2)
                wait_moved(pe, "hT", KD - 1)
                for c, (c0, n) in enumerate(ZCH):
                    pe.wait_ge(w_ld[c % 2], 16 * (c // 2 + 1))
                    for t, (t0, m) in enumerate(TOK):
                        dense(("z", c, t), [(hT[:, k, t0:t0 + m], wview(c)[:, k, :]) for k in range(KD)], m, n)
                pe.wait_ge(lat_ready, 1)
                for k in range(2):
                    turn("cqT", k, parts=tokens(z, CQ + 128 * k))
                pe.wait_ge(lat_ready, 3)
                turn("ckvT", parts=tokens(z, CKV))
                turn("krT", parts=[(krr[0:m, t, :, :].rearrange("p r c -> p (r c)"), m, 128, t0) for t, (t0, m) in enumerate(TOK)])
                pe.wait_ge(uq_ld, 48)
                turn("ukT", parts=[(wuk[:, 128 * g:128 * g + 128], 128, 128, g * 128) for g in range(HP)])
                wait_moved(pe, "cqT", 1)
                for t, (t0, m) in enumerate(TOK):
                    for n in range(2):
                        dense(("q", t, n), [(cqT[:, k, t0:t0 + m], wuq[:, k, n * 288:(n + 1) * 288]) for k in range(2)], m, 288)
                pe.wait_ge(qk_ready, 1)
                for g in range(HP):
                    turn("qbT", g, parts=tokens(z, QB + 128 * g))
                for g in range(HP):
                    turn("kbT", g, parts=tokens(z, KB + 128 * g))
                pe.wait_ge(q_ready, 1)
                for g in range(HP):
                    turn("qnT", g, parts=tokens(q, 128 * g))
                for g, hs in enumerate((4, 2)):
                    turn("qrT", g, parts=tokens(q, NH * NOPE + 128 * g, 32 * hs))
                turn("qrS", parts=[(qrr[0:NB, h, :, :].rearrange("p r c -> p (r c)"), NB, 128, h * NB)
                                   for h in range(NH)])
                wait_moved(pe, "qnT", HP - 1)
                for h in range(NH):
                    r0 = 64 * (h % 2)
                    dense(("qlT", h), [(ukT[r0:r0 + 64, h // 2, :], qnT[r0:r0 + 64, h // 2, :])], 128, T)
                for t in range(2):
                    dense(("va", t), [(ckvT[:, 128 * t:128 * t + 128], wuv)], 128, 384)
                pe.wait_ge(conv_ld, 32)
                turn("cw", parts=[(cwr[:, 128 * c:128 * c + 128], CW, 128, CW * c) for c in range(2)])
                for c in range(2):
                    turn("sc", c, parts=[(scr[:, s, 128 * c:128 * c + 128], 120, 128, 120 * s) for s in range(2)])
                pe.wait_ge(g_ready, 1)
                for c in range(2):
                    turn("gT", c, parts=tokens(z, GA + 128 * c))
                wait_moved(pe, "qlT", NH - 1)
                wait_moved(pe, "va", 1)

                def scores(u):
                    o = begin("S", u)
                    h = u % NH
                    for i, c0 in ((0, 0), (1, 128)):
                        K = 128 * (i + 1)
                        qs = slice(128 * i, 128 * i + 128)
                        if u < NH:
                            r0 = 32 * (h % 4)
                            pe.matmul(o[:, c0:c0 + K], qlT[:, h, qs], ckvT[:, 0:K], start=True, stop=False)
                            mm = pe.matmul(o[:, c0:c0 + K], qrT[r0:r0 + 32, h // 4, qs], krT[r0:r0 + 32, 0:K], start=False, stop=True)
                        else:
                            r0 = 64 * (h % 2)
                            mm = pe.matmul(o[:, c0:c0 + K], qbT[r0:r0 + 64, h // 2, qs], kbT[r0:r0 + 64, h // 2, 0:K], start=True, stop=True)
                    mm.then_inc(product, 1)

                def turn_probs(u):
                    if u < NH:
                        pe.wait_ge(exp_ready, u + 1)
                    else:
                        pe.wait_ge(cnt_ready, u - NH + 1)
                    turn("PT", u, parts=[(prob[:, u % 2, 128 * i:128 * i + 128], 128, 128, 128 * i) for i in range(3)])

                def mix_values(u):
                    wait_moved(pe, "PT", u)
                    o = begin("O", u)
                    v = [va[:, t, 64 * u:64 * u + 64] if u < NH else z[:, t, VB + 64 * (u - NH):VB + 64 * (u - NH) + 64] for t in range(2)]
                    pt = probT[:, u % 2, :]
                    pe.matmul(o[:, 0:64], pt[:, 0:128], v[0], start=True, stop=True)
                    pe.matmul(o[:, 64:128], pt[:, 128:256], v[0], start=True, stop=False)
                    pe.matmul(o[:, 64:128], pt[:, 256:384], v[1], start=False, stop=True).then_inc(product, 1)

                for s in range(2 * NH + 2):
                    if s < 2 * NH:
                        scores(s)
                    if 1 <= s <= 2 * NH:
                        turn_probs(s - 1)
                    if s >= 2:
                        mix_values(s - 2)
                wait_moved(pe, "O", 2 * NH - 1)
                for g in range(2 * HP):
                    turn("mT", g, parts=[(oAB[:, t, 128 * g:128 * g + 128], 128, 128, 128 * t) for t in range(2)])
                pe.wait_ge(y_ready, 1)
                for t, (t0, m) in enumerate(TOK):
                    turn("yt", t, parts=[(yT[:, c, t0:t0 + m], 128, m, 128 * c) for c in range(2)])
                pe.wait_ge(ln_ready, 3)
                for c in range(2):
                    turn("ycT", c, parts=tokens(yt, 128 * c))

                def score_past(b):
                    wait_moved(pe, "cT", b, 3)
                    wait_moved(pe, "rT", b)
                    o = begin("ST", b)
                    for g in range(NPG // 4):
                        pe.matmul(o[:, 24 * g:24 * g + 24], rT[:, b % 2, g, :], qrB[:, b, :, :], start=True, stop=False, skip_group_check=True)
                        for i in range(4 * g, 4 * g + 4):
                            mm = pe.matmul(o[:, NH * i:NH * i + NH], cT[:, b % 2, 128 * i:128 * i + 128], qlT[:, :, SEQ + b],
                                           start=False, stop=True, skip_group_check=True)
                    mm.then_inc(product, 1)

                def past_half(half):
                    pe.wait_ge(past_ld, l * (16 * 2 * NB) + 16 * NB * (half + 1))
                    for b in range(4 * half, 4 * half + 5):
                        if b < 4 * half + 4:
                            for g in range(4):
                                turn("cT", b, g, parts=[(past[:, b % 4, 4 * g + i, :], 128, 128, 128 * i) for i in range(4)])
                            turn("rT", b, parts=[(pastr[:, b % 4, 4 * g:4 * g + 4, :].rearrange("p g c -> p (g c)"), 128, 128, 128 * g) for g in range(4)])
                        if b > 4 * half:
                            score_past(b - 1)

                def maxima(n, c):
                    pe.wait_ge(smx_ready, n + 1 if n < 1 else (2 if n == 2 else 3))
                    turn("mx", n, parts=[(smx[:, n, 0:c], 128, c, 0)])
                    pe.wait_ge(sdg_ready, n + 1 if n < 1 else (2 if n == 2 else 3))
                    dense(("mb", n), [(ones[0:c, :], sdg[0:c, n, 0:c])], 128, c)
                    pe.wait_ge(sden_ready, n + 1 if n < 1 else (2 if n == 2 else 3))
                    dense(("dn", n), [(ones[:, :], sden[:, n, 0:c])], 128, c)

                def latent_mix(half):
                    o = begin("ol", half)
                    pe.matmul(o[:, 0:24], z[0:NB, 2, CKV:CKV + LAT], STm[0:NB, :, NPG, :], start=True, stop=False, skip_group_check=True)
                    for b in range(4):
                        for g in range(NPG):
                            mm = pe.matmul(o[:, NH * b:NH * b + NH], past[:, b, g, :], STm[:, b, g, :], start=False,
                                           stop=(g == NPG - 1), skip_group_check=True)
                    mm.then_inc(product, 1)

                past_half(0)
                o = begin("ext")
                pe.matmul(o[0:NB, 0:48], ckvT[:, SEQ:T], qlT[:, :, SEQ:T], start=True, stop=False)
                pe.matmul(o[0:NB, 0:48], krT[0:32, SEQ:T], qrS[0:32, :, :], start=False, stop=True).then_inc(product, 1)
                for b in range(NB):
                    dense(("qbc", b), [(ident[0:NB, b:b + 1].to_broadcast([NB, P]), z[0:NB, 2, QB:QB + 384])], 128, 384)
                maxima(0, 24)
                latent_mix(0)
                past_half(1)
                maxima(2, 48)
                maxima(1, 24)
                latent_mix(1)
                wait_moved(pe, "ol", 1)
                o = begin("os")
                for h in range(NH):
                    r0 = 64 * (h % 2)
                    mm = pe.matmul(o[r0:r0 + 64, NB * (h // 2):NB * (h // 2) + NB], wuv[:, HD * h:HD * h + HD], olT[:, :, h],
                                   start=True, stop=True, skip_group_check=True)
                mm.then_inc(product, 1)
                o = begin("ow")
                for h in range(NH):
                    r0 = 64 * (h % 2)
                    pe.matmul(o[r0:r0 + 64, NB * (h // 2):NB * (h // 2) + NB], z[0:NB, 2, VB + 64 * h:VB + 64 * h + 64], STw[0:NB, :, 3, h],
                              start=(h < 2), stop=False, skip_group_check=True)
                for b in range(NB):
                    pe.wait_ge(vw_ld[b % 2], 48 * (b // 2 + 1))
                    for d in range(3):
                        for h in range(NH):
                            r0 = 64 * (h % 2)
                            c0 = NB * (h // 2) + b
                            mm = pe.matmul(o[r0:r0 + 64, c0:c0 + 1], vw[:, b % 2, d, 64 * h:64 * h + 64], STw[:, b, d, h:h + 1],
                                           start=False, stop=(d == 2), skip_group_check=True)
                    mm.then_inc(vw_used if b < NB - 1 else product, 1)
                wait_moved(pe, "mT", 5)
                wait_moved(pe, "ow")
                for c in range(2):
                    pe.wait_ge(w_ld[(5 + c) % 2], 16 * ((5 + c) // 2 + 1))
                    for t, (t0, m) in enumerate(TOK):
                        dense(("xo", c, t), [(mixT[:, k, t0:t0 + m], wview(5 + c)[:, k, :]) for k in range(KD)], m, 512)
                pe.wait_ge(hn_ready, 6)
                for k in range(KD):
                    turn("fT", k, parts=tokens(hf, k * 128))
                pe.wait_ge(sk_ld, 16 * NSUB)
                for g in range(4):
                    turn("skT", g, parts=[(sk[:, 4 * g + i, :], 128, 128, 128 * i) for i in range(4)])
                wait_moved(pe, "fT", KD - 2)
                wait_moved(pe, "fT", KD - 1)
                for n in range(NSUB):
                    w = 7 + n // 4
                    if n % 4 == 0:
                        pe.wait_ge(w_ld[w % 2], 16 * (w // 2 + 1))
                    dense(("pq", n), [(wview(w)[:, k, 128 * (n % 4):128 * (n % 4) + 128], hT[:, k, :]) for k in range(KD)], 128, T)
                wait_moved(pe, "pq", NSUB - 1)
                for t in (2, 0, 1):
                    t0, m = TOK[t]
                    for g in range(4):
                        o = begin("s", t, g)
                        for i in range(4):
                            n = 4 * g + i
                            mm = pe.matmul(o[0:m, 128 * i:128 * i + 128], pqT[:, n, t0:t0 + m], skT[:, n, :], start=True, stop=True)
                        mm.then_inc(product, 1)
                def slots(t):
                    m = TOK[t][1]
                    turn("slot", t, parts=[(sel[0:m, t, s, :], m, 128, 128 * s) for s in range(3)])

                pe.wait_ge(psel_ld, 16 * PH)
                slots(2)
                for b in range(NB + 1):
                    if b < NB:
                        pe.wait_ge(erow_u_ld[b], l * 16 + 16)
                        for half in range(2):
                            turn("gu", b, half, parts=[(gath[b][:, 512 * half + 128 * i:512 * half + 128 * i + 128], 128, 128, 128 * i) for i in range(4)])
                    if b:
                        wait_moved(pe, "gu", b - 1, 1)
                        dense(("gz", b - 1), [(uT[(b - 1) % 2][:, 128 * c:128 * c + 128], hT[:, c, SEQ + b - 1:SEQ + b]) for c in range(KD)], 128, 1)
                pe.wait_ge(sel_ready, 1)
                slots(0)
                pe.wait_ge(coef_ready, NB)
                for half in range(2):
                    if half == 0:
                        pe.wait_ge(erow_v_ld, l * (16 * NB) + 16 * NB)
                    dense(("gy", half), [(coef[:, b, :], gath[b][:, 512 * half:512 * half + 512]) for b in range(NB)], NB, 512)
                pe.wait_ge(sel_ready, 2)
                slots(1)
                wait_moved(pe, "slot", 1)
                wait_moved(pe, "gy", 1)
                for _ in range(2):
                    pe.nop().then_inc(g_prod, 1)
                with pe.Fori(0, SEQ // GT) as it:
                    for g in range(2):
                        pe.wait_ge(hotA_ready, it * 2 + (g + 1))
                        pe.wait_ge(hotB_ready, it * 2 + (g + 1))
                        pe.wait_ge(g_moved, it * 2 + (g + 1))
                        hb = hotB if g == 0 else hotB2
                        for k in range(4):
                            mm = pe.matmul(ps[:, 6 + g, 128 * k:128 * k + 128], hotA[:, 4 * g + k, :], hb[:, k, :], start=True, stop=True)
                        mm.then_inc(g_prod, 1)
                pe.wait_ge(g_moved, 2 * (SEQ // GT) + 2)
                pe.wait_ge(acc_zero, 1)
                for n in range(4):
                    pe.matmul(ps[:, n, :], zeros[:, 0:128], zeros[:, 0:512], start=True, stop=False, skip_group_check=True)
                with pe.Fori(0, LOOPS) as it:
                    def turn_u(k):
                        pe.wait_ge(u_ld[k], it * 16 + 16)
                        for half, sem_ in ((0, uT_v), (1, uT_a)):
                            pe.wait_ge(sem_, it * UN + (k + 1))
                            for i in range(4):
                                c = 4 * half + i
                                mm = pe.transpose(ps[:, 6 + half, 128 * i:128 * i + 128], u_t[k][:, 128 * c:128 * c + 128], ident[:, :])
                            mm.then_inc(turned, 1)

                    def inputs(k):
                        pe.wait_ge(uT_v, it * UN + (k + 2))
                        pe.wait_ge(uT_a, it * UN + (k + 2))
                        pe.wait_ge(gelu_done, it * UN + (k + 1))
                        for c in range(KD):
                            mm = pe.matmul(ps[:, 4 + k % 2, 0:SEQ], uT[k % 2][:, 128 * c:128 * c + 128], hT[:, c, 0:SEQ], start=(c == 0), stop=(c == KD - 1))
                            if c == 0:
                                mm.then_inc(u_free[k], 1)
                        mm.then_inc(z_prod, 1)

                    def outputs(k):
                        pe.wait_ge(v_ld[k], it * 16 + 16)
                        pe.wait_ge(w_ready, it * UN + (k + 1))
                        for c in range(KD):
                            w = v_t[k][:, 128 * c:128 * c + 128]
                            mm = pe.matmul(ps[:, c // 2, 256 * (c % 2):256 * (c % 2) + 256], w, wgt_t[k % 2][:, 0:SEQ],
                                           start=False, stop=False, skip_group_check=True)
                        mm.then_inc(v_free[k], 1)

                    for k in range(UN + 2):
                        if k < UN:
                            turn_u(k)
                        if 1 <= k <= UN:
                            inputs(k - 1)
                        if k >= 2:
                            outputs(k - 2)
                pe.transpose(ps[:, 5, 0:128], ident[:, :], ident[:, :]).then_inc(acc_done, 1)
                pe.wait_ge(y_moved, 1)
                for c in range(2):
                    for t, (t0, m) in enumerate(TOK[:2]):
                        turn("xT", c, t, parts=[(yacc[:, 4 * c + i, t0:t0 + m], 128, m, 128 * i) for i in range(4)])
                pe.wait_ge(product, len(JOBS))
                layer_end(pe, 0)

        @block.scalar
        def _(act):
            def read(*name):
                who, n = READ[name]
                seen[0] += 1
                assert who == "A" and n == seen[0], name
                return arrive(act, *name)

            seen = [0]
            act.wait_ge(ones_set, 1)
            act.wait_ge(consts_ld, 16 * 24)
            with act.Fori(0, DEPTH) as l:
                seen[0] = 0

                def roots(k, cols):
                    act.wait_ge(sq_ready, k[0])
                    act.activation(stat[:, cols], stat[:, cols], ACT.Sqrt).then_inc(std_ready, 1)

                roots((3,), slice(0, 3))
                act.wait_ge(small_ld, 16 * 10)
                for k in range(1, KD, 2):
                    o = read("hT", k)
                    act.activation(hT[:, k, :], o[:, 0:T], ACT.Copy, scale=g_mix[:, k:k + 1]).then_inc(moved_a, 1)
                act.wait_ge(pad_set, 2)
                for c, (c0, n) in enumerate(ZCH):
                    for t, (t0, m) in enumerate(TOK):
                        o = read("z", c, t)
                        if c < 4:
                            act.copy(z[0:m, t, c0:c0 + n], o[0:m, 0:n]).then_inc(moved_a, 1)
                        else:
                            act.copy(z[0:m, t, GA:GA + CC], o[0:m, 0:CC])
                            act.activation(z[0:m, t, GB:GB + CC], o[0:m, CC:2 * CC], ACT.Sigmoid).then_inc(moved_a, 1)
                    if c == 1:
                        roots((4,), slice(3, 9))
                for k in range(2):
                    o = read("cqT", k)
                    act.activation(cqT[:, k, :], o[:, 0:T], ACT.Copy, scale=g_q[:, k:k + 1]).then_inc(moved_a, 1)
                o = read("ckvT")
                act.copy(ckvT, o[:, 0:T]).then_inc(moved_a, 1)
                o = read("krT")
                act.copy(krT, o[:, 0:T]).then_inc(moved_a, 1)
                o = read("ukT")
                act.copy(ukT.rearrange("p g c -> p (g c)"), o[:, 0:384]).then_inc(moved_a, 1)
                for t, (t0, m) in enumerate(TOK):
                    for n in range(2):
                        o = read("q", t, n)
                        oh = o[0:m, 0:288].rearrange("p (h x) -> p h x", h=3)
                        qn = q[0:m, t, 192 * n:192 * n + 192].rearrange("p (h x) -> p h x", h=3)
                        qr = q[0:m, t, NH * NOPE + 96 * n:NH * NOPE + 96 * n + 96].rearrange("p (h x) -> p h x", h=3)
                        act.copy(qn, oh[:, :, 0:NOPE])
                        act.copy(qr, oh[:, :, NOPE:]).then_inc(moved_a, 1)
                for g in range(HP):
                    o = read("qnT", g)
                    act.copy(qnT[:, g, :], o[:, 0:T]).then_inc(moved_a, 1)
                o = read("qrT", 0)
                act.copy(qrT[:, 0, :], o[:, 0:T]).then_inc(moved_a, 1)
                o = read("qrT", 1)
                act.copy(qrT[0:64, 1, :], o[0:64, 0:T]).then_inc(moved_a, 1)
                o = read("qrS")
                for i in range(4):
                    act.copy(qrB[32 * i:32 * i + 32, :, i, :], o[32 * i:32 * i + 32, 0:48].rearrange("p (h b) -> p b h", h=NH))
                act.copy(qrS.rearrange("p h b -> p (h b)"), o[:, 0:48]).then_inc(moved_a, 1)
                for t in range(2):
                    o = read("va", t)
                    act.copy(va[:, t, :], o[:, 0:384]).then_inc(moved_a, 1)
                o = read("cw")
                act.copy(cwT.rearrange("p c j -> p (c j)"), o[:, 0:2 * CW]).then_inc(moved_a, 1)
                for c in range(2):
                    o = read("sc", c)
                    act.copy(gsT[:, c, :, 0:CW - 1], o[:, 0:240].rearrange("p (b j) -> p b j", b=NB)).then_inc(moved_a, 1)
                for s in range(2 * NH + 1):
                    if s < 2 * NH:
                        act.wait_ge(nmx_ready, s + 1)
                        for i, c0 in ((0, 0), (1, 128)):
                            pr = prob[:, s % 2, c0:c0 + 128 * (i + 1)]
                            e = act.activation(pr, pr, ACT.Exp, bias=nmx[:, s, i:i + 1], scale=SA if s < NH else SB,
                                               accum_out=den[:, s, i:i + 1] if s < NH else None)
                        e.then_inc(exp_ready, 1)
                    if s >= 1:
                        o = read("PT", s - 1)
                        act.copy(probT[:, (s - 1) % 2, :], o[:, 0:384]).then_inc(moved_a, 1)
                for g in range(2 * HP):
                    o = read("mT", g)
                    act.copy(mixT[:, g, 0:SEQ], o[:, 0:SEQ]).then_inc(moved_a, 1)
                for t, (t0, m) in enumerate(TOK):
                    o = read("yt", t)
                    act.copy(yt[0:m, t, :], o[0:m, 0:CC]).then_inc(moved_a, 1)
                roots((5,), slice(9, 12))
                for c in range(2):
                    o = arrive(act, "ycT", c)
                    act.activation(ycs[:, c, :], o[:, 0:T], ACT.Sigmoid, bias=g_lb[:, c:c + 1], scale=g_lg[:, c:c + 1]).then_inc(sig_ready, 1)

                def past_half(half):
                    for b in range(4 * half, 4 * half + 5):
                        if b < 4 * half + 4:
                            for g in range(0, 4, 2):
                                o = read("cT", b, g)
                                act.copy(cT[:, b % 2, 512 * g:512 * g + 512], o[:, 0:512]).then_inc(moved_a, 1)
                            o = read("rT", b)
                            act.copy(rT[:, b % 2, :, :].rearrange("p g k -> p (g k)"), o[:, 0:512]).then_inc(moved_a, 1)
                        if b > 4 * half:
                            o = read("ST", b - 1)
                            act.copy(STm[:, (b - 1) % 4, 0:NPG, :].rearrange("p g h -> p (g h)"), o[:, 0:NPG * NH]).then_inc(moved_a, 1)

                def sample_exp(n, S, scale):
                    wait_moved(act, "mb", n)
                    flat = S.rearrange("p b g h -> p (b g h)")
                    act.activation(flat, flat, ACT.Exp, scale=scale).then_inc(sexp_ready, 1)

                past_half(0)
                sample_exp(0, STm, SA)
                past_half(1)
                sample_exp(2, STw, SB)
                sample_exp(1, STm, SA)
                roots((8,), slice(0, 3))
                for k in range(1, KD, 2):
                    o = read("fT", k)
                    act.activation(hT[:, k, :], o[:, 0:T], ACT.Copy, scale=g_ffn[:, k:k + 1]).then_inc(moved_a, 1)
                for g in range(4):
                    o = read("skT", g)
                    act.copy(skT[:, 4 * g:4 * g + 4, :].rearrange("p n c -> p (n c)"), o[:, 0:512]).then_inc(moved_a, 1)
                for n in range(NSUB):
                    o = read("pq", n)
                    act.copy(pqT[:, n, :], o[:, 0:T]).then_inc(moved_a, 1)
                for t in (2, 0, 1):
                    t0, m = TOK[t]
                    for g in range(4):
                        o = read("s", t, g)
                        act.copy(sc[0:m, t, 4 * g:4 * g + 4, :].rearrange("p n c -> p (n c)"), o[0:m, 0:512]).then_inc(moved_a, 1)
                def slots(t):
                    t0, m = TOK[t]
                    o = read("slot", t)
                    act.copy(slotT[:, :, t0:t0 + m], o[:, 0:384].rearrange("p (s c) -> p s c", s=3)[:, :, 0:m]).then_inc(moved_a, 1)

                act.wait_ge(cand_max, 1)
                act.activation(psel[:, 2, :], psel[:, 2, :], ACT.Exp).then_inc(gexp, 1)
                slots(2)
                act.wait_ge(cand_max, 2)
                act.activation(sel[:, 0, 2, :], sel[:, 0, 2, :], ACT.Exp).then_inc(gexp, 1)
                for b in range(NB + 1):
                    if b < NB:
                        for half in range(2):
                            o = read("gu", b, half)
                            act.copy(uT[b % 2][:, 512 * half:512 * half + 512], o[:, 0:512]).then_inc(moved_a, 1)
                    if b:
                        o = read("gz", b - 1)
                        act.activation(gel[:, b - 1:b], o[:, 0:1], ACT.Gelu).then_inc(moved_a, 1)
                for b in range(NB):
                    if b == 0:
                        wait_moved(act, "gz", NB - 1)
                    act.activation(coef[:, b, b:b + 1], gel[:, b:b + 1], ACT.Copy, scale=slotT[:, 2, SEQ + b:SEQ + b + 1]).then_inc(coef_ready, 1)
                slots(0)
                act.wait_ge(cand_max, 3)
                act.activation(sel[:, 1, 2, :], sel[:, 1, 2, :], ACT.Exp).then_inc(gexp, 1)
                slots(1)
                for _ in range(2):
                    act.nop().then_inc(g_moved, 1)
                with act.Fori(0, SEQ // GT) as it:
                    for g in range(2):
                        act.wait_ge(g_prod, it * 2 + (g + 3))
                        act.copy(G[:, bass.ds(it * GT + 4 * g, 4), :].rearrange("p t j -> p (t j)"), ps[:, 6 + g, :]).then_inc(g_moved, 1)
                act.nop().then_inc(uT_a, 1)
                act.nop().then_inc(gelu_done, 1)
                with act.Fori(0, LOOPS) as it:
                    for k in range(UN + 1):
                        if k < UN:
                            act.wait_ge(turned, it * (2 * UN) + (2 * k + 2))
                            act.copy(uT[k % 2][:, 512:1024], ps[:, 7, :]).then_inc(uT_a, 1)
                        if k >= 1:
                            act.wait_ge(z_prod, it * UN + k)
                            act.activation(act_t[(k - 1) % 2][:, 0:SEQ], ps[:, 4 + (k - 1) % 2, 0:SEQ], ACT.Gelu).then_inc(gelu_done, 1)
                act.wait_ge(gelu_done, NK + 1)
                layer_end(act, 1)
            act.wait_ge(f_sq, 3)
            act.activation(stat[:, 0:3], stat[:, 0:3], ACT.Sqrt).then_inc(f_std, 1)

        @block.vector
        def _(dve):
            steps, seen, last_tap = [0], [0], [0, 0]

            def step(ins):
                steps[0] += 1
                ins.then_inc(vstep, 1)
                return steps[0]

            def settle():
                dve.wait_ge(vstep, steps[0])

            def read(*name):
                who, n = READ[name]
                seen[0] += 1
                assert who == "V" and n == seen[0], name
                return arrive(dve, *name)

            def squares(dst, done):
                for t, (t0, m) in enumerate(TOK):
                    dve.tensor_tensor_reduce(dst[0:m, t, :], X[0:m, t, :], X[0:m, t, :], 1.0 / D, EPS, ALU.mult, ALU.add,
                                             stat[0:m, t:t + 1]).then_inc(done, 1)

            def rotate(x1, x2, cos, sin, ta, tb):
                step(dve.tensor_tensor(ta, x1, sin, ALU.mult))
                step(dve.tensor_tensor(tb, x2, sin, ALU.mult))
                settle()
                step(dve.tensor_tensor(x1, x1, cos, ALU.mult))
                step(dve.tensor_tensor(x2, x2, cos, ALU.mult))
                settle()
                step(dve.tensor_tensor(x1, x1, tb, ALU.subtract))
                return dve.tensor_tensor(x2, x2, ta, ALU.add)

            dve.wait_ge(consts_ld, 16 * 24)
            dve.wait_ge(ones_set, 1)
            dve.memset(eoff[:, :], 0.0)
            dve.memset(coef[:, :, :], 0.0)
            dve.tensor_scalar(pidx[:, :], pages[:, :], 8.0, sub[:, 0:1], ALU.mult, ALU.add).then_inc(rows_ready, 1)
            with dve.Fori(0, DEPTH) as l:
                steps[0], seen[0] = 0, 0

                def norm(dst, k):
                    squares(dst, sq_ready)
                    dve.wait_ge(std_ready, k)
                    step(dve.reciprocal(stat[:, 0:3], stat[:, 0:3]))
                    settle()
                    for t, (t0, m) in enumerate(TOK):
                        dve.tensor_scalar(dst[0:m, t, :], X[0:m, t, :], stat[0:m, t:t + 1], None, ALU.mult).then_inc(hn_ready, 1)

                norm(hn, 1)
                dve.wait_ge(small_ld, 16 * 10)
                for k in range(0, KD, 2):
                    o = read("hT", k)
                    dve.tensor_scalar(hT[:, k, :], o[:, 0:T], g_mix[:, k:k + 1], None, ALU.mult).then_inc(moved_v, 1)
                wait_moved(dve, "z", 0, 2)
                dve.wait_ge(pad_set, 2)
                for i, (c0, n) in enumerate(((CQ, QL), (CKV, LAT))):
                    for t in range(3):
                        zz = z[:, t, c0:c0 + n]
                        step(dve.tensor_tensor_reduce(junk[:, 0:n], zz, zz, 1.0 / n, EPS, ALU.mult, ALU.add, stat[:, 3 + 3 * i + t:4 + 3 * i + t]))
                        settle()
                dve.nop().then_inc(sq_ready, 1)
                dve.wait_ge(std_ready, 2)
                step(dve.reciprocal(stat[:, 3:9], stat[:, 3:9]))
                settle()
                cq, ckv = z[:, :, CQ:CQ + QL], z[:, :, CKV:CKV + LAT]
                dve.tensor_tensor(cq, cq, stat[:, 3:6].unsqueeze(2).to_broadcast([P, 3, QL]), ALU.mult).then_inc(lat_ready, 1)
                step(dve.tensor_tensor(ckv, ckv, stat[:, 6:9].unsqueeze(2).to_broadcast([P, 3, LAT]), ALU.mult))
                settle()
                step(dve.tensor_tensor(ckv, ckv, kvg.unsqueeze(1).to_broadcast([P, 3, LAT]), ALU.mult))
                cosA, sinA, cosB, sinB = rope[:, :, 0:16], rope[:, :, 16:32], rope[:, :, 32:64], rope[:, :, 64:96]
                ra = ropet[:, 0:1152]
                rb = ropet[:, 1152:2304]

                def cut3(a, n):
                    return a[:, 0:3 * n].rearrange("p (t c) -> p t c", t=3)

                rotate(z[:, :, KR:KR + 16], z[:, :, KR + 16:KR + 32], cosA, sinA, cut3(ra, 16), cut3(rb, 16)).then_inc(lat_ready, 1)
                dve.wait_ge(lat_ready, 2)
                settle()
                dve.tensor_copy(krr, z[:, :, KR:KR + ROPE].unsqueeze(2).to_broadcast([P, 3, 4, ROPE])).then_inc(lat_ready, 1)
                wait_moved(dve, "z", 2, 2)
                for t in range(3):
                    x = z[:, t, QB:QB + 768].rearrange("p (h s c) -> p h s c", h=2 * NH, s=2)
                    tt = [r[:, 384 * t:384 * t + 384].rearrange("p (h c) -> p h c", h=2 * NH) for r in (ra, rb)]
                    last = rotate(x[:, :, 0, :], x[:, :, 1, :], cosB[:, t, :].unsqueeze(1).to_broadcast([P, 2 * NH, 32]),
                                  sinB[:, t, :].unsqueeze(1).to_broadcast([P, 2 * NH, 32]), tt[0], tt[1])
                    step(last)
                settle()
                dve.nop().then_inc(qk_ready, 1)
                wait_moved(dve, "z", 4, 2)
                dve.tensor_tensor(z[:, :, GA:GA + CC], z[:, :, GA:GA + CC], z[:, :, GB:GB + CC], ALU.mult).then_inc(g_ready, 1)
                wait_moved(dve, "q", 2, 1)
                for t, (t0, m) in enumerate(TOK):
                    x = q[0:m, t, NH * NOPE:].rearrange("p (h c) -> p h c", h=NH)
                    tt = [r[0:m, 96 * t:96 * t + 96].rearrange("p (h c) -> p h c", h=NH) for r in (ra, rb)]
                    step(rotate(x[:, :, 0:16], x[:, :, 16:32], cosA[0:m, t, :].unsqueeze(1).to_broadcast([m, NH, 16]),
                                sinA[0:m, t, :].unsqueeze(1).to_broadcast([m, NH, 16]), tt[0], tt[1]))
                settle()
                dve.tensor_copy(qrr[0:NB], q[0:NB, 2, NH * NOPE:].rearrange("p (h c) -> p h c", h=NH).unsqueeze(2).to_broadcast([NB, NH, 4, ROPE])).then_inc(q_ready, 1)
                for g in range(HP):
                    o = read("qbT", g)
                    dve.tensor_copy(qbT[:, g, :], o[:, 0:T]).then_inc(moved_v, 1)
                for g in range(HP):
                    o = read("kbT", g)
                    dve.tensor_copy(kbT[:, g, :], o[:, 0:T]).then_inc(moved_v, 1)
                for h in range(NH):
                    o = read("qlT", h)
                    dve.tensor_copy(qlT[:, h, :], o[:, 0:T]).then_inc(moved_v, 1)
                for c in range(2):
                    o = read("gT", c)
                    step(dve.tensor_copy(gT[:, c, CW - 1:CW - 1 + SEQ], o[:, 0:SEQ]))
                    dve.tensor_copy(gsT[:, c, :, CW - 1], o[:, SEQ:T]).then_inc(moved_v, 1)
                wait_moved(dve, "sc", 1)
                wait_moved(dve, "gT", 1)
                settle()

                def tap(n):
                    j, c = n // 2, n % 2
                    y, x, w = yT[:, c, 0:SEQ], gT[:, c, j:j + SEQ], cwT[:, c, j:j + 1]
                    if j == 0:
                        last_tap[c] = step(dve.tensor_scalar(y, x, w, g_cb[:, c:c + 1], ALU.mult, ALU.add))
                    else:
                        dve.wait_ge(vstep, last_tap[c])
                        last_tap[c] = step(dve.scalar_tensor_tensor(y, x, w, y, ALU.mult, ALU.add))

                taps = iter(range(2 * CW))
                for s in range(2 * NH + 2):
                    if s < 2 * NH:
                        o = read("S", s)
                        dve.tensor_tensor(prob[:, s % 2, :], o[:, 0:384], mbias if s < NH else cbias, ALU.add).then_inc(moved_v, 1)
                        wait_moved(dve, "S", s)
                        for i, c0 in ((0, 0), (1, 128)):
                            step(dve.tensor_reduce(nmx[:, s, i:i + 1], prob[:, s % 2, c0:c0 + 128 * (i + 1)], AX, ALU.max))
                        settle()
                        dve.tensor_scalar(nmx[:, s, :], nmx[:, s, :], -SA if s < NH else -SB, None, ALU.mult).then_inc(nmx_ready, 1)
                    u = s - 1
                    if NH <= u < 2 * NH:
                        dve.wait_ge(exp_ready, u + 1)
                        for i, c0 in ((0, 0), (1, 128)):
                            c1 = c0 + 128 * (i + 1)
                            e = dve.tensor_tensor_reduce(prob[:, u % 2, c0:c1], prob[:, u % 2, c0:c1], cnt[:, c0:c1], 1.0, 0.0,
                                                         ALU.mult, ALU.add, den[:, u, i:i + 1])
                            if i == 0:
                                step(e)
                        e.then_inc(cnt_ready, 1)
                    for n in range(5):
                        k = next(taps, None)
                        if k is not None:
                            tap(k)
                    u = s - 2
                    if u >= 0:
                        if u < NH:
                            dve.wait_ge(exp_ready, u + 1)
                        else:
                            dve.wait_ge(cnt_ready, u - NH + 1)
                        step(dve.reciprocal(rden[:, u, :], den[:, u, :]))
                        o = read("O", u)
                        settle()
                        dve.tensor_tensor(oAB[:, :, 64 * u:64 * u + 64], o[:, 0:128].rearrange("p (t c) -> p t c", t=2),
                                          rden[:, u, :].unsqueeze(2).to_broadcast([P, 2, 64]), ALU.mult).then_inc(moved_v, 1)
                for k in taps:
                    tap(k)
                dve.wait_ge(product, NUM["mT", 2 * HP - 1] + 1)
                for c in range(2):
                    t1 = junk[:, c * 248:(c + 1) * 248].rearrange("p (b j) -> p b j", b=NB)
                    step(dve.tensor_tensor(t1, gsT[:, c, :, :], cwT[:, c, :].unsqueeze(1).to_broadcast([P, NB, CW]), ALU.mult))
                    settle()
                    step(dve.tensor_reduce(yT[:, c, SEQ:T], t1, AX, ALU.add))
                    settle()
                    step(dve.tensor_scalar(yT[:, c, SEQ:T], yT[:, c, SEQ:T], g_cb[:, c:c + 1], None, ALU.add))
                settle()
                dve.nop().then_inc(y_ready, 1)
                for t, (t0, m) in enumerate(TOK):
                    wait_moved(dve, "yt", t)
                    step(dve.bn_stats(bnst[0:m, t, 0:6], yt[0:m, t, :]))
                    settle()
                    step(dve.bn_aggr(bnst[0:m, t, 6:8], bnst[0:m, t, 0:6]))
                    settle()
                    step(dve.tensor_scalar(stat[0:m, 9 + t:10 + t], bnst[0:m, t, 7:8], EPS, None, ALU.add))
                settle()
                dve.nop().then_inc(sq_ready, 1)
                dve.wait_ge(std_ready, 3)
                step(dve.reciprocal(stat[:, 9:12], stat[:, 9:12]))
                settle()
                for t, (t0, m) in enumerate(TOK):
                    dve.tensor_scalar(yt[0:m, t, :], yt[0:m, t, :], bnst[0:m, t, 6:7], stat[0:m, 9 + t:10 + t],
                                      ALU.subtract, ALU.mult).then_inc(ln_ready, 1)
                for c in range(2):
                    o = read("ycT", c)
                    dve.wait_ge(sig_ready, c + 1)
                    step(dve.tensor_scalar(ycs[:, 2, :], o[:, 0:T], g_lg[:, c:c + 1], g_lb[:, c:c + 1], ALU.mult, ALU.add))
                    settle()
                    dve.tensor_tensor(mixT[:, 6 + c, :], ycs[:, 2, :], ycs[:, c, :], ALU.mult).then_inc(moved_v, 1)
                    wait_moved(dve, "ycT", c)

                def past_half(half):
                    for b in range(4 * half, 4 * half + 4):
                        for g in range(1, 4, 2):
                            o = read("cT", b, g)
                            dve.tensor_copy(cT[:, b % 2, 512 * g:512 * g + 512], o[:, 0:512]).then_inc(moved_v, 1)

                def new_keys(half):
                    step(dve.tensor_tensor(STm[0:NB, :, NPG, :], extS[:, :, 4 * half:4 * half + 4].rearrange("p h b -> p b h"),
                                           diag[:, 4 * half:4 * half + 4].unsqueeze(2).to_broadcast([NB, 4, NH]), ALU.add))
                    settle()

                def chain(n, S, c, order, last_slot):
                    ng, nb = S.shape[2], S.shape[1]

                    def bc(a):
                        return a.rearrange("p (b h) -> p b h", b=nb).unsqueeze(2).to_broadcast([P, nb, ng, NH])

                    dve.tensor_reduce(smx[:, n, 0:c].rearrange("p (b h) -> p b h", b=nb), S.rearrange("p b g h -> p b h g"),
                                      AX, ALU.max).then_inc(smx_ready, 1)
                    o = read("mx", n)
                    dve.tensor_reduce(smc[0:c, n:n + 1], o[0:c, 0:128], AX, ALU.max).then_inc(moved_v, 1)
                    wait_moved(dve, "mx", n)
                    dve.tensor_scalar(sdg[0:c, n, 0:c], ident[0:c, 0:c], smc[0:c, n:n + 1], None, ALU.mult).then_inc(sdg_ready, 1)
                    o = read("mb", n)
                    for b in range(nb):
                        e = dve.tensor_tensor(S[:, b, :, :], S[:, b, :, :], o[:, NH * b:NH * b + NH].unsqueeze(1).to_broadcast([P, ng, NH]),
                                              ALU.subtract)
                        if b < nb - 1:
                            step(e)
                    settle()
                    e.then_inc(moved_v, 1)
                    dve.wait_ge(sexp_ready, order)
                    if last_slot:
                        step(dve.tensor_scalar(S[:, :, ng - 1, :], S[:, :, ng - 1, :], float(len(DIL)), None, ALU.mult))
                        settle()
                    dve.tensor_reduce(sden[:, n, 0:c].rearrange("p (b h) -> p b h", b=nb), S.rearrange("p b g h -> p b h g"),
                                      AX, ALU.add).then_inc(sden_ready, 1)
                    o = read("dn", n)
                    dve.reciprocal(srd[:, n, 0:c], o[:, 0:c]).then_inc(moved_v, 1)
                    wait_moved(dve, "dn", n)

                def latents_out(half):
                    o = read("ol", half)
                    dve.tensor_tensor(olT[:, 4 * half:4 * half + 4, :].rearrange("p b h -> p (b h)"), o[:, 0:24],
                                      srd[:, half, 0:24], ALU.mult).then_inc(moved_v, 1)

                past_half(0)
                step(dve.memset(STm[:, :, NPG, :], NEG))
                step(dve.memset(STw[:, :, 3, :], NEG))
                settle()
                o = read("ext")
                dve.tensor_copy(extS.rearrange("p h b -> p (h b)"), o[0:NB, 0:48]).then_inc(moved_v, 1)
                wait_moved(dve, "ext")
                new_keys(0)
                for b in range(NB):
                    o = read("qbc", b)
                    dve.wait_ge(kw_ld, 48 * (b + 1))
                    e = dve.tensor_tensor(kprod, kw, o[:, 0:384].unsqueeze(1).to_broadcast([P, 3, 384]), ALU.mult)
                    e.then_inc(moved_v, 1)
                    wait_moved(dve, "qbc", b)
                    dve.tensor_reduce(STw[:, b, 0:3, :], kprod.rearrange("p d (h c) -> p d h c", h=NH), AX, ALU.add).then_inc(kw_used, 1)
                    dve.wait_ge(kw_used, b + 1)
                step(dve.tensor_tensor(kprod[0:NB, 0, :], z[0:NB, 2, QB:QB + 384], z[0:NB, 2, KB:KB + 384], ALU.mult))
                settle()
                step(dve.tensor_reduce(kprod[0:NB, 1, 0:NH], kprod[0:NB, 0, :].rearrange("p (h c) -> p h c", h=NH), AX, ALU.add))
                settle()
                step(dve.tensor_tensor(STw[0:NB, :, 3, :], kprod[0:NB, 1, 0:NH].unsqueeze(1).to_broadcast([NB, NB, NH]),
                                       diag[:, :].unsqueeze(2).to_broadcast([NB, NB, NH]), ALU.add))
                for b in range(4):
                    wait_moved(dve, "ST", b)
                settle()
                chain(0, STm, 24, 1, False)
                latents_out(0)
                past_half(1)
                wait_moved(dve, "ST", 7)
                step(dve.memset(STm[:, :, NPG, :], NEG))
                settle()
                new_keys(1)
                chain(2, STw, 48, 2, True)
                chain(1, STm, 24, 3, False)
                latents_out(1)
                o = read("os")
                dve.tensor_copy(mixT[:, 0:3, SEQ:T], o[:, 0:24].rearrange("p (g b) -> p g b", g=3)).then_inc(moved_v, 1)
                o = read("ow")
                rd = srd[:, 2, :].rearrange("p (b g a) -> p b g a", b=NB, g=HP)
                for a in range(2):
                    e = dve.tensor_tensor(mixT[64 * a:64 * a + 64, 3:6, SEQ:T], o[64 * a:64 * a + 64, 0:24].rearrange("p (g b) -> p g b", g=3),
                                          rd[64 * a:64 * a + 64, :, :, a].rearrange("p b g -> p g b"), ALU.mult)
                    if a == 0:
                        step(e)
                settle()
                e.then_inc(moved_v, 1)

                def add_to_x(name, tiles=3):
                    for c in range(2):
                        for t, (t0, m) in enumerate(TOK[:tiles]):
                            o = read(name, c, t)
                            xs = X[0:m, t, 512 * c:512 * c + 512]
                            dve.tensor_tensor(xs, xs, o[0:m, 0:512], ALU.add).then_inc(moved_v, 1)
                    wait_moved(dve, name, 1, tiles - 1)

                add_to_x("xo")
                dve.wait_ge(stored, 1)
                norm(hf, 4)
                for k in range(0, KD, 2):
                    o = read("fT", k)
                    dve.tensor_scalar(hT[:, k, :], o[:, 0:T], g_ffn[:, k:k + 1], None, ALU.mult).then_inc(moved_v, 1)

                def top16(*rows):
                    done = [steps[0]] * len(rows)

                    def each(op):
                        for i, r in enumerate(rows):
                            dve.wait_ge(vstep, done[i])
                            done[i] = step(op(*r))

                    each(lambda v, ix, src: dve.max(v[:, 0:8], src))
                    each(lambda v, ix, src: dve.max_index(ix[:, 0:8], v[:, 0:8], src))
                    each(lambda v, ix, src: dve.match_replace(src, v[:, 0:8], src, -3.0e38))
                    each(lambda v, ix, src: dve.max(v[:, 8:16], src))
                    each(lambda v, ix, src: dve.max_index(ix[:, 8:16], v[:, 8:16], src))

                def chosen(dst, ci_, ab, abf, hot_, tf, m, heads):
                    civ = ci_.bitcast(U32)
                    step(dve.tensor_single_scalar(ab[:, 0].bitcast(U32), civ, 4, ALU.logical_shift_right))
                    step(dve.tensor_single_scalar(ab[:, 1].bitcast(U32), civ, 15, ALU.bitwise_and))
                    settle()
                    step(dve.tensor_copy(abf, ab.bitcast(U32)))
                    settle()
                    n = heads * TOPK
                    for s in range(2):
                        io = iota[0:m, 0:TOPK].unsqueeze(1).to_broadcast([m, n, TOPK])
                        ch = (abf[:, s, :, :].rearrange("p h k -> p (h k)") if heads > 1 else abf[:, s, :]).unsqueeze(2).to_broadcast([m, n, TOPK])
                        flat = hot_.rearrange("p h k a -> p (h k) a") if heads > 1 else hot_
                        step(dve.tensor_tensor(flat, io, ch, ALU.is_equal))
                        settle()
                        step(dve.tensor_tensor(hot_, hot_, tf(s), ALU.mult))
                        settle()
                        step(dve.tensor_reduce(dst(s), flat, AX, ALU.add))
                        settle()

                dve.wait_ge(scp_ld, 16 * NSUB)
                settle()
                top16((tpk[:, 0, :], tpi.bitcast(U32), scp))
                settle()
                dve.tensor_copy(tpk[:, 1, :], tpi.bitcast(U32)).then_inc(p1_ready, 1)

                def first(t):
                    wait_moved(dve, "s", t, 3)
                    for n in range(0, NSUB, 4):
                        top16(*[(top[:, i, :], topi[:, i, :].bitcast(U32), sc[:, t, i, :]) for i in range(n, n + 4)])
                    settle()
                    step(dve.tensor_copy(topf, topi.bitcast(U32)))

                def sample_gates():
                    dve.wait_ge(tq_ld, 16)
                    dve.wait_ge(p1_ready, 1)
                    step(dve.tensor_tensor(pcand, tpk[0:64, 0, :].unsqueeze(2).to_broadcast([64, TOPK, TOPK]),
                                           tq[:, 0, :].unsqueeze(1).to_broadcast([64, TOPK, TOPK]), ALU.add))
                    settle()
                    top16((pcs, pci.bitcast(U32), pcand.rearrange("p a b -> p (a b)")))
                    settle()
                    chosen(lambda s: psel[:, s, :], pci, pab, pabf, phot,
                           lambda s: (tpk[0:64, 1, :] if s == 0 else tq[:, 1, :]).unsqueeze(1).to_broadcast([64, TOPK, TOPK]), 64, 1)
                    dve.tensor_scalar(psel[:, 2, :], pcs, pcs[:, 0:1], None, ALU.subtract).then_inc(cand_max, 1)
                    dve.wait_ge(gexp, 1)
                    step(dve.tensor_reduce(psum2[:, 0:1], psel[:, 2, :], AX, ALU.add))
                    settle()
                    step(dve.reciprocal(psum2[:, 1:2], psum2[:, 0:1]))
                    settle()
                    dve.tensor_scalar(psel[:, 2, :], psel[:, 2, :], psum2[:, 1:2], None, ALU.mult).then_inc(p2_ready, 1)

                def second(t):
                    tv = top.rearrange("p (h s) k -> p h s k", s=2)
                    tf = topf.rearrange("p (h s) k -> p h s k", s=2)
                    step(dve.tensor_tensor(cand.rearrange("p h (a b) -> p h a b", a=TOPK),
                                           tv[:, :, 0, :].unsqueeze(3).to_broadcast([P, PH, TOPK, TOPK]),
                                           tv[:, :, 1, :].unsqueeze(2).to_broadcast([P, PH, TOPK, TOPK]), ALU.add))
                    settle()
                    for h in range(0, PH, 4):
                        top16(*[(cs[:, i, :], ci[:, i, :].bitcast(U32), cand[:, i, :]) for i in range(h, h + 4)])
                    settle()
                    gt = sel[:, t, 2, :].rearrange("p (h k) -> p h k", h=PH)
                    dve.tensor_tensor(gt, cs, cs[:, :, 0:1].to_broadcast([P, PH, TOPK]), ALU.subtract).then_inc(cand_max, 1)
                    chosen(lambda s: sel[:, t, s, :], ci, cab, cabf, hot,
                           lambda s: tf[:, :, s, :].unsqueeze(2).to_broadcast([P, PH, TOPK, TOPK]), P, PH)
                    dve.wait_ge(gexp, t + 2)
                    step(dve.tensor_reduce(hsum[:, 0, :], gt, AX, ALU.add))
                    settle()
                    step(dve.reciprocal(hsum[:, 1, :], hsum[:, 0, :]))
                    settle()
                    dve.tensor_tensor(gt, gt, hsum[:, 1, :].unsqueeze(2).to_broadcast([P, PH, TOPK]), ALU.mult).then_inc(sel_ready, 1)
                    dve.wait_ge(sel_ready, t + 1)

                first(0)
                sample_gates()
                wait_moved(dve, "slot", 2)
                step(dve.scalar_tensor_tensor(efl[:, :], slotT[:, 0, SEQ:T], float(NK), slotT[:, 1, SEQ:T], ALU.mult, ALU.add))
                settle()
                dve.tensor_scalar(eidx[:, :], efl[:, :], eoff[:, 0:1], None, ALU.add).then_inc(e_ready, 1)
                second(0)
                first(1)
                second(1)
                for half in range(2):
                    o = read("gy", half)
                    xs = X[0:NB, 2, 512 * half:512 * half + 512]
                    dve.tensor_tensor(xs, xs, o[0:NB, 0:512], ALU.add).then_inc(moved_v, 1)
                dve.memset(zeros, 0.0).then_inc(acc_zero, 1)
                wait_moved(dve, "slot", 1)
                with dve.Fori(0, SEQ // GT) as it:
                    for g in range(2):
                        dve.wait_ge(g_prod, it * 2 + (g + 1))
                        hb = hotB if g == 0 else hotB2
                        ta = slotT[:, 0, bass.ds(it * GT + 4 * g, 4)].unsqueeze(2).to_broadcast([P, 4, P])
                        dve.tensor_tensor(hotA[:, 4 * g:4 * g + 4, :], iota[:, :].unsqueeze(1).to_broadcast([P, 4, P]), ta,
                                          ALU.is_equal).then_inc(hotA_ready, 1)
                        for k in range(4):
                            tk = bass.ds(it * GT + (4 * g + k), 1)
                            e = dve.tensor_scalar(hb[:, k, :], iota[:, :], slotT[:, 1, tk], slotT[:, 2, tk], ALU.is_equal, ALU.mult)
                        e.then_inc(hotB_ready, 1)
                dve.nop().then_inc(uT_v, 1)
                with dve.Fori(0, LOOPS) as it:
                    for k in range(UN + 1):
                        if k < UN:
                            dve.wait_ge(turned, it * (2 * UN) + (2 * k + 1))
                            dve.tensor_copy(uT[k % 2][:, 0:512], ps[:, 6, :]).then_inc(uT_v, 1)
                        if k >= 1:
                            dve.wait_ge(gelu_done, it * UN + (k + 1))
                            j = it * UN + (k - 1)
                            dve.tensor_tensor(wgt_t[(k - 1) % 2][:, 0:SEQ], act_t[(k - 1) % 2][:, 0:SEQ], G[:, :, bass.ds(j, 1)].rearrange("p t o -> p (t o)"),
                                              ALU.mult).then_inc(w_ready, 1)
                dve.wait_ge(acc_done, 1)
                dve.wait_ge(w_ready, NK)
                for n in range(4):
                    step(dve.tensor_copy(yacc[:, 2 * n:2 * n + 2, 0:SEQ], ps[:, n, :].rearrange("p (c t) -> p c t", c=2)))
                settle()
                dve.nop().then_inc(y_moved, 1)
                add_to_x("xT", 2)
                n_rows = A["cache_kv_latent"].shape[1] * 8
                dve.tensor_scalar(pidx[:, :], pidx[:, :], float(n_rows), None, ALU.add).then_inc(rows_ready, 1)
                step(dve.tensor_scalar(eoff[:, :], eoff[:, :], float(NK * NK), None, ALU.add))
                settle()
                layer_end(dve, 2)
            squares(fin, f_sq)
            dve.wait_ge(f_std, 1)
            dve.reciprocal(stat[:, 0:3], stat[:, 0:3]).then_inc(f_step, 1)
            dve.wait_ge(f_step, 1)
            dve.wait_ge(f_gld, 16)
            for t, (t0, m) in enumerate(TOK):
                dve.scalar_tensor_tensor(fin[0:m, t, :], X[0:m, t, :], stat[0:m, t:t + 1], gfin[0:m, :], ALU.mult, ALU.mult).then_inc(f_y, 1)


def constants():
    f = np.float32
    pos = np.zeros((P, 3), f)
    pos[:, 0], pos[:, 1] = np.arange(P), P + np.arange(P)
    pos[:, 2] = PAST
    rope = np.zeros((P, 3, 96), f)
    for dim, a in ((ROPE, 0), (HD, 32)):
        half = dim // 2
        inv = np.power(f(10000.0), -np.arange(half, dtype=f) * f(2.0) / f(dim)).astype(f)
        ang = (pos[:, :, None] * inv).astype(f)
        rope[:, :, a:a + half] = np.cos(ang)
        rope[:, :, a + half:a + 2 * half] = np.sin(ang)
    qi = np.arange(P)[:, None]
    dist = np.concatenate([qi - np.arange(P), P + qi - np.arange(2 * P)], axis=1)
    cnt = sum(((dist >= 0) & (dist <= 128 * d) & (dist % d == 0)).astype(f) for d in DIL)
    masks = np.concatenate([cnt, np.where(cnt > 0, 0, NEG), np.where(dist >= 0, 0, NEG)], axis=1).astype(f)
    return {
        "ident": np.eye(P, dtype=f),
        "iota": np.tile(np.arange(P, dtype=f), (P, 1)),
        "rope": rope,
        "sub": (np.arange(P, dtype=f) % 8)[:, None],
        "diag": np.where(np.eye(NB) > 0, 0, NEG).astype(f),
        "masks": masks,
    }


_OUTS = [(1, SEQ, D), (NB, 1, D), (DEPTH, 1, SEQ, LAT), (DEPTH, 1, SEQ, ROPE), (DEPTH, 1, SEQ, NH, HD), (DEPTH, 1, SEQ, NH, HD),
         (DEPTH, 1, CW - 1, CC), (DEPTH, NB, 1, LAT), (DEPTH, NB, 1, ROPE), (DEPTH, NB, PAST, NH, HD), (DEPTH, NB, PAST, NH, HD),
         (DEPTH, NB, CW - 1, CC)]


def kernel(**inputs):
    import concourse.bacc as _bacc
    from concourse.bass_utils import run_bass_kernel_spmd as _run

    nc = _bacc.Bacc("TRN2", target_bir_lowering=False, num_devices=1)
    arrays, A, C = {}, {}, {}
    for name, a in inputs.items():
        a = np.ascontiguousarray(a)
        arrays[f"in_{name}"] = a
        A[name] = nc.dram_tensor(f"in_{name}", a.shape, mybir.dt.from_np(a.dtype), kind="ExternalInput").ap()
    for name, a in constants().items():
        arrays[f"const_{name}"] = a
        C[name] = nc.dram_tensor(f"const_{name}", a.shape, F32, kind="ExternalInput").ap()
    outs = [nc.dram_tensor(f"out_{i}", s, F32, kind="ExternalOutput").ap() for i, s in enumerate(_OUTS)]
    program(nc, A, C, outs)
    r = _run(nc, [arrays], core_ids=[0])
    return tuple(r.results[0][f"out_{i}"] for i in range(len(_OUTS)))
```

```python
from contextlib import ExitStack

import numpy as np
import concourse.bass as bass
from concourse import mybir

F32 = mybir.dt.float32
F32R = mybir.dt.float32r
I32 = mybir.dt.int32
U32 = mybir.dt.uint32
ALU = mybir.AluOpType
ACT = mybir.ActivationFunctionType
AX = mybir.AxisListType.X

P = 128
D = 1024
KD = D // P
SEQ, NB = 256, 8
T = SEQ + NB
TOK = [(0, 128), (128, 128), (256, 8)]
DEPTH = 2
PAST, PAGE = 2048, 128
NPG = PAST // PAGE
NH = 6
HP = NH // 2
NOPE, ROPE, LAT = 64, 32, 128
HD = 64
QL = 256
CW, CC = 31, 256
CQ, CKV, KR, QB, KB, VB, GA, GB = 0, 256, 384, 416, 800, 1184, 1568, 1824
ZC = 2080
ZCH = [(0, 416), (416, 384), (800, 384), (1184, 384), (1568, 512)]
UQ = NH * (NOPE + ROPE)
SA, SB = float((NOPE + ROPE) ** -0.5), float(HD ** -0.5)
PH, NK, TOPK = 8, 128, 16
NSUB = 2 * PH
EPS = 1e-6
NEG = -1e30
DIL = (1, 4, 16)
UN = 4
LOOPS = NK // UN
STREAM = 9 * 1024 + 4 * (SEQ + NB)
GT = 8


def job_plan():
    jobs = [(("hT", k), "VA"[k % 2]) for k in range(KD)]
    jobs += [(("z", c, t), "A") for c in range(5) for t in range(3)]
    jobs += [(("cqT", 0), "A"), (("cqT", 1), "A"), (("ckvT",), "A"), (("krT",), "A"), (("ukT",), "A")]
    jobs += [(("q", t, n), "A") for t in range(3) for n in range(2)]
    jobs += [(("qbT", g), "V") for g in range(HP)] + [(("kbT", g), "V") for g in range(HP)]
    jobs += [(("qnT", g), "A") for g in range(HP)] + [(("qrT", g), "A") for g in range(2)] + [(("qrS",), "A")]
    jobs += [(("qlT", h), "V") for h in range(NH)]
    jobs += [(("va", t), "A") for t in range(2)]
    jobs += [(("cw",), "A"), (("sc", 0), "A"), (("sc", 1), "A"), (("gT", 0), "V"), (("gT", 1), "V")]
    for s in range(2 * NH + 2):
        if s < 2 * NH:
            jobs.append((("S", s), "V"))
        if 1 <= s <= 2 * NH:
            jobs.append((("PT", s - 1), "A"))
        if s >= 2:
            jobs.append((("O", s - 2), "V"))
    jobs += [(("mT", g), "A") for g in range(2 * HP)]
    jobs += [(("yt", t), "A") for t in range(3)]
    jobs += [(("ycT", c), "V") for c in range(2)]

    def pages(half):
        out = []
        for b in range(4 * half, 4 * half + 5):
            if b < 4 * half + 4:
                out += [(("cT", b, g), "A") for g in range(4)] + [(("rT", b), "A")]
            if b > 4 * half:
                out.append((("ST", b - 1), "A"))
            if b < 4:
                out += [(("qbc", 2 * b), "V"), (("qbc", 2 * b + 1), "V")]
        return out

    jobs += [(("ext",), "V")] + pages(0)
    jobs += [((name, n), "V") for name in ("mx", "mb", "dn") for n in (0, 2)]
    jobs += [(("ol", 0), "V"), (("ow",), "V"), (("olT", 0), "V")] + pages(1)
    jobs += [(("mx", 1), "V"), (("mb", 1), "V"), (("dn", 1), "V"), (("ol", 1), "V"), (("olT", 1), "V"), (("os",), "V")]
    jobs += [(("xo", c, t), "V") for c in range(2) for t in range(3)]
    jobs += [(("fT", k), "VA"[k % 2]) for k in range(KD)]
    jobs += [(("skT", g), "A") for g in range(4)]
    for g in range(4):
        jobs += [(("pq", n), "A") for n in range(4 * g, 4 * g + 4)]
        if g:
            jobs += [(("s", t, g - 1), "A") for t in (2, 0, 1)]
    jobs += [(("s", t, 3), "A") for t in (2, 0, 1)]
    jobs += [(("slot", 2), "A")]
    for b in range(NB + 1):
        if b < NB:
            jobs += [(("gu", b, 0), "A"), (("gu", b, 1), "A")]
        if b:
            jobs.append((("gz", b - 1), "A"))
    jobs += [(("slot", 0), "A"), (("gy", 0), "V"), (("gy", 1), "V"), (("slot", 1), "A")]
    jobs += [(("xT", c, t), "V") for c in range(2) for t in range(2)]
    return jobs


JOBS = job_plan()
NUM = {name: n for n, (name, _) in enumerate(JOBS)}
READ = {}
for _n, (_name, _who) in enumerate(JOBS):
    READ[_name] = (_who, sum(w == _who for _, w in JOBS[:_n + 1]))


def program(nc, A, C, outs):
    (y_p, y_s, lat_p, kr_p, wk_p, wv_p, cv_p, lat_s, kr_s, wk_s, wv_s, cv_s) = outs
    with ExitStack() as ctx:
        def sb(name, shape, dt=F32):
            return ctx.enter_context(nc.sbuf_tensor(name, shape, dt))

        layer_sems = []

        def sem(name):
            s = ctx.enter_context(nc.semaphore(name))
            layer_sems.append(s)
            return s

        X = sb("X", [P, 3, D])
        ident = sb("ident", [P, P])
        iota = sb("iota", [P, P])
        ones = sb("ones", [P, P])
        rope = sb("rope", [P, 3, 96])
        gains = sb("gains", [P, 2 * KD + 2 + 2 * 3])
        stat = sb("stat", [P, 16])
        bnst = sb("bnst", [P, 3, 8])
        nmx = sb("nmx", [P, 2 * NH, 2])
        den = sb("den", [P, 2 * NH, 2])
        rden = sb("rden", [P, 2 * NH, 2])
        diag = sb("diag", [NB, NB])
        pages = sb("pages", [P, NB], I32)
        pidx = sb("pidx", [P, NB], I32)
        sub = sb("sub", [P, 1])
        eoff = sb("eoff", [P, 1])
        eidx = sb("eidx", [P, NB], I32)
        efl = sb("efl", [P, NB])
        coef = sb("coef", [P, NB, NB])
        gel = sb("gel", [P, NB])
        g_mix, g_ffn, g_q = gains[:, 0:KD], gains[:, KD:2 * KD], gains[:, 2 * KD:2 * KD + 2]
        g_cb, g_lg, g_lb = (gains[:, 2 * KD + 2 + 2 * i:2 * KD + 4 + 2 * i] for i in range(3))

        BIG = SEQ * P
        big = sb("big", [P, BIG + 1664])
        with nc.sbuf_tensor("region", [P, STREAM + (KD + 3) * T + GT * P + 4 * P], F32) as region:
            pass
        stream = region[:, 0:STREAM]
        hT = region[:, STREAM:STREAM + KD * T].rearrange("p (k t) -> p k t", k=KD)
        o_hot = STREAM + KD * T
        hotA = region[:, o_hot:o_hot + GT * P].rearrange("p (a b) -> p a b", a=GT)
        hotB = region[:, o_hot + GT * P:o_hot + (GT + 4) * P].rearrange("p (a b) -> p a b", a=4)
        o_slot = o_hot + (GT + 4) * P
        slotT = region[:, o_slot:o_slot + 3 * T].rearrange("p (s t) -> p s t", s=3)
        wslot = [stream[:, i * 4096:(i + 1) * 4096] for i in range(2)]
        u_t = [stream[:, i * 1024:(i + 1) * 1024] for i in range(UN)]
        gath = [stream[:, i * 1024:(i + 1) * 1024] for i in range(NB)]
        uTs = [hotA[:, :, :].rearrange("p a b -> p (a b)"), stream[:, 8192:9216]]
        nw = stream[:, 9216:9216 + T]
        dist = stream[:, 9216 + T:9216 + T + 128]
        ring = sb("ring", [P, 5 * 1024])
        parts = sb("parts", [P, 9 * 1024], F32R)
        hp = [parts[:, i * KD * SEQ:(i + 1) * KD * SEQ].rearrange("p (k t) -> p k t", k=KD) for i in range(2)]
        uT = [parts[:, (4 + i) * 1024:(5 + i) * 1024] for i in range(2)]
        vp = [parts[:, (6 + i) * 1024:(7 + i) * 1024] for i in range(2)]
        wp = [[parts[:, 8192 + (2 * i + p) * SEQ:8192 + (2 * i + p + 1) * SEQ] for p in range(2)] for i in range(2)]
        G = big[:, 0:BIG].rearrange("p (t j) -> p t j", j=P)
        at = [0]

        def cut(n):
            a = at[0]
            at[0] += n
            assert at[0] <= BIG + 1664, at[0]
            return big[:, a:a + n]

        z = cut(3 * ZC).rearrange("p (t c) -> p t c", t=3)
        hn = z.rearrange("p t c -> p (t c)")[:, 0:3 * D].rearrange("p (t c) -> p t c", t=3)
        wuk, wuv = cut(NH * NOPE), cut(NH * HD)
        ukT = cut(HP * 128).rearrange("p (g c) -> p g c", g=HP)
        qnT = cut(HP * T).rearrange("p (g t) -> p g t", g=HP)
        qrT = cut(2 * T).rearrange("p (g t) -> p g t", g=2)
        qkT = cut(2 * HP * T)
        qbT = qkT[:, 0:HP * T].rearrange("p (g t) -> p g t", g=HP)
        kbT = qkT[:, HP * T:2 * HP * T].rearrange("p (g t) -> p g t", g=HP)
        krT = cut(T)
        ckvT = cut(T)
        cqT = cut(2 * T).rearrange("p (g t) -> p g t", g=2)
        qlT = cut(NH * T).rearrange("p (h t) -> p h t", h=NH)
        qrS = cut(NH * NB).rearrange("p (h b) -> p h b", h=NH)
        qrB = cut(NB * 4 * NH).rearrange("p (b i h) -> p b i h", b=NB, i=4)
        mixT = cut(KD * T).rearrange("p (k t) -> p k t", k=KD)
        kvg = cut(LAT)
        past = cut(4 * NPG * LAT).rearrange("p (b g c) -> p b g c", b=4, g=NPG)
        kw = cut(3 * 384).rearrange("p (d c) -> p d c", d=3)
        vw = cut(2 * 3 * 384).rearrange("p (s d c) -> p s d c", s=2, d=3)
        base = at[0]
        cnt = hotB[:, :, :].rearrange("p a b -> p (a b)")[:, 0:384]
        cbias = cut(384)
        mbias = cut(384)
        prob = slotT[:, :, :].rearrange("p s t -> p (s t)")[:, 0:768].rearrange("p (s c) -> p s c", s=2)
        probT = hotA[:, :, :].rearrange("p a b -> p (a b)")[:, 0:768].rearrange("p (s c) -> p s c", s=2)
        wuq = cut(2 * UQ).rearrange("p (k c) -> p k c", k=2)
        q = cut(3 * UQ).rearrange("p (t c) -> p t c", t=3)
        va = cut(2 * 384).rearrange("p (t c) -> p t c", t=2)
        oAB = cut(2 * 768).rearrange("p (t c) -> p t c", t=2)
        gT = cut(2 * 286).rearrange("p (c t) -> p c t", c=2)
        gsT = cut(2 * NB * CW).rearrange("p (c b j) -> p c b j", c=2, b=NB)
        cwT = cut(2 * CW).rearrange("p (c j) -> p c j", c=2)
        yT = qnT.rearrange("p g t -> p (g t)")[:, 0:2 * T].rearrange("p (c t) -> p c t", c=2)
        krr = kw.rearrange("p d c -> p (d c)")[:, 0:384].rearrange("p (t r c) -> p t r c", t=3, r=4)
        qrr = kw.rearrange("p d c -> p (d c)")[:, 384:384 + 768].rearrange("p (h r c) -> p h r c", h=NH, r=4)
        cwr = oAB[0:CW, 0, 0:256]
        scr = probT.rearrange("p s c -> p (s c)")[0:120, 0:512].rearrange("p (s c) -> p s c", s=2)
        ropet = vw.rearrange("p s d c -> p (s d c)")
        junk = oAB.rearrange("p t c -> p (t c)")[:, 512:512 + 768]
        yt = q.rearrange("p t c -> p (t c)")[:, 0:768].rearrange("p (t c) -> p t c", t=3)
        ycs = q.rearrange("p t c -> p (t c)")[:, 768:768 + 3 * T].rearrange("p (s t) -> p s t", s=3)
        at[0] = base
        cT = cut(2 * NPG * 128).rearrange("p (s k) -> p s k", s=2)
        rT = cut(2 * 512).rearrange("p (s g k) -> p s g k", s=2, g=4)
        STm = cut(4 * 17 * NH).rearrange("p (b g h) -> p b g h", b=4, g=17)
        STw = cut(NB * 4 * NH).rearrange("p (b g h) -> p b g h", b=NB, g=4)
        smc = cut(4)
        smx = cut(3 * 48).rearrange("p (n c) -> p n c", n=3)
        sden = cut(3 * 48).rearrange("p (n c) -> p n c", n=3)
        srd = cut(3 * 48).rearrange("p (n c) -> p n c", n=3)
        sdg = cut(3 * 48).rearrange("p (n c) -> p n c", n=3)
        extS = cut(48).rearrange("p (h b) -> p h b", h=NH)[0:NB]
        olT = cut(48).rearrange("p (b h) -> p b h", b=NB)
        olr = cut(512)[0:NH]
        kprod = qkT[:, 0:3 * 384].rearrange("p (d c) -> p d c", d=3)
        pastr = stream[:, 8192:8192 + 4 * NPG * ROPE].rearrange("p (b g c) -> p b g c", b=4, g=NPG)
        at[0] = 0
        hf = cut(3 * D).rearrange("p (t c) -> p t c", t=3)
        sk = cut(NSUB * 128).rearrange("p (n c) -> p n c", n=NSUB)
        skT = cut(NSUB * 128).rearrange("p (n c) -> p n c", n=NSUB)
        pqT = cut(NSUB * T).rearrange("p (n t) -> p n t", n=NSUB)
        sc = cut(3 * NSUB * NK).rearrange("p (t n c) -> p t n c", t=3, n=NSUB)
        top, topi, topf = (cut(2 * NSUB * TOPK).rearrange("p (t n c) -> p t n c", t=2, n=NSUB) for _ in range(3))
        cand = cut(PH * 256).rearrange("p (h c) -> p h c", h=PH)
        cs = cut(PH * TOPK).rearrange("p (h c) -> p h c", h=PH)
        ci = cut(PH * TOPK).rearrange("p (h c) -> p h c", h=PH)
        cab = cut(2 * PH * TOPK).rearrange("p (s h c) -> p s h c", s=2, h=PH)
        cabf = cut(2 * PH * TOPK).rearrange("p (s h c) -> p s h c", s=2, h=PH)
        hot = cut(PH * TOPK * TOPK).rearrange("p (h k a) -> p h k a", h=PH, k=TOPK)
        sel = cut(3 * 3 * 128).rearrange("p (t s c) -> p t s c", t=3, s=3)
        hsum = cut(2 * PH).rearrange("p (s h) -> p s h", s=2)
        hotB2 = big[:, BIG:BIG + 512].rearrange("p (a b) -> p a b", a=4)
        yacc = big[:, 0:KD * SEQ].rearrange("p (k t) -> p k t", k=KD)
        v_t = [stream[:, 4096:5120], big[:, BIG + 512:BIG + 1536]]
        act_t = [big[:, BIG + i * SEQ:BIG + (i + 1) * SEQ] for i in range(2)]
        zeros = big[:, BIG:BIG + 512]
        scp = hotB2.rearrange("p a b -> p (a b)")[:, 0:NK]
        tpk = hotB2.rearrange("p a b -> p (a b)")[:, 128:160].rearrange("p (s k) -> p s k", s=2)
        tpi = hotB2.rearrange("p a b -> p (a b)")[:, 160:176]
        tq = hotB2.rearrange("p a b -> p (a b)")[0:64, 176:208].rearrange("p (s k) -> p s k", s=2)
        pcs = hotB2.rearrange("p a b -> p (a b)")[0:64, 208:224]
        pci = hotB2.rearrange("p a b -> p (a b)")[0:64, 224:240]
        pab = hotB2.rearrange("p a b -> p (a b)")[0:64, 240:272].rearrange("p (s k) -> p s k", s=2)
        pabf = hotB2.rearrange("p a b -> p (a b)")[0:64, 272:304].rearrange("p (s k) -> p s k", s=2)
        psel = hotB2.rearrange("p a b -> p (a b)")[0:64, 304:352].rearrange("p (s k) -> p s k", s=3)
        psum2 = hotB2.rearrange("p a b -> p (a b)")[0:64, 352:354]
        pcand = cut(256)[0:64].rearrange("p (a b) -> p a b", a=TOPK)
        phot = cut(256)[0:64].rearrange("p (a b) -> p a b", a=TOPK)
        fin = stream[:, 0:3 * D].rearrange("p (t c) -> p t c", t=3)
        gfin = stream[:, 4096:4096 + D]

        ps = ctx.enter_context(nc.psum_tensor("ps", [P, 8, 512], F32))

        product = sem("product")
        moved_v = sem("moved_by_vector")
        moved_a = sem("moved_by_scalar")
        gm_ld = sem("mixer_gain_loaded")
        small_ld = sem("small_loads")
        w_ld = [sem("weights_even"), sem("weights_odd")]
        uq_ld = sem("wuq_loaded")
        conv_ld = sem("conv_loaded")
        kw_ld = sem("window_keys_loaded")
        vw_ld = [sem("window_values_even"), sem("window_values_odd")]
        vw_used = sem("window_values_used")
        sk_ld = sem("subkeys_loaded")
        vstep = sem("vector_step")
        pad_set = sem("pads_set")
        sq_ready = sem("squares_ready")
        std_ready = sem("std_ready")
        hn_ready = sem("normed_ready")
        lat_ready = sem("latents_ready")
        qk_ready = sem("window_qk_ready")
        q_ready = sem("q_rotated")
        sig_ready = sem("sigmoid_ready")
        g_ready = sem("glu_ready")
        nmx_ready = sem("negmax_ready")
        exp_ready = sem("exp_ready")
        cnt_ready = sem("counted_ready")
        y_ready = sem("conv_ready")
        ln_ready = sem("conv_normed")
        smx_ready = sem("sample_max_ready")
        sdg_ready = sem("sample_diag_ready")
        sexp_ready = sem("sample_exp_ready")
        sden_ready = sem("sample_den_ready")
        stored = sem("stores_done")
        cand_max = sem("gate_logits_ready")
        gexp = sem("gate_exp_ready")
        sel_ready = sem("selection_ready")
        scp_ld = sem("sample_scores_spread")
        p1_ready = sem("sample_tops_ready")
        tq_ld = sem("sample_tops_paired")
        p2_ready = sem("sample_gates_ready")
        psel_ld = sem("sample_selection_gathered")
        e_ready = sem("expert_rows_ready")
        coef_ready = sem("sample_weights_ready")
        hotA_ready = sem("onehot_a_ready")
        hotB_ready = sem("onehot_b_ready")
        dist_ready = sem("onehot_distance")
        hotC_ready = sem("onehot_b_by_scalar")
        g_prod = sem("gate_product")
        g_moved = sem("gate_moved")
        g_done = sem("gates_done")
        acc_zero = sem("acc_zero")
        u_ld = [sem(f"u_loaded{i}") for i in range(UN)]
        v_ld = [sem(f"v_loaded{i}") for i in range(2)]
        u_free = [sem(f"u_free{i}") for i in range(UN)]
        v_free = [sem(f"v_free{i}") for i in range(2)]
        h_high = sem("tokens_high")
        h_low = sem("tokens_low")
        half_used = sem("uT_half_used")
        v_high = sem("v_high")
        v_low = sem("v_low")
        v_used = sem("v_used")
        w_full = sem("weights_full")
        w_high = sem("weights_high")
        turned = sem("u_turned")
        acc_done = sem("acc_done")
        uT_low = sem("uT_low")
        uT_high = sem("uT_high")
        z_prod = sem("expert_inputs")
        gelu_done = sem("gelu_done")
        w_ready = sem("expert_weights")
        y_moved = sem("peer_out_moved")
        copied = sem("window_copied")
        ended = sem("engines_at_layer_end")
        f_gld = ctx.enter_context(nc.semaphore("final_gain_loaded"))
        store = ctx.enter_context(nc.semaphore("store"))
        past_ld = ctx.enter_context(nc.semaphore("past_loaded"))
        erow_u_ld = [ctx.enter_context(nc.semaphore(f"u_rows_gathered{b}")) for b in range(NB)]
        erow_v_ld = ctx.enter_context(nc.semaphore("v_rows_gathered"))
        rows_ready = ctx.enter_context(nc.semaphore("past_rows_ready"))
        past_asked = ctx.enter_context(nc.semaphore("past_asked"))
        consts_ld = ctx.enter_context(nc.semaphore("consts_loaded"))
        ones_set = ctx.enter_context(nc.semaphore("ones_set"))
        go = [ctx.enter_context(nc.semaphore(f"next_layer_{e}")) for e in ("pe", "act", "dve", "pool")]
        f_sq, f_std, f_out, f_step, f_y = (ctx.enter_context(nc.semaphore(n)) for n in
                                     ("final_squares", "final_std", "final_stored", "final_step", "final_y"))
        moved = {"V": moved_v, "A": moved_a}
        def wait_moved(eng, *name):
            who, n = READ[name]
            eng.wait_ge(moved[who], n)

        def wait_count(eng, s, n):
            if not (isinstance(n, int) and n <= 0):
                eng.wait_ge(s, n)

        def bank(*name):
            return ps[:, NUM[name] % 8]

        def arrive(eng, *name):
            eng.wait_ge(product, NUM[name] + 1)
            return bank(*name)

        def layer_end(eng, i):
            eng.nop().then_inc(ended, 1)
            eng.wait_ge(go[i], 1)
            eng.sem_clear(go[i])

        def L(name, l):
            a = A[name][bass.ds(l, 1)]
            names = " ".join("abcdef"[:len(a.shape) - 1])
            return a.rearrange(f"o {names} -> (o {names.split(' ')[0]}) {' '.join(names.split(' ')[1:])}")

        def O(ap, l):
            a = ap[bass.ds(l, 1)]
            names = "abcdef"[:len(a.shape) - 1]
            return a.rearrange(f"o {' '.join(names)} -> (o {names[0]}) {' '.join(names[1:])}")

        WCH = ([("w_in", c0, n) for c0, n in ZCH] + [("w_out", 512 * c, 512) for c in range(2)]
               + [("peer_wq", 512 * c, 512) for c in range(4)])

        W_LAST = [NUM["z", c, 2] + 1 for c in range(5)] + [NUM["xo", c, 2] + 1 for c in range(2)]
        W_LAST += [NUM["pq", 4 * c + 3] + 1 for c in range(4)]

        def wview(n):
            k = WCH[n][2]
            return wslot[n % 2][:, 0:KD * k].rearrange("p (k c) -> p k c", k=KD)

        block = ctx.enter_context(nc.Block())

        @block.sync
        def _(sp):
            sp.dma_start(ident[:, :], C["ident"]).then_inc(consts_ld, 16)
            sp.dma_start(iota[:, :], C["iota"]).then_inc(consts_ld, 16)
            sp.dma_start(rope[:, :, :], C["rope"]).then_inc(consts_ld, 16)
            sp.dma_start(diag[:, :], C["diag"]).then_inc(consts_ld, 16)
            sp.dma_start(sub[:, :], C["sub"]).then_inc(consts_ld, 16)
            with nc.allow_non_contiguous_dma(reason="page numbers to the partitions that load them, 4 KB once"):
                for g in range(P // 8):
                    sp.dma_start(pages[8 * g:8 * g + 8, :],
                                 A["page_table"].rearrange("b g -> g b")[g:g + 1, :].to_broadcast([8, NB])).then_inc(consts_ld, 16)
            for t, (t0, n) in enumerate(TOK[:2]):
                sp.dma_start(X[:, t, :], A["x_prompt"][0, t0:t0 + n, :]).then_inc(consts_ld, 16)
            sp.dma_start(X[0:NB, 2, :], A["x_sample"].rearrange("b s d -> (b s) d")).then_inc(consts_ld, 16)
            sp.wait_ge(consts_ld, 16 * 24)

            with sp.Fori(0, DEPTH) as l:
                def load_w(n):
                    if n >= 2:
                        sp.wait_ge(product, W_LAST[n - 2])
                    name, c0, k = WCH[n]
                    src = L(name, l).rearrange("(k p) c -> p k c", p=P)[:, :, c0:c0 + k]
                    sp.dma_start(wview(n), src).then_inc(w_ld[n % 2], 16)

                def window_rows(name, b, d):
                    lo = PAST - 128 * d
                    rows = L(name, l)[b, lo:PAST, :, :]
                    return rows.rearrange("(k r) h c -> k r (h c)", r=d)[:, 0, :]

                with nc.allow_non_contiguous_dma(reason="per-channel gains, a few KB"):
                    sp.dma_start(g_mix, L("norm_mix", l).rearrange("(k p) -> p k", p=P)).then_inc(gm_ld, 16)
                    load_w(0)
                    sp.dma_start(g_ffn, L("norm_ffn", l).rearrange("(k p) -> p k", p=P)).then_inc(small_ld, 16)
                    sp.dma_start(g_q, L("q_norm", l).rearrange("(k p) -> p k", p=P)).then_inc(small_ld, 16)
                    sp.dma_start(g_cb, L("conv_b", l).rearrange("(k p) -> p k", p=P)).then_inc(small_ld, 16)
                    sp.dma_start(g_lg, L("conv_ln_g", l).rearrange("(k p) -> p k", p=P)).then_inc(small_ld, 16)
                    sp.dma_start(g_lb, L("conv_ln_b", l).rearrange("(k p) -> p k", p=P)).then_inc(small_ld, 16)
                sp.dma_start(kvg, A["kv_norm"][bass.ds(l, 1)].to_broadcast([P, LAT])).then_inc(small_ld, 16)
                for i, m in enumerate((cnt, cbias, mbias)):
                    sp.dma_start(m, C["masks"][:, i * 384:(i + 1) * 384]).then_inc(small_ld, 16)
                load_w(1)
                sp.dma_start(wuq, L("w_uq", l).rearrange("(k p) c -> p k c", p=P)).then_inc(uq_ld, 16)
                wukv_src = L("w_ukv", l).rearrange("c (h a x) -> c a h x", h=NH, a=2)
                sp.dma_start(wuk.rearrange("p (h x) -> p h x", h=NH), wukv_src[:, 0]).then_inc(uq_ld, 16)
                sp.dma_start(wuv.rearrange("p (h x) -> p h x", h=NH), wukv_src[:, 1]).then_inc(uq_ld, 16)
                sp.dma_start(cwr, L("conv_w", l)).then_inc(conv_ld, 16)
                sp.dma_start(scr, L("state_conv", l).rearrange("(s b) j c -> (b j) s c", s=2)).then_inc(conv_ld, 16)
                for n in range(2, 7):
                    load_w(n)

                def load_kw(b):
                    if b >= 1:
                        wait_moved(sp, "qbc", b - 1)
                    for i, d in enumerate(DIL):
                        sp.dma_start(kw[:, i, :], window_rows("state_win_k", b, d)).then_inc(kw_ld, 16)

                def load_vw(b):
                    if b >= 2:
                        sp.wait_ge(vw_used, b - 1)
                    for i, d in enumerate(DIL):
                        sp.dma_start(vw[:, b % 2, i, :], window_rows("state_win_v", b, d)).then_inc(vw_ld[b % 2], 16)

                wait_moved(sp, "qrS")
                load_kw(0)
                sp.wait_ge(q_ready, 1)
                load_vw(0)
                load_vw(1)
                for b in range(1, NB):
                    load_kw(b)
                for b in range(2, NB):
                    load_vw(b)
                sp.wait_ge(stored, 1)
                sp.wait_ge(product, W_LAST[6])
                for n in range(NSUB):
                    sp.dma_start(sk[:, n, :], L("peer_subkeys", l)[n // 2, n % 2]).then_inc(sk_ld, 16)
                for n in range(7, 11):
                    load_w(n)
                for n in range(NSUB):
                    h, side = n // 2, n % 2
                    if n % 4 == 0:
                        wait_moved(sp, "s", 2, n // 4)
                    sp.dma_start(scp[64 * side + NB * h:64 * side + NB * h + NB, :], sc[0:NB, 2, n, :]).then_inc(scp_ld, 16)
                sp.wait_ge(p1_ready, 1)
                sp.dma_start(tq, tpk[64:128, :, :]).then_inc(tq_ld, 16)
                sp.wait_ge(p2_ready, 1)
                for h in range(PH):
                    sp.dma_start(sel[0:NB, 2, :, TOPK * h:TOPK * h + TOPK], psel[NB * h:NB * h + NB, :, :]).then_inc(psel_ld, 16)
                sp.wait_ge(product, NUM["gy", 1] + 1)
                u_l = L("peer_u", l).rearrange("(i j) d -> i j d", j=NK)
                v_l = L("peer_v", l).rearrange("(i j) d -> i j d", j=NK)
                for k in range(2):
                    sp.nop().then_inc(v_free[k], 1)

                def load_u(k, j):
                    sp.dma_start(u_t[k], u_l[:, bass.ds(j, 1), :].rearrange("i o d -> i (o d)")).then_inc(u_ld[k], 16)

                for k in range(UN):
                    load_u(k, k)
                sp.wait_ge(hotA_ready, 1)

                def stream_tiles(b, last):
                    for half, (src, dst) in enumerate((("state_win_k", wk_s), ("state_win_v", wv_s))):
                        s_ap = L(src, l)[bass.ds(b, 1), 1:PAST].rearrange("o r h c -> (o r) (h c)")
                        d_ap = O(dst, l)[bass.ds(b, 1), 0:PAST - 1].rearrange("o r h c -> (o r) (h c)")
                        for m in range(2):
                            for k in range(UN):
                                j = b * (4 * UN) + (half * 2 * UN + m * UN + k)
                                sp.wait_ge(v_free[k % 2], 1)
                                sp.sem_clear(v_free[k % 2])
                                sp.dma_start(v_t[k % 2], v_l[:, bass.ds(j, 1), :].rearrange("i o d -> i (o d)")).then_inc(v_ld[k % 2], 16)
                                if not (last and half == 1 and m == 1):
                                    sp.wait_ge(u_free[k], 1)
                                    sp.sem_clear(u_free[k])
                                    load_u(k, j + UN)
                            if m == 0:
                                sp.dma_start(d_ap, s_ap).then_inc(copied, 16)

                with sp.Fori(0, NB - 1) as b:
                    stream_tiles(b, False)
                stream_tiles(NB - 1, True)
                sp.wait_ge(copied, 16 * 2 * NB)
                sp.wait_ge(ended, 4)
                for s in layer_sems:
                    sp.sem_clear(s)
                for s in go:
                    sp.nop().then_inc(s, 1)
            sp.dma_start(gfin, A["norm_final"].rearrange("(o d) -> o d", o=1).to_broadcast([P, D])).then_inc(f_gld, 16)
            for t, (t0, n) in enumerate(TOK):
                sp.wait_ge(f_y, t + 1)
                dst = y_p[0, t0:t0 + n, :] if t < 2 else y_s.rearrange("b s d -> (b s) d")
                sp.dma_start(dst, fin[0:n, t, :]).then_inc(f_out, 16)
            sp.wait_ge(f_out, 16 * 3)

        @block.gpsimd
        def _(pool):
            pool.memset(ones[:, :], 1.0)
            pool.memset(stat[:, :], 1.0).then_inc(ones_set, 1)
            with pool.Fori(0, DEPTH) as l:
                pool.wait_ge(rows_ready, l + 1)
                pool.nop().then_inc(past_asked, 1)
                pool.memset(z[:, 2, :], 0.0).then_inc(pad_set, 1)
                pool.memset(gT[:, :, 0:CW - 1], 0.0)
                pool.memset(qrB.rearrange("p b i h -> p (b i h)"), 0.0).then_inc(pad_set, 1)
                n_st = [0]

                def load_past(half):
                    for b in range(4):
                        row = bass.IndirectOffsetOnAxis(ap=pidx[:, 4 * half + b:4 * half + b + 1].bitcast(U32), axis=0)
                        for dst, name in ((past, "cache_kv_latent"), (pastr, "cache_k_rope")):
                            pool.indirect_dma_start(dst[:, b, :, :].rearrange("p g c -> p (g c)"), None,
                                                    A[name].rearrange("l n (s t) c -> (l n s) (t c)", s=8), row).then_inc(past_ld, 16)

                load_past(0)

                def put(dst, src):
                    pool.dma_start(dst, src).then_inc(store, 16)
                    n_st[0] += 16

                def put_tokens(prompt, sample, col, n, rows=2):
                    for t in range(2):
                        put(O(prompt, l)[0, 128 * t:128 * t + 128], z[:, t, col:col + n])
                    put(sample, z[0:NB, 2, col:col + n])

                pool.wait_ge(lat_ready, 2)
                for t in range(2):
                    put(O(lat_p, l)[0, 128 * t:128 * t + 128, :], z[:, t, CKV:CKV + LAT])
                    put(O(kr_p, l)[0, 128 * t:128 * t + 128, :], z[:, t, KR:KR + ROPE])
                put(O(lat_s, l)[:, 0, :], z[0:NB, 2, CKV:CKV + LAT])
                put(O(kr_s, l)[:, 0, :], z[0:NB, 2, KR:KR + ROPE])
                pool.wait_ge(qk_ready, 1)
                for t in range(2):
                    put(O(wk_p, l)[0, 128 * t:128 * t + 128].rearrange("r h c -> r (h c)"), z[:, t, KB:KB + 384])
                put(O(wk_s, l)[:, PAST - 1].rearrange("b h c -> b (h c)"), z[0:NB, 2, KB:KB + 384])
                wait_moved(pool, "z", 3, 2)
                for t in range(2):
                    put(O(wv_p, l)[0, 128 * t:128 * t + 128].rearrange("r h c -> r (h c)"), z[:, t, VB:VB + 384])
                put(O(wv_s, l)[:, PAST - 1].rearrange("b h c -> b (h c)"), z[0:NB, 2, VB:VB + 384])
                pool.wait_ge(g_ready, 1)
                put(O(cv_p, l)[0], z[128 - (CW - 1):128, 1, GA:GA + CC])
                put(O(cv_s, l)[:, CW - 2, :], z[0:NB, 2, GA:GA + CC])
                put(O(cv_s, l)[:, 0:CW - 2, :], L("state_conv", l)[:, 1:CW - 1, :])
                pool.wait_ge(store, l * n_st[0] + n_st[0])
                pool.nop().then_inc(stored, 1)
                pool.wait_ge(product, NUM["ol", 0] + 1)
                load_past(1)
                pool.wait_ge(e_ready, 1)
                for name in ("peer_u", "peer_v"):
                    for b in range(NB):
                        if name == "peer_v":
                            pool.wait_ge(product, NUM["gu", b, 1] + 1)
                        row = bass.IndirectOffsetOnAxis(ap=eidx[:, b:b + 1].bitcast(U32), axis=0)
                        pool.indirect_dma_start(gath[b], None, A[name].rearrange("l e d -> (l e) d"), row).then_inc(erow_u_ld[b] if name == "peer_u" else erow_v_ld, 16)
                layer_end(pool, 3)

        @block.tensor
        def _(pe):
            def begin(*name):
                n = NUM[name]
                if n >= 8:
                    wait_moved(pe, *JOBS[n - 8][0])
                return ps[:, n % 8]

            def turn(*name, parts):
                o = begin(*name)
                for src, rows, cols, c0 in parts:
                    mm = pe.transpose(o[0:cols, c0:c0 + rows], src, ident[0:rows, 0:rows])
                mm.then_inc(product, 1)

            def dense(name, parts, n_out, cols):
                o = begin(*name)
                for i, (lhs, rhs) in enumerate(parts):
                    mm = pe.matmul(o[0:n_out, 0:cols], lhs, rhs, start=(i == 0), stop=(i == len(parts) - 1))
                mm.then_inc(product, 1)

            def tokens(src, c0, n=128):
                return [(src[0:m, t, c0:c0 + n], m, n, t0) for t, (t0, m) in enumerate(TOK)]

            pe.wait_ge(consts_ld, 16 * 24)
            pe.wait_ge(ones_set, 1)
            with pe.Fori(0, DEPTH) as l:
                pe.wait_ge(hn_ready, 3)
                for k in range(KD):
                    turn("hT", k, parts=tokens(hn, k * 128))
                wait_moved(pe, "hT", KD - 2)
                wait_moved(pe, "hT", KD - 1)
                for c, (c0, n) in enumerate(ZCH):
                    pe.wait_ge(w_ld[c % 2], 16 * (c // 2 + 1))
                    for t, (t0, m) in enumerate(TOK):
                        dense(("z", c, t), [(hT[:, k, t0:t0 + m], wview(c)[:, k, :]) for k in range(KD)], m, n)
                pe.wait_ge(lat_ready, 1)
                for k in range(2):
                    turn("cqT", k, parts=tokens(z, CQ + 128 * k))
                pe.wait_ge(lat_ready, 3)
                turn("ckvT", parts=tokens(z, CKV))
                turn("krT", parts=[(krr[0:m, t, :, :].rearrange("p r c -> p (r c)"), m, 128, t0) for t, (t0, m) in enumerate(TOK)])
                pe.wait_ge(uq_ld, 48)
                turn("ukT", parts=[(wuk[:, 128 * g:128 * g + 128], 128, 128, g * 128) for g in range(HP)])
                wait_moved(pe, "cqT", 1)
                for t, (t0, m) in enumerate(TOK):
                    for n in range(2):
                        dense(("q", t, n), [(cqT[:, k, t0:t0 + m], wuq[:, k, n * 288:(n + 1) * 288]) for k in range(2)], m, 288)
                pe.wait_ge(qk_ready, 1)
                for g in range(HP):
                    turn("qbT", g, parts=tokens(z, QB + 128 * g))
                for g in range(HP):
                    turn("kbT", g, parts=tokens(z, KB + 128 * g))
                pe.wait_ge(q_ready, 1)
                for g in range(HP):
                    turn("qnT", g, parts=tokens(q, 128 * g))
                for g, hs in enumerate((4, 2)):
                    turn("qrT", g, parts=tokens(q, NH * NOPE + 128 * g, 32 * hs))
                turn("qrS", parts=[(qrr[0:NB, h, :, :].rearrange("p r c -> p (r c)"), NB, 128, h * NB)
                                   for h in range(NH)])
                wait_moved(pe, "qnT", HP - 1)
                for h in range(NH):
                    r0 = 64 * (h % 2)
                    dense(("qlT", h), [(ukT[r0:r0 + 64, h // 2, :], qnT[r0:r0 + 64, h // 2, :])], 128, T)
                for t in range(2):
                    dense(("va", t), [(ckvT[:, 128 * t:128 * t + 128], wuv)], 128, 384)
                pe.wait_ge(conv_ld, 32)
                turn("cw", parts=[(cwr[:, 128 * c:128 * c + 128], CW, 128, CW * c) for c in range(2)])
                for c in range(2):
                    turn("sc", c, parts=[(scr[:, s, 128 * c:128 * c + 128], 120, 128, 120 * s) for s in range(2)])
                pe.wait_ge(g_ready, 1)
                for c in range(2):
                    turn("gT", c, parts=tokens(z, GA + 128 * c))
                wait_moved(pe, "qlT", NH - 1)
                wait_moved(pe, "va", 1)

                def scores(u):
                    o = begin("S", u)
                    h = u % NH
                    for i, c0 in ((0, 0), (1, 128)):
                        K = 128 * (i + 1)
                        qs = slice(128 * i, 128 * i + 128)
                        if u < NH:
                            r0 = 32 * (h % 4)
                            pe.matmul(o[:, c0:c0 + K], qlT[:, h, qs], ckvT[:, 0:K], start=True, stop=False)
                            mm = pe.matmul(o[:, c0:c0 + K], qrT[r0:r0 + 32, h // 4, qs], krT[r0:r0 + 32, 0:K], start=False, stop=True)
                        else:
                            r0 = 64 * (h % 2)
                            mm = pe.matmul(o[:, c0:c0 + K], qbT[r0:r0 + 64, h // 2, qs], kbT[r0:r0 + 64, h // 2, 0:K], start=True, stop=True)
                    mm.then_inc(product, 1)

                def turn_probs(u):
                    if u < NH:
                        pe.wait_ge(exp_ready, u + 1)
                    else:
                        pe.wait_ge(cnt_ready, u - NH + 1)
                    turn("PT", u, parts=[(prob[:, u % 2, 128 * i:128 * i + 128], 128, 128, 128 * i) for i in range(3)])

                def mix_values(u):
                    wait_moved(pe, "PT", u)
                    o = begin("O", u)
                    v = [va[:, t, 64 * u:64 * u + 64] if u < NH else z[:, t, VB + 64 * (u - NH):VB + 64 * (u - NH) + 64] for t in range(2)]
                    pt = probT[:, u % 2, :]
                    pe.matmul(o[:, 0:64], pt[:, 0:128], v[0], start=True, stop=True)
                    pe.matmul(o[:, 64:128], pt[:, 128:256], v[0], start=True, stop=False)
                    pe.matmul(o[:, 64:128], pt[:, 256:384], v[1], start=False, stop=True).then_inc(product, 1)

                for s in range(2 * NH + 2):
                    if s < 2 * NH:
                        scores(s)
                    if 1 <= s <= 2 * NH:
                        turn_probs(s - 1)
                    if s >= 2:
                        mix_values(s - 2)
                wait_moved(pe, "O", 2 * NH - 1)
                for g in range(2 * HP):
                    turn("mT", g, parts=[(oAB[:, t, 128 * g:128 * g + 128], 128, 128, 128 * t) for t in range(2)])
                pe.wait_ge(y_ready, 1)
                for t, (t0, m) in enumerate(TOK):
                    turn("yt", t, parts=[(yT[:, c, t0:t0 + m], 128, m, 128 * c) for c in range(2)])
                pe.wait_ge(ln_ready, 3)
                for c in range(2):
                    turn("ycT", c, parts=tokens(yt, 128 * c))

                def score_past(b):
                    wait_moved(pe, "cT", b, 3)
                    wait_moved(pe, "rT", b)
                    o = begin("ST", b)
                    for g in range(NPG // 4):
                        pe.matmul(o[:, 24 * g:24 * g + 24], rT[:, b % 2, g, :], qrB[:, b, :, :], start=True, stop=False, skip_group_check=True)
                        for i in range(4 * g, 4 * g + 4):
                            mm = pe.matmul(o[:, NH * i:NH * i + NH], cT[:, b % 2, 128 * i:128 * i + 128], qlT[:, :, SEQ + b],
                                           start=False, stop=True, skip_group_check=True)
                    mm.then_inc(product, 1)

                def past_half(half):
                    pe.wait_ge(past_ld, l * (16 * 2 * NB) + 16 * NB * (half + 1))
                    for b in range(4 * half, 4 * half + 5):
                        if b < 4 * half + 4:
                            for g in range(4):
                                turn("cT", b, g, parts=[(past[:, b % 4, 4 * g + i, :], 128, 128, 128 * i) for i in range(4)])
                            turn("rT", b, parts=[(pastr[:, b % 4, 4 * g:4 * g + 4, :].rearrange("p g c -> p (g c)"), 128, 128, 128 * g) for g in range(4)])
                        if b > 4 * half:
                            score_past(b - 1)
                        if b < 4:
                            for i in (2 * b, 2 * b + 1):
                                dense(("qbc", i), [(ident[0:NB, i:i + 1].to_broadcast([NB, P]), z[0:NB, 2, QB:QB + 384])], 128, 384)

                def maxima(*group):
                    for n, c, order in group:
                        pe.wait_ge(smx_ready, order)
                        turn("mx", n, parts=[(smx[:, n, 0:c], 128, c, 0)])
                    for n, c, order in group:
                        pe.wait_ge(sdg_ready, order)
                        dense(("mb", n), [(ones[0:c, :], sdg[0:c, n, 0:c])], 128, c)
                    for n, c, order in group:
                        pe.wait_ge(sden_ready, order)
                        dense(("dn", n), [(ones[:, :], sden[:, n, 0:c])], 128, c)

                def latent_mix(half):
                    o = begin("ol", half)
                    for b in range(4):
                        pe.matmul(o[0:NH, 128 * b:128 * b + 128], STm[0:NB, b, NPG, :], z[0:NB, 2, CKV:CKV + LAT], start=True, stop=False,
                                  skip_group_check=True)
                        for g in range(NPG):
                            mm = pe.matmul(o[0:NH, 128 * b:128 * b + 128], STm[:, b, g, :], past[:, b, g, :], start=False,
                                           stop=(g == NPG - 1), skip_group_check=True)
                    mm.then_inc(product, 1)

                def turn_mix(half):
                    wait_moved(pe, "ol", half)
                    turn("olT", half, parts=[(olr[:, 128 * b:128 * b + 128], NH, 128, NH * b) for b in range(4)])

                o = begin("ext")
                pe.matmul(o[0:NB, 0:48], ckvT[:, SEQ:T], qlT[:, :, SEQ:T], start=True, stop=False)
                pe.matmul(o[0:NB, 0:48], krT[0:32, SEQ:T], qrS[0:32, :, :], start=False, stop=True).then_inc(product, 1)
                past_half(0)
                maxima((0, 24, 1), (2, 48, 2))
                latent_mix(0)
                o = begin("ow")
                for h in range(NH):
                    r0 = 64 * (h % 2)
                    pe.matmul(o[r0:r0 + 64, NB * (h // 2):NB * (h // 2) + NB], z[0:NB, 2, VB + 64 * h:VB + 64 * h + 64], STw[0:NB, :, 3, h],
                              start=(h < 2), stop=False, skip_group_check=True)
                for b in range(NB):
                    pe.wait_ge(vw_ld[b % 2], 48 * (b // 2 + 1))
                    for d in range(3):
                        for h in range(NH):
                            r0 = 64 * (h % 2)
                            c0 = NB * (h // 2) + b
                            mm = pe.matmul(o[r0:r0 + 64, c0:c0 + 1], vw[:, b % 2, d, 64 * h:64 * h + 64], STw[:, b, d, h:h + 1],
                                           start=False, stop=(d == 2), skip_group_check=True)
                    mm.then_inc(vw_used if b < NB - 1 else product, 1)
                turn_mix(0)
                past_half(1)
                maxima((1, 24, 3))
                latent_mix(1)
                turn_mix(1)
                wait_moved(pe, "olT", 1)
                o = begin("os")
                for h in range(NH):
                    r0 = 64 * (h % 2)
                    mm = pe.matmul(o[r0:r0 + 64, NB * (h // 2):NB * (h // 2) + NB], wuv[:, HD * h:HD * h + HD], olT[:, :, h],
                                   start=True, stop=True, skip_group_check=True)
                mm.then_inc(product, 1)
                wait_moved(pe, "mT", 5)
                wait_moved(pe, "os")
                for c in range(2):
                    pe.wait_ge(w_ld[(5 + c) % 2], 16 * ((5 + c) // 2 + 1))
                    for t, (t0, m) in enumerate(TOK):
                        dense(("xo", c, t), [(mixT[:, k, t0:t0 + m], wview(5 + c)[:, k, :]) for k in range(KD)], m, 512)
                pe.wait_ge(hn_ready, 6)
                for k in range(KD):
                    turn("fT", k, parts=tokens(hf, k * 128))
                pe.wait_ge(sk_ld, 16 * NSUB)
                for g in range(4):
                    turn("skT", g, parts=[(sk[:, 4 * g + i, :], 128, 128, 128 * i) for i in range(4)])
                wait_moved(pe, "fT", KD - 2)
                wait_moved(pe, "fT", KD - 1)
                for g in range(5):
                    if g < 4:
                        w = 7 + g
                        pe.wait_ge(w_ld[w % 2], 16 * (w // 2 + 1))
                        for n in range(4 * g, 4 * g + 4):
                            dense(("pq", n), [(wview(w)[:, k, 128 * (n % 4):128 * (n % 4) + 128], hT[:, k, :]) for k in range(KD)], 128, T)
                    if g:
                        wait_moved(pe, "pq", 4 * g - 1)
                        for t in (2, 0, 1):
                            t0, m = TOK[t]
                            o = begin("s", t, g - 1)
                            for i in range(4):
                                n = 4 * g - 4 + i
                                mm = pe.matmul(o[0:m, 128 * i:128 * i + 128], pqT[:, n, t0:t0 + m], skT[:, n, :], start=True, stop=True)
                            mm.then_inc(product, 1)

                def slots(t):
                    m = TOK[t][1]
                    turn("slot", t, parts=[(sel[0:m, t, s, :], m, 128, 128 * s) for s in range(3)])

                pe.wait_ge(psel_ld, 16 * PH)
                slots(2)
                for b in range(NB + 1):
                    if b < NB:
                        pe.wait_ge(erow_u_ld[b], l * 16 + 16)
                        for half in range(2):
                            turn("gu", b, half, parts=[(gath[b][:, 512 * half + 128 * i:512 * half + 128 * i + 128], 128, 128, 128 * i) for i in range(4)])
                    if b:
                        wait_moved(pe, "gu", b - 1, 1)
                        dense(("gz", b - 1), [(uTs[(b - 1) % 2][:, 128 * c:128 * c + 128], hT[:, c, SEQ + b - 1:SEQ + b]) for c in range(KD)], 128, 1)
                pe.wait_ge(sel_ready, 1)
                slots(0)
                pe.wait_ge(coef_ready, NB)
                for half in range(2):
                    if half == 0:
                        pe.wait_ge(erow_v_ld, l * (16 * NB) + 16 * NB)
                    dense(("gy", half), [(coef[:, b, :], gath[b][:, 512 * half:512 * half + 512]) for b in range(NB)], NB, 512)
                pe.wait_ge(sel_ready, 2)
                slots(1)
                wait_moved(pe, "slot", 1)
                wait_moved(pe, "gy", 1)
                for _ in range(2):
                    pe.nop().then_inc(g_prod, 1)
                with pe.Fori(0, SEQ // GT) as it:
                    for g in range(2):
                        pe.wait_ge(hotA_ready, it * 2 + (g + 1))
                        pe.wait_ge(hotB_ready, it * 2 + (g + 1))
                        pe.wait_ge(hotC_ready, it * 2 + (g + 1))
                        pe.wait_ge(g_moved, it * 2 + (g + 1))
                        hb = hotB if g == 0 else hotB2
                        for k in range(4):
                            mm = pe.matmul(ps[:, 6 + g, 128 * k:128 * k + 128], hotA[:, 4 * g + k, :], hb[:, k, :], start=True, stop=True)
                        mm.then_inc(g_prod, 1)
                pe.wait_ge(g_moved, 2 * (SEQ // GT) + 2)
                pe.wait_ge(acc_zero, 1)
                for n in range(4):
                    pe.matmul(ps[:, n, :], zeros[:, 0:128], zeros[:, 0:512], start=True, stop=False, skip_group_check=True)
                pe.wait_ge(h_low, 1)

                def expert_steps(it, ks, first=False, last=False):
                    for k in ks:
                        if not last:
                            pe.wait_ge(u_ld[k], it * 16 + 32)
                            for half in range(2):
                                wait_count(pe, uT_low, it * 8 + (7 + 2 * k + half))
                                for i in range(4):
                                    c = 4 * half + i
                                    mm = pe.transpose(ps[:, 6 + half, 128 * i:128 * i + 128], u_t[k][:, 128 * c:128 * c + 128], ident[:, :])
                                mm.then_inc(turned, 1)
                        if (not first or k >= 1) and (not last or k == 0):
                            wait_count(pe, gelu_done, it * 4 + (2 + k))
                            z_o = ps[:, 4 + (k + 1) % 2, 0:SEQ]
                            for half in range(2):
                                pe.wait_ge(uT_low, it * 8 + (7 + 2 * k + half))
                                for c in range(4 * half, 4 * half + 4):
                                    for n, (a, b) in enumerate(((0, 0), (0, 1), (1, 0))):
                                        mm = pe.matmul(z_o, uT[a][:, 128 * c:128 * c + 128], hp[b][:, c, :],
                                                       start=(c == 0 and n == 0), stop=(c == KD - 1 and n == 2))
                                        if c == 0 and n == 0:
                                            mm.then_inc(u_free[(k - 1) % UN], 1)
                                mm.then_inc(half_used if half == 0 else z_prod, 1)
                        if not first or k >= 2:
                            pe.wait_ge(w_ready, it * 4 + (3 + k))
                            for half in range(2):
                                pe.wait_ge(v_low, it * 8 + (5 + 2 * k + half))
                                for c in range(4 * half, 4 * half + 4):
                                    for n, (a, b) in enumerate(((0, 0), (0, 1), (1, 0))):
                                        mm = pe.matmul(ps[:, c // 2, 256 * (c % 2):256 * (c % 2) + 256], vp[a][:, 128 * c:128 * c + 128],
                                                       wp[k % 2][b], start=False, stop=False, skip_group_check=True)
                                        if c == 4 and n == 0:
                                            mm.then_inc(v_free[k % 2], 1)
                                mm.then_inc(v_used, 1)

                expert_steps(-1, range(UN), first=True)
                with pe.Fori(0, LOOPS - 1) as it:
                    expert_steps(it, range(UN))
                expert_steps(LOOPS - 1, range(2), last=True)
                pe.transpose(ps[:, 5, 0:128], ident[:, :], ident[:, :]).then_inc(acc_done, 1)
                pe.wait_ge(y_moved, 1)
                for c in range(2):
                    for t, (t0, m) in enumerate(TOK[:2]):
                        turn("xT", c, t, parts=[(yacc[:, 4 * c + i, t0:t0 + m], 128, m, 128 * i) for i in range(4)])
                pe.wait_ge(product, len(JOBS))
                layer_end(pe, 0)

        @block.scalar
        def _(act):
            def read(*name):
                who, n = READ[name]
                seen[0] += 1
                assert who == "A" and n == seen[0], name
                return arrive(act, *name)

            seen = [0]
            act.wait_ge(ones_set, 1)
            act.wait_ge(consts_ld, 16 * 24)
            with act.Fori(0, DEPTH) as l:
                seen[0] = 0

                def roots(k, cols):
                    act.wait_ge(sq_ready, k[0])
                    act.activation(stat[:, cols], stat[:, cols], ACT.Sqrt).then_inc(std_ready, 1)

                roots((3,), slice(0, 3))
                act.wait_ge(gm_ld, 16)
                for k in range(1, KD, 2):
                    o = read("hT", k)
                    act.activation(hT[:, k, :], o[:, 0:T], ACT.Copy, scale=g_mix[:, k:k + 1]).then_inc(moved_a, 1)
                act.wait_ge(small_ld, 16 * 9)
                act.wait_ge(pad_set, 2)
                for c, (c0, n) in enumerate(ZCH):
                    for t, (t0, m) in enumerate(TOK):
                        o = read("z", c, t)
                        if c < 4:
                            act.copy(z[0:m, t, c0:c0 + n], o[0:m, 0:n]).then_inc(moved_a, 1)
                        else:
                            act.copy(z[0:m, t, GA:GA + CC], o[0:m, 0:CC])
                            act.activation(z[0:m, t, GB:GB + CC], o[0:m, CC:2 * CC], ACT.Sigmoid).then_inc(moved_a, 1)
                    if c == 1:
                        roots((4,), slice(3, 9))
                for k in range(2):
                    o = read("cqT", k)
                    act.activation(cqT[:, k, :], o[:, 0:T], ACT.Copy, scale=g_q[:, k:k + 1]).then_inc(moved_a, 1)
                o = read("ckvT")
                act.copy(ckvT, o[:, 0:T]).then_inc(moved_a, 1)
                o = read("krT")
                act.copy(krT, o[:, 0:T]).then_inc(moved_a, 1)
                o = read("ukT")
                act.copy(ukT.rearrange("p g c -> p (g c)"), o[:, 0:384]).then_inc(moved_a, 1)
                for t, (t0, m) in enumerate(TOK):
                    for n in range(2):
                        o = read("q", t, n)
                        oh = o[0:m, 0:288].rearrange("p (h x) -> p h x", h=3)
                        qn = q[0:m, t, 192 * n:192 * n + 192].rearrange("p (h x) -> p h x", h=3)
                        qr = q[0:m, t, NH * NOPE + 96 * n:NH * NOPE + 96 * n + 96].rearrange("p (h x) -> p h x", h=3)
                        act.copy(qn, oh[:, :, 0:NOPE])
                        act.copy(qr, oh[:, :, NOPE:]).then_inc(moved_a, 1)
                for g in range(HP):
                    o = read("qnT", g)
                    act.copy(qnT[:, g, :], o[:, 0:T]).then_inc(moved_a, 1)
                o = read("qrT", 0)
                act.copy(qrT[:, 0, :], o[:, 0:T]).then_inc(moved_a, 1)
                o = read("qrT", 1)
                act.copy(qrT[0:64, 1, :], o[0:64, 0:T]).then_inc(moved_a, 1)
                o = read("qrS")
                for i in range(4):
                    act.copy(qrB[32 * i:32 * i + 32, :, i, :], o[32 * i:32 * i + 32, 0:48].rearrange("p (h b) -> p b h", h=NH))
                act.copy(qrS.rearrange("p h b -> p (h b)"), o[:, 0:48]).then_inc(moved_a, 1)
                for t in range(2):
                    o = read("va", t)
                    act.copy(va[:, t, :], o[:, 0:384]).then_inc(moved_a, 1)
                o = read("cw")
                act.copy(cwT.rearrange("p c j -> p (c j)"), o[:, 0:2 * CW]).then_inc(moved_a, 1)
                for c in range(2):
                    o = read("sc", c)
                    act.copy(gsT[:, c, :, 0:CW - 1], o[:, 0:240].rearrange("p (b j) -> p b j", b=NB)).then_inc(moved_a, 1)
                for s in range(2 * NH + 1):
                    if s < 2 * NH:
                        act.wait_ge(nmx_ready, s + 1)
                        for i, c0 in ((0, 0), (1, 128)):
                            pr = prob[:, s % 2, c0:c0 + 128 * (i + 1)]
                            e = act.activation(pr, pr, ACT.Exp, bias=nmx[:, s, i:i + 1], scale=SA if s < NH else SB,
                                               accum_out=den[:, s, i:i + 1] if s < NH else None)
                        e.then_inc(exp_ready, 1)
                    if s >= 1:
                        o = read("PT", s - 1)
                        act.copy(probT[:, (s - 1) % 2, :], o[:, 0:384]).then_inc(moved_a, 1)
                for g in range(2 * HP):
                    o = read("mT", g)
                    act.copy(mixT[:, g, 0:SEQ], o[:, 0:SEQ]).then_inc(moved_a, 1)
                for t, (t0, m) in enumerate(TOK):
                    o = read("yt", t)
                    act.copy(yt[0:m, t, :], o[0:m, 0:CC]).then_inc(moved_a, 1)
                roots((5,), slice(9, 12))
                for c in range(2):
                    o = arrive(act, "ycT", c)
                    act.activation(ycs[:, c, :], o[:, 0:T], ACT.Sigmoid, bias=g_lb[:, c:c + 1], scale=g_lg[:, c:c + 1]).then_inc(sig_ready, 1)

                def past_half(half):
                    for b in range(4 * half, 4 * half + 5):
                        if b < 4 * half + 4:
                            for g in range(4):
                                o = read("cT", b, g)
                                act.copy(cT[:, b % 2, 512 * g:512 * g + 512], o[:, 0:512]).then_inc(moved_a, 1)
                            o = read("rT", b)
                            act.copy(rT[:, b % 2, :, :].rearrange("p g k -> p (g k)"), o[:, 0:512]).then_inc(moved_a, 1)
                        if b > 4 * half:
                            o = read("ST", b - 1)
                            act.copy(STm[:, (b - 1) % 4, 0:NPG, :].rearrange("p g h -> p (g h)"), o[:, 0:NPG * NH]).then_inc(moved_a, 1)

                def sample_exp(n, S, scale):
                    wait_moved(act, "mb", n)
                    flat = S.rearrange("p b g h -> p (b g h)")
                    act.activation(flat, flat, ACT.Exp, scale=scale).then_inc(sexp_ready, 1)

                past_half(0)
                sample_exp(0, STm, SA)
                sample_exp(2, STw, SB)
                past_half(1)
                sample_exp(1, STm, SA)
                roots((8,), slice(0, 3))
                for k in range(1, KD, 2):
                    o = read("fT", k)
                    act.activation(hT[:, k, :], o[:, 0:T], ACT.Copy, scale=g_ffn[:, k:k + 1]).then_inc(moved_a, 1)
                for g in range(4):
                    o = read("skT", g)
                    act.copy(skT[:, 4 * g:4 * g + 4, :].rearrange("p n c -> p (n c)"), o[:, 0:512]).then_inc(moved_a, 1)
                for g in range(5):
                    if g < 4:
                        for n in range(4 * g, 4 * g + 4):
                            o = read("pq", n)
                            act.copy(pqT[:, n, :], o[:, 0:T]).then_inc(moved_a, 1)
                    if g:
                        for t in (2, 0, 1):
                            t0, m = TOK[t]
                            o = read("s", t, g - 1)
                            act.copy(sc[0:m, t, 4 * g - 4:4 * g, :].rearrange("p n c -> p (n c)"), o[0:m, 0:512]).then_inc(moved_a, 1)
                def slots(t):
                    t0, m = TOK[t]
                    o = read("slot", t)
                    act.copy(slotT[:, :, t0:t0 + m], o[:, 0:384].rearrange("p (s c) -> p s c", s=3)[:, :, 0:m]).then_inc(moved_a, 1)

                act.wait_ge(cand_max, 1)
                act.activation(psel[:, 2, :], psel[:, 2, :], ACT.Exp).then_inc(gexp, 1)
                slots(2)
                act.wait_ge(cand_max, 2)
                act.activation(sel[:, 0, 2, :], sel[:, 0, 2, :], ACT.Exp).then_inc(gexp, 1)
                for b in range(NB + 1):
                    if b < NB:
                        for half in range(2):
                            o = read("gu", b, half)
                            act.copy(uTs[b % 2][:, 512 * half:512 * half + 512], o[:, 0:512]).then_inc(moved_a, 1)
                    if b:
                        o = read("gz", b - 1)
                        act.activation(gel[:, b - 1:b], o[:, 0:1], ACT.Gelu).then_inc(moved_a, 1)
                for b in range(NB):
                    if b == 0:
                        wait_moved(act, "gz", NB - 1)
                    act.activation(coef[:, b, b:b + 1], gel[:, b:b + 1], ACT.Copy, scale=slotT[:, 2, SEQ + b:SEQ + b + 1]).then_inc(coef_ready, 1)
                slots(0)
                act.wait_ge(cand_max, 3)
                act.activation(sel[:, 1, 2, :], sel[:, 1, 2, :], ACT.Exp).then_inc(gexp, 1)
                slots(1)
                act.wait_ge(product, NUM["gy", 1] + 1)
                act.copy(hp[0], hT[:, :, 0:SEQ]).then_inc(h_high, 1)
                for _ in range(2):
                    act.nop().then_inc(g_moved, 1)
                wait_moved(act, "slot", 1)
                act.activation(nw, slotT[:, 2, :], ACT.Copy, scale=-1.0).then_inc(dist_ready, 1)

                def onehot(hb, tk, n):
                    act.activation(dist, iota[:, :], ACT.Abs, bias=slotT[:, 1, tk], scale=-1.0).then_inc(dist_ready, 1)
                    act.wait_ge(dist_ready, n + 2)
                    act.activation(hb[:, 3, :], dist, ACT.Relu, bias=slotT[:, 2, tk], scale=nw[:, tk]).then_inc(hotC_ready, 1)

                onehot(hotB, slice(3, 4), 0)
                with act.Fori(0, SEQ // GT) as it:
                    for g in range(2):
                        act.wait_ge(g_prod, it * 2 + (g + 2))
                        act.wait_ge(hotC_ready, it * 2 + (g + 1))
                        onehot(hotB2 if g == 0 else hotB, bass.ds(it * GT + (4 * g + 7), 1), it * 2 + (g + 1))
                        act.wait_ge(g_prod, it * 2 + (g + 3))
                        act.copy(G[:, bass.ds(it * GT + 4 * g, 4), :].rearrange("p t j -> p (t j)"), ps[:, 6 + g, :]).then_inc(g_moved, 1)
                act.wait_ge(h_low, 1)

                def expert_steps(it, ks, first=False, last=False):
                    for k in ks:
                        if not first or k >= 2:
                            act.wait_ge(v_ld[k % 2], it * 32 + 16 * ((k + 2) // 2 + 1))
                            for half in range(2):
                                wait_count(act, v_used, it * 8 + (3 + 2 * k + half))
                                act.copy(vp[0][:, 512 * half:512 * half + 512], v_t[k % 2][:, 512 * half:512 * half + 512]).then_inc(v_high, 1)
                        if not last:
                            for half in range(2):
                                wait_count(act, (half_used, z_prod)[half], it * 4 + (4 + k))
                                act.wait_ge(turned, it * 8 + (9 + 2 * k + half))
                                act.copy(uT[0][:, 512 * half:512 * half + 512], ps[:, 6 + half, :]).then_inc(uT_high, 1)
                        if (not first or k >= 1) and (not last or k == 0):
                            act.wait_ge(z_prod, it * 4 + (4 + k))
                            act.activation(act_t[(k + 1) % 2], ps[:, 4 + (k + 1) % 2, 0:SEQ], ACT.Gelu).then_inc(gelu_done, 1)

                expert_steps(-1, range(UN), first=True)
                with act.Fori(0, LOOPS - 1) as it:
                    expert_steps(it, range(UN))
                expert_steps(LOOPS - 1, range(2), last=True)
                act.wait_ge(gelu_done, NK)
                layer_end(act, 1)
            act.wait_ge(f_sq, 3)
            act.activation(stat[:, 0:3], stat[:, 0:3], ACT.Sqrt).then_inc(f_std, 1)

        @block.vector
        def _(dve):
            steps, seen, last_tap = [0], [0], [0, 0]

            def step(ins):
                steps[0] += 1
                ins.then_inc(vstep, 1)
                return steps[0]

            def settle():
                dve.wait_ge(vstep, steps[0])

            def read(*name):
                who, n = READ[name]
                seen[0] += 1
                assert who == "V" and n == seen[0], name
                return arrive(dve, *name)

            def squares(dst, done):
                for t, (t0, m) in enumerate(TOK):
                    dve.tensor_tensor_reduce(dst[0:m, t, :], X[0:m, t, :], X[0:m, t, :], 1.0 / D, EPS, ALU.mult, ALU.add,
                                             stat[0:m, t:t + 1]).then_inc(done, 1)

            def rotate(x1, x2, cos, sin, ta, tb):
                step(dve.tensor_tensor(ta, x1, sin, ALU.mult))
                step(dve.tensor_tensor(tb, x2, sin, ALU.mult))
                settle()
                step(dve.tensor_tensor(x1, x1, cos, ALU.mult))
                step(dve.tensor_tensor(x2, x2, cos, ALU.mult))
                settle()
                step(dve.tensor_tensor(x1, x1, tb, ALU.subtract))
                return dve.tensor_tensor(x2, x2, ta, ALU.add)

            dve.wait_ge(consts_ld, 16 * 24)
            dve.wait_ge(ones_set, 1)
            dve.memset(eoff[:, :], 0.0)
            dve.memset(coef[:, :, :], 0.0)
            dve.tensor_scalar(pidx[:, :], pages[:, :], 8.0, sub[:, 0:1], ALU.mult, ALU.add).then_inc(rows_ready, 1)
            with dve.Fori(0, DEPTH) as l:
                steps[0], seen[0] = 0, 0

                def norm(dst, k):
                    squares(dst, sq_ready)
                    dve.wait_ge(std_ready, k)
                    step(dve.reciprocal(stat[:, 0:3], stat[:, 0:3]))
                    settle()
                    for t, (t0, m) in enumerate(TOK):
                        dve.tensor_scalar(dst[0:m, t, :], X[0:m, t, :], stat[0:m, t:t + 1], None, ALU.mult).then_inc(hn_ready, 1)

                norm(hn, 1)
                dve.wait_ge(gm_ld, 16)
                for k in range(0, KD, 2):
                    o = read("hT", k)
                    dve.tensor_scalar(hT[:, k, :], o[:, 0:T], g_mix[:, k:k + 1], None, ALU.mult).then_inc(moved_v, 1)
                dve.wait_ge(small_ld, 16 * 9)
                wait_moved(dve, "z", 0, 2)
                dve.wait_ge(pad_set, 2)
                for i, (c0, n) in enumerate(((CQ, QL), (CKV, LAT))):
                    for t in range(3):
                        zz = z[:, t, c0:c0 + n]
                        step(dve.tensor_tensor_reduce(junk[:, 0:n], zz, zz, 1.0 / n, EPS, ALU.mult, ALU.add, stat[:, 3 + 3 * i + t:4 + 3 * i + t]))
                        settle()
                dve.nop().then_inc(sq_ready, 1)
                dve.wait_ge(std_ready, 2)
                step(dve.reciprocal(stat[:, 3:9], stat[:, 3:9]))
                settle()
                cq, ckv = z[:, :, CQ:CQ + QL], z[:, :, CKV:CKV + LAT]
                dve.tensor_tensor(cq, cq, stat[:, 3:6].unsqueeze(2).to_broadcast([P, 3, QL]), ALU.mult).then_inc(lat_ready, 1)
                step(dve.tensor_tensor(ckv, ckv, stat[:, 6:9].unsqueeze(2).to_broadcast([P, 3, LAT]), ALU.mult))
                settle()
                step(dve.tensor_tensor(ckv, ckv, kvg.unsqueeze(1).to_broadcast([P, 3, LAT]), ALU.mult))
                cosA, sinA, cosB, sinB = rope[:, :, 0:16], rope[:, :, 16:32], rope[:, :, 32:64], rope[:, :, 64:96]
                ra = ropet[:, 0:1152]
                rb = ropet[:, 1152:2304]

                def cut3(a, n):
                    return a[:, 0:3 * n].rearrange("p (t c) -> p t c", t=3)

                rotate(z[:, :, KR:KR + 16], z[:, :, KR + 16:KR + 32], cosA, sinA, cut3(ra, 16), cut3(rb, 16)).then_inc(lat_ready, 1)
                dve.wait_ge(lat_ready, 2)
                settle()
                dve.tensor_copy(krr, z[:, :, KR:KR + ROPE].unsqueeze(2).to_broadcast([P, 3, 4, ROPE])).then_inc(lat_ready, 1)
                wait_moved(dve, "z", 2, 2)
                for t in range(3):
                    x = z[:, t, QB:QB + 768].rearrange("p (h s c) -> p h s c", h=2 * NH, s=2)
                    tt = [r[:, 384 * t:384 * t + 384].rearrange("p (h c) -> p h c", h=2 * NH) for r in (ra, rb)]
                    last = rotate(x[:, :, 0, :], x[:, :, 1, :], cosB[:, t, :].unsqueeze(1).to_broadcast([P, 2 * NH, 32]),
                                  sinB[:, t, :].unsqueeze(1).to_broadcast([P, 2 * NH, 32]), tt[0], tt[1])
                    step(last)
                settle()
                dve.nop().then_inc(qk_ready, 1)
                wait_moved(dve, "z", 4, 2)
                dve.tensor_tensor(z[:, :, GA:GA + CC], z[:, :, GA:GA + CC], z[:, :, GB:GB + CC], ALU.mult).then_inc(g_ready, 1)
                wait_moved(dve, "q", 2, 1)
                for t, (t0, m) in enumerate(TOK):
                    x = q[0:m, t, NH * NOPE:].rearrange("p (h c) -> p h c", h=NH)
                    tt = [r[0:m, 96 * t:96 * t + 96].rearrange("p (h c) -> p h c", h=NH) for r in (ra, rb)]
                    step(rotate(x[:, :, 0:16], x[:, :, 16:32], cosA[0:m, t, :].unsqueeze(1).to_broadcast([m, NH, 16]),
                                sinA[0:m, t, :].unsqueeze(1).to_broadcast([m, NH, 16]), tt[0], tt[1]))
                settle()
                dve.tensor_copy(qrr[0:NB], q[0:NB, 2, NH * NOPE:].rearrange("p (h c) -> p h c", h=NH).unsqueeze(2).to_broadcast([NB, NH, 4, ROPE])).then_inc(q_ready, 1)
                for g in range(HP):
                    o = read("qbT", g)
                    dve.tensor_copy(qbT[:, g, :], o[:, 0:T]).then_inc(moved_v, 1)
                for g in range(HP):
                    o = read("kbT", g)
                    dve.tensor_copy(kbT[:, g, :], o[:, 0:T]).then_inc(moved_v, 1)
                for h in range(NH):
                    o = read("qlT", h)
                    dve.tensor_copy(qlT[:, h, :], o[:, 0:T]).then_inc(moved_v, 1)
                for c in range(2):
                    o = read("gT", c)
                    step(dve.tensor_copy(gT[:, c, CW - 1:CW - 1 + SEQ], o[:, 0:SEQ]))
                    dve.tensor_copy(gsT[:, c, :, CW - 1], o[:, SEQ:T]).then_inc(moved_v, 1)
                wait_moved(dve, "sc", 1)
                wait_moved(dve, "gT", 1)
                settle()

                def tap(n):
                    j, c = n // 2, n % 2
                    y, x, w = yT[:, c, 0:SEQ], gT[:, c, j:j + SEQ], cwT[:, c, j:j + 1]
                    if j == 0:
                        last_tap[c] = step(dve.tensor_scalar(y, x, w, g_cb[:, c:c + 1], ALU.mult, ALU.add))
                    else:
                        dve.wait_ge(vstep, last_tap[c])
                        last_tap[c] = step(dve.scalar_tensor_tensor(y, x, w, y, ALU.mult, ALU.add))

                taps = iter(range(2 * CW))
                for s in range(2 * NH + 2):
                    if s < 2 * NH:
                        o = read("S", s)
                        dve.tensor_tensor(prob[:, s % 2, :], o[:, 0:384], mbias if s < NH else cbias, ALU.add).then_inc(moved_v, 1)
                        wait_moved(dve, "S", s)
                        for i, c0 in ((0, 0), (1, 128)):
                            step(dve.tensor_reduce(nmx[:, s, i:i + 1], prob[:, s % 2, c0:c0 + 128 * (i + 1)], AX, ALU.max))
                        settle()
                        dve.tensor_scalar(nmx[:, s, :], nmx[:, s, :], -SA if s < NH else -SB, None, ALU.mult).then_inc(nmx_ready, 1)
                    u = s - 1
                    if NH <= u < 2 * NH:
                        dve.wait_ge(exp_ready, u + 1)
                        for i, c0 in ((0, 0), (1, 128)):
                            c1 = c0 + 128 * (i + 1)
                            e = dve.tensor_tensor_reduce(prob[:, u % 2, c0:c1], prob[:, u % 2, c0:c1], cnt[:, c0:c1], 1.0, 0.0,
                                                         ALU.mult, ALU.add, den[:, u, i:i + 1])
                            if i == 0:
                                step(e)
                        e.then_inc(cnt_ready, 1)
                    for n in range(5):
                        k = next(taps, None)
                        if k is not None:
                            tap(k)
                    u = s - 2
                    if u >= 0:
                        if u < NH:
                            dve.wait_ge(exp_ready, u + 1)
                        else:
                            dve.wait_ge(cnt_ready, u - NH + 1)
                        step(dve.reciprocal(rden[:, u, :], den[:, u, :]))
                        o = read("O", u)
                        settle()
                        dve.tensor_tensor(oAB[:, :, 64 * u:64 * u + 64], o[:, 0:128].rearrange("p (t c) -> p t c", t=2),
                                          rden[:, u, :].unsqueeze(2).to_broadcast([P, 2, 64]), ALU.mult).then_inc(moved_v, 1)
                for k in taps:
                    tap(k)
                dve.wait_ge(product, NUM["mT", 2 * HP - 1] + 1)
                for c in range(2):
                    t1 = junk[:, c * 248:(c + 1) * 248].rearrange("p (b j) -> p b j", b=NB)
                    step(dve.tensor_tensor(t1, gsT[:, c, :, :], cwT[:, c, :].unsqueeze(1).to_broadcast([P, NB, CW]), ALU.mult))
                    settle()
                    step(dve.tensor_reduce(yT[:, c, SEQ:T], t1, AX, ALU.add))
                    settle()
                    step(dve.tensor_scalar(yT[:, c, SEQ:T], yT[:, c, SEQ:T], g_cb[:, c:c + 1], None, ALU.add))
                settle()
                dve.nop().then_inc(y_ready, 1)
                for t, (t0, m) in enumerate(TOK):
                    wait_moved(dve, "yt", t)
                    step(dve.bn_stats(bnst[0:m, t, 0:6], yt[0:m, t, :]))
                    settle()
                    step(dve.bn_aggr(bnst[0:m, t, 6:8], bnst[0:m, t, 0:6]))
                    settle()
                    step(dve.tensor_scalar(stat[0:m, 9 + t:10 + t], bnst[0:m, t, 7:8], EPS, None, ALU.add))
                settle()
                dve.nop().then_inc(sq_ready, 1)
                dve.wait_ge(std_ready, 3)
                step(dve.reciprocal(stat[:, 9:12], stat[:, 9:12]))
                settle()
                for t, (t0, m) in enumerate(TOK):
                    dve.tensor_scalar(yt[0:m, t, :], yt[0:m, t, :], bnst[0:m, t, 6:7], stat[0:m, 9 + t:10 + t],
                                      ALU.subtract, ALU.mult).then_inc(ln_ready, 1)
                for c in range(2):
                    o = read("ycT", c)
                    dve.wait_ge(sig_ready, c + 1)
                    step(dve.tensor_scalar(ycs[:, 2, :], o[:, 0:T], g_lg[:, c:c + 1], g_lb[:, c:c + 1], ALU.mult, ALU.add))
                    settle()
                    dve.tensor_tensor(mixT[:, 6 + c, :], ycs[:, 2, :], ycs[:, c, :], ALU.mult).then_inc(moved_v, 1)
                    wait_moved(dve, "ycT", c)

                def new_keys(half):
                    step(dve.tensor_tensor(STm[0:NB, :, NPG, :], extS[:, :, 4 * half:4 * half + 4].rearrange("p h b -> p b h"),
                                           diag[:, 4 * half:4 * half + 4].unsqueeze(2).to_broadcast([NB, 4, NH]), ALU.add))
                    settle()

                def softmax(*group):
                    def bc(S, a):
                        return a.rearrange("p (b h) -> p b h", b=S.shape[1])

                    for n, S, c, order, last_slot in group:
                        dve.tensor_reduce(bc(S, smx[:, n, 0:c]), S.rearrange("p b g h -> p b h g"), AX, ALU.max).then_inc(smx_ready, 1)
                    for n, S, c, order, last_slot in group:
                        o = read("mx", n)
                        dve.tensor_reduce(smc[0:c, n:n + 1], o[0:c, 0:128], AX, ALU.max).then_inc(moved_v, 1)
                    for n, S, c, order, last_slot in group:
                        wait_moved(dve, "mx", n)
                        dve.tensor_scalar(sdg[0:c, n, 0:c], ident[0:c, 0:c], smc[0:c, n:n + 1], None, ALU.mult).then_inc(sdg_ready, 1)
                    for n, S, c, order, last_slot in group:
                        o = read("mb", n)
                        nb, ng = S.shape[1], S.shape[2]
                        for b in range(nb):
                            e = dve.tensor_tensor(S[:, b, :, :], S[:, b, :, :], o[:, NH * b:NH * b + NH].unsqueeze(1).to_broadcast([P, ng, NH]),
                                                  ALU.subtract)
                            if b < nb - 1:
                                step(e)
                        settle()
                        e.then_inc(moved_v, 1)
                    for n, S, c, order, last_slot in group:
                        dve.wait_ge(sexp_ready, order)
                        if last_slot:
                            new = S[:, :, S.shape[2] - 1, :]
                            step(dve.tensor_scalar(new, new, float(len(DIL)), None, ALU.mult))
                            settle()
                        dve.tensor_reduce(bc(S, sden[:, n, 0:c]), S.rearrange("p b g h -> p b h g"), AX, ALU.add).then_inc(sden_ready, 1)
                    for n, S, c, order, last_slot in group:
                        o = read("dn", n)
                        dve.reciprocal(srd[:, n, 0:c], o[:, 0:c]).then_inc(moved_v, 1)
                        wait_moved(dve, "dn", n)

                def latents_raw(half):
                    o = read("ol", half)
                    dve.tensor_copy(olr, o[0:NH, 0:512]).then_inc(moved_v, 1)

                def latents_out(half):
                    o = read("olT", half)
                    dve.tensor_tensor(olT[:, 4 * half:4 * half + 4, :].rearrange("p b h -> p (b h)"), o[:, 0:24],
                                      srd[:, half, 0:24], ALU.mult).then_inc(moved_v, 1)

                o = read("ext")
                step(dve.memset(STm[:, :, NPG, :], NEG))
                step(dve.memset(STw[:, :, 3, :], NEG))
                settle()
                dve.tensor_copy(extS.rearrange("p h b -> p (h b)"), o[0:NB, 0:48]).then_inc(moved_v, 1)
                wait_moved(dve, "ext")
                new_keys(0)
                for b in range(NB):
                    o = read("qbc", b)
                    dve.wait_ge(kw_ld, 48 * (b + 1))
                    e = dve.tensor_tensor(kprod, kw, o[:, 0:384].unsqueeze(1).to_broadcast([P, 3, 384]), ALU.mult)
                    e.then_inc(moved_v, 1)
                    wait_moved(dve, "qbc", b)
                    step(dve.tensor_reduce(STw[:, b, 0:3, :], kprod.rearrange("p d (h c) -> p d h c", h=NH), AX, ALU.add))
                    settle()
                step(dve.tensor_tensor(kprod[0:NB, 0, :], z[0:NB, 2, QB:QB + 384], z[0:NB, 2, KB:KB + 384], ALU.mult))
                settle()
                step(dve.tensor_reduce(kprod[0:NB, 1, 0:NH], kprod[0:NB, 0, :].rearrange("p (h c) -> p h c", h=NH), AX, ALU.add))
                settle()
                step(dve.tensor_tensor(STw[0:NB, :, 3, :], kprod[0:NB, 1, 0:NH].unsqueeze(1).to_broadcast([NB, NB, NH]),
                                       diag[:, :].unsqueeze(2).to_broadcast([NB, NB, NH]), ALU.add))
                for b in range(4):
                    wait_moved(dve, "ST", b)
                settle()
                softmax((0, STm, 24, 1, False), (2, STw, 48, 2, True))
                latents_raw(0)
                o = read("ow")
                rd = srd[:, 2, :].rearrange("p (b g a) -> p b g a", b=NB, g=HP)
                for a in range(2):
                    e = dve.tensor_tensor(mixT[64 * a:64 * a + 64, 3:6, SEQ:T], o[64 * a:64 * a + 64, 0:24].rearrange("p (g b) -> p g b", g=3),
                                          rd[64 * a:64 * a + 64, :, :, a].rearrange("p b g -> p g b"), ALU.mult)
                    if a == 0:
                        step(e)
                settle()
                e.then_inc(moved_v, 1)
                latents_out(0)
                wait_moved(dve, "ST", 7)
                step(dve.memset(STm[:, :, NPG, :], NEG))
                settle()
                new_keys(1)
                softmax((1, STm, 24, 3, False))
                latents_raw(1)
                latents_out(1)
                o = read("os")
                dve.tensor_copy(mixT[:, 0:3, SEQ:T], o[:, 0:24].rearrange("p (g b) -> p g b", g=3)).then_inc(moved_v, 1)
                def add_to_x(name, tiles=3):
                    for c in range(2):
                        for t, (t0, m) in enumerate(TOK[:tiles]):
                            o = read(name, c, t)
                            xs = X[0:m, t, 512 * c:512 * c + 512]
                            dve.tensor_tensor(xs, xs, o[0:m, 0:512], ALU.add).then_inc(moved_v, 1)
                    wait_moved(dve, name, 1, tiles - 1)

                add_to_x("xo")
                dve.wait_ge(stored, 1)
                norm(hf, 4)
                for k in range(0, KD, 2):
                    o = read("fT", k)
                    dve.tensor_scalar(hT[:, k, :], o[:, 0:T], g_ffn[:, k:k + 1], None, ALU.mult).then_inc(moved_v, 1)

                def top16(*rows):
                    done = [steps[0]] * len(rows)

                    def each(op):
                        for i, r in enumerate(rows):
                            dve.wait_ge(vstep, done[i])
                            done[i] = step(op(*r))

                    each(lambda v, ix, src: dve.max(v[:, 0:8], src))
                    each(lambda v, ix, src: dve.max_index(ix[:, 0:8], v[:, 0:8], src))
                    each(lambda v, ix, src: dve.match_replace(src, v[:, 0:8], src, -3.0e38))
                    each(lambda v, ix, src: dve.max(v[:, 8:16], src))
                    each(lambda v, ix, src: dve.max_index(ix[:, 8:16], v[:, 8:16], src))

                def chosen(dst, ci_, ab, abf, hot_, tf, m, heads):
                    civ = ci_.bitcast(U32)
                    step(dve.tensor_single_scalar(ab[:, 0].bitcast(U32), civ, 4, ALU.logical_shift_right))
                    step(dve.tensor_single_scalar(ab[:, 1].bitcast(U32), civ, 15, ALU.bitwise_and))
                    settle()
                    step(dve.tensor_copy(abf, ab.bitcast(U32)))
                    settle()
                    n = heads * TOPK
                    for s in range(2):
                        io = iota[0:m, 0:TOPK].unsqueeze(1).to_broadcast([m, n, TOPK])
                        ch = (abf[:, s, :, :].rearrange("p h k -> p (h k)") if heads > 1 else abf[:, s, :]).unsqueeze(2).to_broadcast([m, n, TOPK])
                        flat = hot_.rearrange("p h k a -> p (h k) a") if heads > 1 else hot_
                        step(dve.tensor_tensor(flat, io, ch, ALU.is_equal))
                        settle()
                        step(dve.tensor_tensor(hot_, hot_, tf(s), ALU.mult))
                        settle()
                        step(dve.tensor_reduce(dst(s), flat, AX, ALU.add))
                        settle()

                def sample_tops():
                    dve.wait_ge(scp_ld, 16 * NSUB)
                    settle()
                    top16((tpk[:, 0, :], tpi.bitcast(U32), scp))
                    settle()
                    dve.tensor_copy(tpk[:, 1, :], tpi.bitcast(U32)).then_inc(p1_ready, 1)

                for g in range(4):
                    if g == 3:
                        sample_tops()
                    for t in range(2):
                        wait_moved(dve, "s", t, g)
                        top16(*[(top[:, t, i, :], topi[:, t, i, :].bitcast(U32), sc[:, t, i, :]) for i in range(4 * g, 4 * g + 4)])
                settle()
                step(dve.tensor_copy(topf, topi.bitcast(U32)))
                def sample_gates():
                    dve.wait_ge(tq_ld, 16)
                    dve.wait_ge(p1_ready, 1)
                    step(dve.tensor_tensor(pcand, tpk[0:64, 0, :].unsqueeze(2).to_broadcast([64, TOPK, TOPK]),
                                           tq[:, 0, :].unsqueeze(1).to_broadcast([64, TOPK, TOPK]), ALU.add))
                    settle()
                    top16((pcs, pci.bitcast(U32), pcand.rearrange("p a b -> p (a b)")))
                    settle()
                    chosen(lambda s: psel[:, s, :], pci, pab, pabf, phot,
                           lambda s: (tpk[0:64, 1, :] if s == 0 else tq[:, 1, :]).unsqueeze(1).to_broadcast([64, TOPK, TOPK]), 64, 1)
                    dve.tensor_scalar(psel[:, 2, :], pcs, pcs[:, 0:1], None, ALU.subtract).then_inc(cand_max, 1)
                    dve.wait_ge(gexp, 1)
                    step(dve.tensor_reduce(psum2[:, 0:1], psel[:, 2, :], AX, ALU.add))
                    settle()
                    step(dve.reciprocal(psum2[:, 1:2], psum2[:, 0:1]))
                    settle()
                    dve.tensor_scalar(psel[:, 2, :], psel[:, 2, :], psum2[:, 1:2], None, ALU.mult).then_inc(p2_ready, 1)

                def second(t):
                    tv = top[:, t, :, :].rearrange("p (h s) k -> p h s k", s=2)
                    tf = topf[:, t, :, :].rearrange("p (h s) k -> p h s k", s=2)
                    step(dve.tensor_tensor(cand.rearrange("p h (a b) -> p h a b", a=TOPK),
                                           tv[:, :, 0, :].unsqueeze(3).to_broadcast([P, PH, TOPK, TOPK]),
                                           tv[:, :, 1, :].unsqueeze(2).to_broadcast([P, PH, TOPK, TOPK]), ALU.add))
                    settle()
                    for h in range(0, PH, 4):
                        top16(*[(cs[:, i, :], ci[:, i, :].bitcast(U32), cand[:, i, :]) for i in range(h, h + 4)])
                    settle()
                    gt = sel[:, t, 2, :].rearrange("p (h k) -> p h k", h=PH)
                    dve.tensor_tensor(gt, cs, cs[:, :, 0:1].to_broadcast([P, PH, TOPK]), ALU.subtract).then_inc(cand_max, 1)
                    chosen(lambda s: sel[:, t, s, :], ci, cab, cabf, hot,
                           lambda s: tf[:, :, s, :].unsqueeze(2).to_broadcast([P, PH, TOPK, TOPK]), P, PH)
                    dve.wait_ge(gexp, t + 2)
                    step(dve.tensor_reduce(hsum[:, 0, :], gt, AX, ALU.add))
                    settle()
                    step(dve.reciprocal(hsum[:, 1, :], hsum[:, 0, :]))
                    settle()
                    dve.tensor_tensor(gt, gt, hsum[:, 1, :].unsqueeze(2).to_broadcast([P, PH, TOPK]), ALU.mult).then_inc(sel_ready, 1)
                    dve.wait_ge(sel_ready, t + 1)

                sample_gates()
                wait_moved(dve, "slot", 2)
                step(dve.scalar_tensor_tensor(efl[:, :], slotT[:, 0, SEQ:T], float(NK), slotT[:, 1, SEQ:T], ALU.mult, ALU.add))
                settle()
                dve.tensor_scalar(eidx[:, :], efl[:, :], eoff[:, 0:1], None, ALU.add).then_inc(e_ready, 1)
                second(0)
                second(1)
                for half in range(2):
                    o = read("gy", half)
                    xs = X[0:NB, 2, 512 * half:512 * half + 512]
                    dve.tensor_tensor(xs, xs, o[0:NB, 0:512], ALU.add).then_inc(moved_v, 1)
                wait_moved(dve, "slot", 1)
                with dve.Fori(0, SEQ // GT) as it:
                    for g in range(2):
                        dve.wait_ge(g_prod, it * 2 + (g + 1))
                        hb = hotB if g == 0 else hotB2
                        ta = slotT[:, 0, bass.ds(it * GT + 4 * g, 4)].unsqueeze(2).to_broadcast([P, 4, P])
                        dve.tensor_tensor(hotA[:, 4 * g:4 * g + 4, :], iota[:, :].unsqueeze(1).to_broadcast([P, 4, P]), ta,
                                          ALU.is_equal).then_inc(hotA_ready, 1)
                        for k in range(3):
                            tk = bass.ds(it * GT + (4 * g + k), 1)
                            e = dve.tensor_scalar(hb[:, k, :], iota[:, :], slotT[:, 1, tk], slotT[:, 2, tk], ALU.is_equal, ALU.mult)
                        e.then_inc(hotB_ready, 1)
                dve.wait_ge(g_prod, 2 * (SEQ // GT) + 2)
                dve.memset(zeros, 0.0).then_inc(acc_zero, 1)
                dve.wait_ge(h_high, 1)
                dve.tensor_tensor(hp[1], hT[:, :, 0:SEQ], hp[0], ALU.subtract).then_inc(h_low, 1)
                dve.wait_ge(h_low, 1)

                def expert_steps(it, ks, first=False, last=False):
                    for k in ks:
                        if not first or k >= 2:
                            for half in range(2):
                                h = slice(512 * half, 512 * half + 512)
                                dve.wait_ge(v_high, it * 8 + (5 + 2 * k + half))
                                dve.tensor_tensor(vp[1][:, h], v_t[k % 2][:, h], vp[0][:, h], ALU.subtract).then_inc(v_low, 1)
                        if not last:
                            for half in range(2):
                                h = slice(512 * half, 512 * half + 512)
                                dve.wait_ge(uT_high, it * 8 + (9 + 2 * k + half))
                                dve.tensor_tensor(uT[1][:, h], ps[:, 6 + half, :], uT[0][:, h], ALU.subtract).then_inc(uT_low, 1)
                        if (not first or k >= 1) and (not last or k == 0):
                            w, (high, low) = act_t[(k + 1) % 2], wp[(k + 1) % 2]
                            dve.wait_ge(gelu_done, it * 4 + (4 + k))
                            dve.tensor_tensor(w, w, G[:, :, bass.ds(it * 4 + (3 + k), 1)].rearrange("p t o -> p (t o)"),
                                              ALU.mult).then_inc(w_full, 1)
                            dve.wait_ge(w_full, it * 4 + (4 + k))
                            dve.tensor_copy(high, w).then_inc(w_high, 1)
                            dve.wait_ge(w_high, it * 4 + (4 + k))
                            dve.tensor_tensor(low, w, high, ALU.subtract).then_inc(w_ready, 1)

                expert_steps(-1, range(UN), first=True)
                with dve.Fori(0, LOOPS - 1) as it:
                    expert_steps(it, range(UN))
                expert_steps(LOOPS - 1, range(2), last=True)
                dve.wait_ge(acc_done, 1)
                dve.wait_ge(w_ready, NK)
                for n in range(4):
                    step(dve.tensor_copy(yacc[:, 2 * n:2 * n + 2, 0:SEQ], ps[:, n, :].rearrange("p (c t) -> p c t", c=2)))
                settle()
                dve.nop().then_inc(y_moved, 1)
                add_to_x("xT", 2)
                n_rows = A["cache_kv_latent"].shape[1] * 8
                dve.tensor_scalar(pidx[:, :], pidx[:, :], float(n_rows), None, ALU.add).then_inc(rows_ready, 1)
                step(dve.tensor_scalar(eoff[:, :], eoff[:, :], float(NK * NK), None, ALU.add))
                settle()
                layer_end(dve, 2)
            squares(fin, f_sq)
            dve.wait_ge(f_std, 1)
            dve.reciprocal(stat[:, 0:3], stat[:, 0:3]).then_inc(f_step, 1)
            dve.wait_ge(f_step, 1)
            dve.wait_ge(f_gld, 16)
            for t, (t0, m) in enumerate(TOK):
                dve.scalar_tensor_tensor(fin[0:m, t, :], X[0:m, t, :], stat[0:m, t:t + 1], gfin[0:m, :], ALU.mult, ALU.mult).then_inc(f_y, 1)


def constants():
    f = np.float32
    pos = np.zeros((P, 3), f)
    pos[:, 0], pos[:, 1] = np.arange(P), P + np.arange(P)
    pos[:, 2] = PAST
    rope = np.zeros((P, 3, 96), f)
    for dim, a in ((ROPE, 0), (HD, 32)):
        half = dim // 2
        inv = np.power(f(10000.0), -np.arange(half, dtype=f) * f(2.0) / f(dim)).astype(f)
        ang = (pos[:, :, None] * inv).astype(f)
        rope[:, :, a:a + half] = np.cos(ang)
        rope[:, :, a + half:a + 2 * half] = np.sin(ang)
    qi = np.arange(P)[:, None]
    dist = np.concatenate([qi - np.arange(P), P + qi - np.arange(2 * P)], axis=1)
    cnt = sum(((dist >= 0) & (dist <= 128 * d) & (dist % d == 0)).astype(f) for d in DIL)
    masks = np.concatenate([cnt, np.where(cnt > 0, 0, NEG), np.where(dist >= 0, 0, NEG)], axis=1).astype(f)
    return {
        "ident": np.eye(P, dtype=f),
        "iota": np.tile(np.arange(P, dtype=f), (P, 1)),
        "rope": rope,
        "sub": (np.arange(P, dtype=f) % 8)[:, None],
        "diag": np.where(np.eye(NB) > 0, 0, NEG).astype(f),
        "masks": masks,
    }


_OUTS = [(1, SEQ, D), (NB, 1, D), (DEPTH, 1, SEQ, LAT), (DEPTH, 1, SEQ, ROPE), (DEPTH, 1, SEQ, NH, HD), (DEPTH, 1, SEQ, NH, HD),
         (DEPTH, 1, CW - 1, CC), (DEPTH, NB, 1, LAT), (DEPTH, NB, 1, ROPE), (DEPTH, NB, PAST, NH, HD), (DEPTH, NB, PAST, NH, HD),
         (DEPTH, NB, CW - 1, CC)]


def kernel(**inputs):
    import concourse.bacc as _bacc
    from concourse.bass_utils import run_bass_kernel_spmd as _run

    nc = _bacc.Bacc("TRN2", target_bir_lowering=False, num_devices=1)
    arrays, A, C = {}, {}, {}
    for name, a in inputs.items():
        a = np.ascontiguousarray(a)
        arrays[f"in_{name}"] = a
        A[name] = nc.dram_tensor(f"in_{name}", a.shape, mybir.dt.from_np(a.dtype), kind="ExternalInput").ap()
    for name, a in constants().items():
        arrays[f"const_{name}"] = a
        C[name] = nc.dram_tensor(f"const_{name}", a.shape, F32, kind="ExternalInput").ap()
    outs = [nc.dram_tensor(f"out_{i}", s, F32, kind="ExternalOutput").ap() for i, s in enumerate(_OUTS)]
    program(nc, A, C, outs)
    r = _run(nc, [arrays], core_ids=[0])
    return tuple(r.results[0][f"out_{i}"] for i in range(len(_OUTS)))
```
